# Optimizing a Trainium2 kernel written in Bass

```python
import jax, jax.numpy as jnp
from jax import lax
import numpy as np

D_MODEL = 1024
BATCH = 1
SEQ = 512
DEPTH = 1
DEC_BATCH = 8
DEC_SEQ = 1
PAST_LEN = 4096
PAGE_SIZE = 128

HD = 64
NSA_H = D_MODEL // 128
NSA_KV = 2
NSA_R = NSA_H // NSA_KV
CMP_BLOCK = 64
N_SELECT = 16
WINDOW = 512
FOX_H = D_MODEL // 128
MEM_H = 4
N_MEM = 256
BR_W = NSA_H * HD
MEM_HD = BR_W // MEM_H
N_BRANCH = 3
ROT_DIM = HD // 4
ROPE_THETA = 500000.0
Q_BLOCK = 128
SLC_Q_BLOCK = 64
EPS = 1e-6
NEG = -1e30
BIG = 1e4
TINY = 1e-30
KV_W = NSA_KV * HD
COL_SIZES = (
    BR_W,
    2 * KV_W,
    2 * KV_W,
    2 * KV_W,
    3 * NSA_H,
    BR_W,
    BR_W,
    2 * BR_W,
    FOX_H,
    BR_W,
    BR_W,
    BR_W,
    N_BRANCH * D_MODEL,
)
N_IN = sum(COL_SIZES)

kernel_name = 'nsa_fox_memory_gated_hybrid_step'

def _rmsnorm(x, g):
    xf = x.astype(jnp.float32)
    y = xf * lax.rsqrt(jnp.mean(xf * xf, axis=-1, keepdims=True) + EPS)
    return (y * g.astype(jnp.float32)).astype(x.dtype)

def _rope_partial(x, pos):
    half = ROT_DIM // 2
    inv_freq = ROPE_THETA ** (-jnp.arange(half, dtype=jnp.float32) / half)
    ang = pos[:, None] * inv_freq[None, :]
    cos = jnp.cos(ang)[:, None, :]
    sin = jnp.sin(ang)[:, None, :]
    xr = x[..., :ROT_DIM].astype(jnp.float32)
    x1, x2 = xr[..., :half], xr[..., half:]
    rot = jnp.concatenate([x1 * cos - x2 * sin, x2 * cos + x1 * sin], axis=-1)
    return jnp.concatenate([rot.astype(x.dtype), x[..., ROT_DIM:]], axis=-1)

def _masked_softmax(s, mask, axis=-1):
    s = jnp.where(mask, s.astype(jnp.float32), NEG)
    m = jnp.max(s, axis=axis, keepdims=True)
    e = jnp.where(mask, jnp.exp(s - m), 0.0)
    return e / jnp.maximum(jnp.sum(e, axis=axis, keepdims=True), TINY)

def _project(xn, w_in, b_fgate, pos):
    B, T = xn.shape[:2]
    h = jnp.einsum('btd,dn->btn', xn, w_in)
    splits = np.cumsum(np.array(COL_SIZES))[:-1].tolist()
    (nq, ncmp, nslc, nwin, ngate, nsilu, fq, fkv, flog, fsilu, mq, msilu, bgate) = jnp.split(h, splits, axis=-1)

    def kv_rows(a):
        a = a.reshape(B, T, 2, NSA_KV, HD)
        return jnp.stack([_rope_partial(a[:, :, 0], pos), a[:, :, 1]], axis=2)

    q = _rope_partial(nq.reshape(B, T, NSA_H, HD), pos)
    logf = jax.nn.log_sigmoid(flog.astype(jnp.float32) + b_fgate.astype(jnp.float32))
    return (q, kv_rows(ncmp), kv_rows(nslc), kv_rows(nwin), ngate, nsilu,
            fq.reshape(B, T, FOX_H, HD), fkv.reshape(B, T, 2, FOX_H, HD), logf, fsilu,
            mq.reshape(B, T, MEM_H, MEM_HD), msilu, bgate)

def _compress(rows, w1, w2, pe):
    r = rows.reshape(rows.shape[:-3] + (-1, CMP_BLOCK) + rows.shape[-2:])
    r = r + pe[:, None, :].astype(r.dtype)
    hid = jax.nn.silu(jnp.einsum('...nlgd,lde->...nge', r, w1))
    return jnp.einsum('...nge,ef->...ngf', hid, w2)

def _nsa_combine(gates, o_c, o_s, o_w):
    B, T = gates.shape[:2]
    g = jax.nn.sigmoid(gates.astype(jnp.float32)).reshape(B, T, 3, NSA_KV, NSA_R, 1)
    o = g[:, :, 0] * o_c + g[:, :, 1] * o_s + g[:, :, 2] * o_w
    return o.astype(o_c.dtype).reshape(B, T, BR_W)

def _nsa_prompt(q, cmp, slc, win, gates, w1, w2, pe):
    B, T = q.shape[:2]
    nb = T // CMP_BLOCK
    scale = HD ** -0.5
    qg = q.reshape(B, T, NSA_KV, NSA_R, HD)
    tpos = jnp.arange(T)
    blk = jnp.arange(nb)
    kcb = _compress(cmp[:, :, 0], w1[0], w2[0], pe[0])
    vcb = _compress(cmp[:, :, 1], w1[1], w2[1], pe[1])
    s_c = jnp.einsum('btgrd,bngd->btgrn', qg, kcb) * scale
    readable = (blk[None, :] + 1) * CMP_BLOCK - 1 <= tpos[:, None]
    p_c = _masked_softmax(s_c, readable[None, :, None, None, :])
    o_c = jnp.einsum('btgrn,bngd->btgrd', p_c.astype(vcb.dtype), vcb)
    cur = (tpos // CMP_BLOCK)[:, None]
    imp = jnp.sum(p_c, axis=3)
    sel_score = jnp.where((blk[None, :] < cur)[None, :, None, :], imp,
                          jnp.where((blk[None, :] == cur)[None, :, None, :], BIG, NEG))
    n_sel = min(N_SELECT, nb)
    top_v, top_i = lax.top_k(sel_score, n_sel)
    top_ok = top_v > 0.5 * NEG
    slc_b = slc.reshape(B, nb, CMP_BLOCK, 2, NSA_KV, HD)
    bi = jnp.arange(B)[:, None, None, None]
    gi = jnp.arange(NSA_KV)[None, None, :, None]

    def sel_block(i):
        start = i * SLC_Q_BLOCK
        qb = lax.dynamic_slice_in_dim(qg, start, SLC_Q_BLOCK, axis=1)
        idx = lax.dynamic_slice_in_dim(top_i, start, SLC_Q_BLOCK, axis=1)
        ok = lax.dynamic_slice_in_dim(top_ok, start, SLC_Q_BLOCK, axis=1)
        kv = slc_b[bi, idx, :, :, gi]
        s = jnp.einsum('bqgrd,bqgkld->bqgrkl', qb, kv[..., 0, :]) * scale
        qpos = start + jnp.arange(SLC_Q_BLOCK)
        spos = idx[..., None] * CMP_BLOCK + jnp.arange(CMP_BLOCK)
        m = ok[..., None] & (spos <= qpos[None, :, None, None, None])
        p = _masked_softmax(s, m[:, :, :, None], axis=(-2, -1))
        return jnp.einsum('bqgrkl,bqgkld->bqgrd', p.astype(kv.dtype), kv[..., 1, :])

    o_s = lax.map(sel_block, jnp.arange(T // SLC_Q_BLOCK))
    o_s = jnp.moveaxis(o_s, 0, 1).reshape(B, T, NSA_KV, NSA_R, HD)
    span = Q_BLOCK + WINDOW
    win_p = jnp.pad(win, ((0, 0), (WINDOW, 0), (0, 0), (0, 0), (0, 0)))

    def win_block(i):
        start = i * Q_BLOCK
        qb = lax.dynamic_slice_in_dim(qg, start, Q_BLOCK, axis=1)
        kv = lax.dynamic_slice_in_dim(win_p, start, span, axis=1)
        s = jnp.einsum('bqgrd,bsgd->bqgrs', qb, kv[:, :, 0]) * scale
        qpos = start + jnp.arange(Q_BLOCK)
        spos = start - WINDOW + jnp.arange(span)
        m = (spos[None, :] <= qpos[:, None]) & (spos[None, :] >= qpos[:, None] - WINDOW) & (spos[None, :] >= 0)
        p = _masked_softmax(s, m[None, :, None, None, :])
        return jnp.einsum('bqgrs,bsgd->bqgrd', p.astype(kv.dtype), kv[:, :, 1])

    o_w = lax.map(win_block, jnp.arange(T // Q_BLOCK))
    o_w = jnp.moveaxis(o_w, 0, 1).reshape(B, T, NSA_KV, NSA_R, HD)
    return _nsa_combine(gates, o_c, o_s, o_w)

def _nsa_sample(q, cmp, slc, win, gates, pool_cmp, pool_slc, win_state, page_table, l, w1, w2, pe):
    DB, S1 = q.shape[:2]
    past = page_table.shape[1] * PAGE_SIZE
    nb = past // CMP_BLOCK
    scale = HD ** -0.5
    qg = q.reshape(DB, S1, NSA_KV, NSA_R, HD)
    qpos = past + jnp.arange(S1)
    causal = jnp.arange(S1)[None, :] <= jnp.arange(S1)[:, None]
    kc_rows = pool_cmp[l, page_table, :, 0].reshape(DB, past, NSA_KV, HD)
    vc_rows = pool_cmp[l, page_table, :, 1].reshape(DB, past, NSA_KV, HD)
    kcb = _compress(kc_rows, w1[0], w2[0], pe[0])
    vcb = _compress(vc_rows, w1[1], w2[1], pe[1])
    s_c = jnp.einsum('bqgrd,bngd->bqgrn', qg, kcb) * scale
    p_c = jax.nn.softmax(s_c.astype(jnp.float32), axis=-1)
    o_c = jnp.einsum('bqgrn,bngd->bqgrd', p_c.astype(vcb.dtype), vcb)
    imp = jnp.sum(p_c, axis=3)
    k1 = min(N_SELECT - 1, nb)
    _, idx = lax.top_k(imp, k1)
    bpp = PAGE_SIZE // CMP_BLOCK
    phys = page_table[jnp.arange(DB)[:, None, None, None], idx // bpp]
    rows = (idx % bpp)[..., None] * CMP_BLOCK + jnp.arange(CMP_BLOCK)
    gi = jnp.arange(NSA_KV)[None, None, :, None, None]
    kv_sel = pool_slc[l, phys[..., None], rows, :, gi]
    n_past = k1 * CMP_BLOCK
    s_past = (jnp.einsum('bqgrd,bqgkld->bqgrkl', qg, kv_sel[..., 0, :]) * scale).reshape(DB, S1, NSA_KV, NSA_R, n_past)
    s_cur = jnp.einsum('bqgrd,bsgd->bqgrs', qg, slc[:, :, 0]) * scale
    m = jnp.concatenate([jnp.ones((S1, n_past), bool), causal], axis=-1)
    p = _masked_softmax(jnp.concatenate([s_past.astype(jnp.float32), s_cur.astype(jnp.float32)], axis=-1),
                        m[None, :, None, None, :]).astype(q.dtype)
    o_s = (jnp.einsum('bqgrkl,bqgkld->bqgrd', p[..., :n_past].reshape(DB, S1, NSA_KV, NSA_R, k1, CMP_BLOCK), kv_sel[..., 1, :])
           + jnp.einsum('bqgrs,bsgd->bqgrd', p[..., n_past:], slc[:, :, 1]))
    wb = win_state.shape[1]
    kv_w = jnp.concatenate([win_state, win], axis=1)
    spos = past - wb + jnp.arange(wb + S1)
    mw = (spos[None, :] <= qpos[:, None]) & (spos[None, :] >= qpos[:, None] - WINDOW)
    s_w = jnp.einsum('bqgrd,bsgd->bqgrs', qg, kv_w[:, :, 0]) * scale
    p_w = _masked_softmax(s_w, mw[None, :, None, None, :])
    o_w = jnp.einsum('bqgrs,bsgd->bqgrd', p_w.astype(kv_w.dtype), kv_w[:, :, 1])
    return _nsa_combine(gates, o_c, o_s, o_w), kv_w[:, S1:]

def _fox_prompt(q, kv, logf):
    B, T = q.shape[:2]
    scale = HD ** -0.5
    k, v = kv[:, :, 0], kv[:, :, 1]
    c = jnp.swapaxes(jnp.cumsum(logf, axis=1), 1, 2)
    kpos = jnp.arange(T)

    def block(i):
        start = i * Q_BLOCK
        qb = lax.dynamic_slice_in_dim(q, start, Q_BLOCK, axis=1)
        cb = lax.dynamic_slice_in_dim(c, start, Q_BLOCK, axis=2)
        s = jnp.einsum('bqhd,bshd->bhqs', qb, k).astype(jnp.float32) * scale + cb[..., :, None] - c[..., None, :]
        qpos = start + jnp.arange(Q_BLOCK)
        p = _masked_softmax(s, (kpos[None, :] <= qpos[:, None])[None, None])
        return jnp.einsum('bhqs,bshd->bqhd', p.astype(v.dtype), v)

    o = lax.map(block, jnp.arange(T // Q_BLOCK))
    return jnp.moveaxis(o, 0, 1).reshape(B, T, FOX_H * HD)

def _fox_sample(q, kv, logf, pool_kv, pool_logf, page_table, l):
    DB, S1 = q.shape[:2]
    past = page_table.shape[1] * PAGE_SIZE
    scale = HD ** -0.5
    k_past = pool_kv[l, page_table, :, 0].reshape(DB, past, FOX_H, HD)
    v_past = pool_kv[l, page_table, :, 1].reshape(DB, past, FOX_H, HD)
    lf_past = pool_logf[l, page_table].reshape(DB, past, FOX_H).astype(jnp.float32)
    r_past = jnp.swapaxes(lax.cumsum(lf_past, axis=1, reverse=True) - lf_past, 1, 2)
    a_new = jnp.swapaxes(jnp.cumsum(logf, axis=1), 1, 2)
    s_p = jnp.einsum('bqhd,bshd->bhqs', q, k_past).astype(jnp.float32) * scale + a_new[..., :, None] + r_past[..., None, :]
    s_n = jnp.einsum('bqhd,bshd->bhqs', q, kv[:, :, 0]).astype(jnp.float32) * scale + a_new[..., :, None] - a_new[..., None, :]
    causal = jnp.arange(S1)[None, :] <= jnp.arange(S1)[:, None]
    m = jnp.concatenate([jnp.ones((S1, past), bool), causal], axis=-1)
    p = _masked_softmax(jnp.concatenate([s_p, s_n], axis=-1), m[None, None]).astype(q.dtype)
    o = (jnp.einsum('bhqs,bshd->bqhd', p[..., :past], v_past)
         + jnp.einsum('bhqs,bshd->bqhd', p[..., past:], kv[:, :, 1]))
    return o.reshape(DB, S1, FOX_H * HD)

def _mem_kv(mem, g_mem, w_mem_kv):
    B, M = mem.shape[:2]
    mn = _rmsnorm(mem, g_mem)
    return jnp.einsum('bmd,dn->bmn', mn, w_mem_kv).reshape(B, M, 2, MEM_H, MEM_HD)

def _mem_attn(q, mkv):
    B, T = q.shape[:2]
    s = jnp.einsum('bthd,bmhd->bhtm', q, mkv[:, :, 0]).astype(jnp.float32) * (MEM_HD ** -0.5)
    p = jax.nn.softmax(s, axis=-1)
    return jnp.einsum('bhtm,bmhd->bthd', p.astype(mkv.dtype), mkv[:, :, 1]).reshape(B, T, BR_W)

def _merge(o_nsa, o_fox, o_mem, nsilu, fsilu, msilu, bgate, w_branch, w_out, g_post):
    B, T = o_nsa.shape[:2]
    br = jnp.stack([o_nsa * jax.nn.silu(nsilu), o_fox * jax.nn.silu(fsilu), o_mem * jax.nn.silu(msilu)], axis=2)
    z = jnp.einsum('btkw,kwd->btkd', br, w_branch)
    g = jax.nn.sigmoid(bgate.reshape(B, T, N_BRANCH, D_MODEL))
    merged = jnp.sum(g * z, axis=2)
    return _rmsnorm(jnp.einsum('btd,de->bte', merged, w_out), g_post)

def setup_inputs(seed: int = 0) -> dict:
    key = jax.random.key(seed)
    ks = jax.random.split(key, 24)
    f32 = jnp.float32
    n_pages = PAST_LEN // PAGE_SIZE
    n_used = DEC_BATCH * n_pages
    n_pool = n_used + max(1, n_used // 4)
    win_buf = min(WINDOW, PAST_LEN)

    def nrm(k, shape, scale=1.0):
        return scale * jax.random.normal(k, shape, f32)

    perm = jax.random.permutation(ks[8], n_pool)[:n_used]
    return {
        'x_prompt': nrm(ks[0], (BATCH, SEQ, D_MODEL)),
        'x_sample': nrm(ks[1], (DEC_BATCH, DEC_SEQ, D_MODEL)),
        'cache_nsa_cmp': nrm(ks[2], (DEPTH, n_pool, PAGE_SIZE, 2, NSA_KV, HD)),
        'cache_nsa_slc': nrm(ks[3], (DEPTH, n_pool, PAGE_SIZE, 2, NSA_KV, HD)),
        'state_nsa_win': nrm(ks[4], (DEPTH, DEC_BATCH, win_buf, 2, NSA_KV, HD)),
        'cache_fox_kv': nrm(ks[5], (DEPTH, n_pool, PAGE_SIZE, 2, FOX_H, HD)),
        'cache_fox_logf': jax.nn.log_sigmoid(3.0 + nrm(ks[6], (DEPTH, n_pool, PAGE_SIZE, FOX_H))),
        'cache_mem_kv': nrm(ks[7], (DEPTH, DEC_BATCH, N_MEM, 2, MEM_H, MEM_HD)),
        'page_table': perm.reshape(DEC_BATCH, n_pages).astype(jnp.int32),
        'mem_prompt': nrm(ks[9], (BATCH, N_MEM, D_MODEL)),
        'g_pre': 1.0 + nrm(ks[10], (DEPTH, D_MODEL), 0.1),
        'g_post': 1.0 + nrm(ks[11], (DEPTH, D_MODEL), 0.1),
        'g_mem': 1.0 + nrm(ks[12], (DEPTH, D_MODEL), 0.1),
        'w_in': nrm(ks[13], (DEPTH, D_MODEL, N_IN), D_MODEL ** -0.5),
        'b_fgate': jax.random.uniform(ks[14], (DEPTH, FOX_H), f32, 1.0, 4.0),
        'w_mem_kv': nrm(ks[15], (DEPTH, D_MODEL, 2 * BR_W), D_MODEL ** -0.5),
        'w_cmp1': nrm(ks[16], (DEPTH, 2, CMP_BLOCK, HD, HD), (CMP_BLOCK * HD) ** -0.5),
        'w_cmp2': nrm(ks[17], (DEPTH, 2, HD, HD), HD ** -0.5),
        'pe_cmp': nrm(ks[18], (DEPTH, 2, CMP_BLOCK, HD), 0.1),
        'w_branch': nrm(ks[19], (DEPTH, N_BRANCH, BR_W, D_MODEL), BR_W ** -0.5),
        'w_out': nrm(ks[20], (DEPTH, D_MODEL, D_MODEL), D_MODEL ** -0.5),
    }

def reference(x_prompt, x_sample, cache_nsa_cmp, cache_nsa_slc, state_nsa_win, cache_fox_kv,
              cache_fox_logf, cache_mem_kv, page_table, mem_prompt, g_pre, g_post, g_mem, w_in,
              b_fgate, w_mem_kv, w_cmp1, w_cmp2, pe_cmp, w_branch, w_out):
    T = x_prompt.shape[1]
    S1 = x_sample.shape[1]
    past = page_table.shape[1] * PAGE_SIZE
    pos_p = jnp.arange(T, dtype=jnp.float32)
    pos_s = jnp.arange(S1, dtype=jnp.float32) + jnp.float32(past)
    xp, xs = x_prompt, x_sample
    p_cmp, p_slc, p_win, p_fkv, p_flog, p_mem = [], [], [], [], [], []
    s_cmp, s_slc, s_win, s_fkv, s_flog = [], [], [], [], []
    for l in range(DEPTH):
        (q, cmp, slc, win, ngate, nsilu, fq, fkv, flog, fsilu, mq, msilu, bgate) = _project(
            _rmsnorm(xp, g_pre[l]), w_in[l], b_fgate[l], pos_p)
        o_nsa = _nsa_prompt(q, cmp, slc, win, ngate, w_cmp1[l], w_cmp2[l], pe_cmp[l])
        o_fox = _fox_prompt(fq, fkv, flog)
        mkv = _mem_kv(mem_prompt, g_mem[l], w_mem_kv[l])
        o_mem = _mem_attn(mq, mkv)
        xp = xp + _merge(o_nsa, o_fox, o_mem, nsilu, fsilu, msilu, bgate, w_branch[l], w_out[l], g_post[l])
        p_cmp.append(cmp)
        p_slc.append(slc)
        p_win.append(win[:, T - min(WINDOW, T):])
        p_fkv.append(fkv)
        p_flog.append(flog)
        p_mem.append(mkv)
        (q, cmp, slc, win, ngate, nsilu, fq, fkv, flog, fsilu, mq, msilu, bgate) = _project(
            _rmsnorm(xs, g_pre[l]), w_in[l], b_fgate[l], pos_s)
        o_nsa, new_win = _nsa_sample(q, cmp, slc, win, ngate, cache_nsa_cmp, cache_nsa_slc, state_nsa_win[l],
                                     page_table, l, w_cmp1[l], w_cmp2[l], pe_cmp[l])
        o_fox = _fox_sample(fq, fkv, flog, cache_fox_kv, cache_fox_logf, page_table, l)
        o_mem = _mem_attn(mq, cache_mem_kv[l])
        xs = xs + _merge(o_nsa, o_fox, o_mem, nsilu, fsilu, msilu, bgate, w_branch[l], w_out[l], g_post[l])
        s_cmp.append(cmp)
        s_slc.append(slc)
        s_win.append(new_win)
        s_fkv.append(fkv)
        s_flog.append(flog)
    return (xp, xs, jnp.stack(p_cmp), jnp.stack(p_slc), jnp.stack(p_win), jnp.stack(p_fkv), jnp.stack(p_flog), jnp.stack(p_mem), jnp.stack(s_cmp), jnp.stack(s_slc), jnp.stack(s_win), jnp.stack(s_fkv), jnp.stack(s_flog))


_drawn_inputs = setup_inputs


def setup_inputs(seed=0):
    import zlib

    import numpy as np

    out = dict(_drawn_inputs(seed))
    spreads = {}
    factors = {}
    for name, (base, spread) in spreads.items():
        noise = np.random.default_rng([zlib.crc32(name.encode()), seed]).standard_normal(out[name].shape)
        drawn = base * np.exp(spread * noise) if base else spread * noise
        out[name] = __import__('jax').numpy.asarray(drawn.astype(out[name].dtype))
    for name, factor in factors.items():
        out[name] = (out[name] * factor).astype(out[name].dtype)
    return out
```

```python
from contextlib import ExitStack

import numpy as np

import concourse.bass as bass
from concourse import mybir

F32 = mybir.dt.float32
I32 = mybir.dt.int32
U32 = mybir.dt.uint32
ACT = mybir.ActivationFunctionType
ALU = mybir.AluOpType
AX = mybir.AxisListType.X
P = 128
D = 1024
DC = D // P
T = 512
NT = T // P
NB = 8
TT = T + NB
TH = TT // 2
HD = 64
H = 8
G = 2
R = H // G
MH = 4
NM = 256
PAGES = 32
POOL = 320
CB = 64
NBLK = PAGES * P // CB
NSEL = 15
WIN = 512
BRW = 512
EPS = 1e-6
NEG = -1e30
TINY = 1e-30
SCALE = HD ** -0.5
MSCALE = 128 ** -0.5

C_Q, C_CMP, C_SLC, C_WIN, C_GATE, C_NSILU = 0, 512, 768, 1024, 1280, 1304
C_FQ, C_FKV, C_FLOG, C_FSILU = 1816, 2328, 3352, 3360
C_MQ, C_MSILU, C_BGATE, N_IN = 3872, 4384, 4896, 7968
M_CMP, M_SLC, M_WIN, M_FK, M_FV, M_ALL = 0, 256, 512, 768, 1280, 1792
K_Q, K_FQ, K_MQ, K_FK, K_KD, K_ALL = 0, 4, 8, 12, 16, 20

CONSTS = dict(ident=128, ones=128, swap=128, dup=256, dupall=128, causal=128, later=128, wsuf=128,
              cum=512, ropec=TT, ropes=TT, cneg=32, c01=32, diag=NB, newneg=1, lcol=1,
              blk=NBLK, blkrow=NBLK, jmask=8, epart=128, headrow=H)
AT, at = {}, 0
for name, n in CONSTS.items():
    AT[name] = at
    at += n
NC = at


class Shared:
    pass


class Chunk:

    def __init__(self, col, w, mem, store=None, rope=None, turn=None, dup=None, chunks=1, last=None):
        self.col, self.w, self.mem, self.store, self.rope, self.turn = col, w, mem, store, rope, turn
        self.dup, self.chunks, self.last = dup, chunks, last


def constants():
    c = np.zeros((P, NC), np.float32)
    p = np.arange(P)
    col = lambda n: c[:, AT[n]:AT[n] + CONSTS[n]]
    col("ident")[:] = np.eye(P)
    col("ones")[:] = 1
    half = 8
    r = p % HD
    for a in range(P):
        if r[a] < half:
            col("swap")[a, a + half] = col("swap")[a + half, a] = 1
    for g in range(2):
        for m in range(P):
            col("dup")[g * 64 + m % 64, g * P + m] = 1
    col("dupall")[:] = (p[:, None] % 64) == (p[None] % 64)
    col("causal")[:] = np.where(p[None] <= p[:, None], 0, NEG)
    col("later")[:] = p[:, None] > p[None]
    col("wsuf")[:] = (p[:, None] // PAGES == p[None] // PAGES) & (p[:, None] > p[None])
    col("cum")[:] = np.arange(512)[None] >= p[:, None]
    pos = np.concatenate([np.arange(T), np.full(NB, PAGES * P)]).astype(np.float32)
    inv = np.float32(500000.0) ** (-np.arange(half, dtype=np.float32) / np.float32(half))
    ang = (pos[None] * inv[:, None]).astype(np.float32)
    col("ropec")[:] = 1
    for a in range(P):
        if r[a] < 2 * half:
            col("ropec")[a] = np.cos(ang[r[a] % half])
            col("ropes")[a] = np.sin(ang[r[a] % half]) * (-1 if r[a] < half else 1)
    sel = np.zeros((24, 12 * P + H * P), np.float32)
    for h in range(H):
        sel[h, (12 + h) * P:(13 + h) * P] = 1
    t = (np.arange(NT)[None, :, None, None] * P + p[:, None, None, None])
    b = (np.arange(2)[None, None, :, None] + 2 * np.arange(NT)[None, None, None, :])
    ok = ((b + 1) * CB - 1 <= t).reshape(P, 32)
    col("cneg")[:] = np.where(ok, 0, NEG)
    col("c01")[:] = ok
    col("diag")[:] = np.where(p[:, None] == np.arange(NB)[None], 0, NEG)
    col("newneg")[:, 0] = np.where(p < 64, 0, NEG)
    col("lcol")[:, 0] = p % CB
    col("blk")[:] = np.arange(NBLK)[None]
    col("blkrow")[:] = (np.arange(NBLK)[None] % 2) * CB
    col("jmask")[:] = (p[:, None] // 2) == np.arange(8)[None]
    col("epart")[:] = (p[:, None] % 2) == (p[None] // 64)
    col("headrow")[:] = (p[:, None] // 8) == np.arange(H)[None]
    for br in range(3):
        for ch in range(4):
            for m in range(P):
                sel[br * 8 + 2 * ch + m // 64, (br * 4 + ch) * P + m] = 1
    return c, sel


def compress(k):
    nc, ps, wait = k.nc, k.ps, k.wait
    with ExitStack() as cx:
        sb, sem = k.makers(cx)
        w1 = sb("c_w1", [P, 2, CB, P])
        page = [sb(f"c_page{i}", [P, PAGES + 1, 256]) for i in range(2)]
        const_in, table_in, w_in, pe_in = sem("c_const_in"), sem("c_table_in"), sem("c_w_in"), sem("c_pe_in")
        w_zero, pe_placed = sem("c_w_zero"), sem("c_pe_placed")
        page_in = [sem(f"c_page_in{i}") for i in range(2)]
        page_free = [sem(f"c_page_free{i}") for i in range(2)]
        hid_done, act_bias, z_done, e_done, h_done, h_free = (sem("c_hid_done"), sem("c_bias"), sem("c_z_done"),
                                                     sem("c_e_done"), sem("c_h_done"), sem("c_h_free"))
        blocks_done, blocks_out = sem("c_blocks_done"), sem("c_blocks_out")
        pe = sb("c_pe", [P, 2, HD])
        z = sb("c_z", [P, 2, 2, PAGES + 1])
        ez = sb("c_ez", [P, 2, 2, PAGES + 1])
        hid = sb("c_hid", [P, 2, 2, PAGES])
        hp = ps[0][:, 0:132].rearrange("p (v g n) -> p v g n", v=2, g=2)
        w1_d = k.w_cmp1[0]

        k.prime(*page_free, z_done, h_done, blocks_done, blocks_out)
        with nc.Block() as block:
            @block.sync
            def _(sp):
                sp.dma_start(k.cst[:, :], k.consts).then_inc(const_in, 16)
                sp.dma_start(k.table[:, :], k.page_table.rearrange("b n -> (b n)").unsqueeze(0)).then_inc(table_in, 16)
                for half in range(2):
                    rows = slice(64 * half, 64 * half + 64)
                    sp.dma_start(pe[rows, :, :], k.pe_cmp[0].rearrange("v l d -> l v d")).then_inc(pe_in, 16)
                    for v in range(2):
                        sp.dma_start(w1[rows, v, :, rows], w1_d[v]).then_inc(w_in, 16)
                        sp.dma_start(k.w2b[rows, v, rows], k.w_cmp2[0, v]).then_inc(w_in, 16)
                        for other in range(2):
                            sp.dma_start(k.w2d[rows, v, 64 * other:64 * other + 64], k.w_cmp2[0, v]).then_inc(w_in, 16)
                wait(sp, table_in, 16)
                with sp.Fori(0, NB // 2) as pair:
                    for s in range(2):
                        with sp.Fori(0, PAGES) as j:
                            wait(sp, page_free[s], pair)
                            pg = sp.value_load(k.table[0:1, bass.ds(pair * (2 * PAGES) + s * PAGES + j, 1)],
                                               min_val=0, max_val=POOL - 1)
                            sp.dma_start(page[s][:, bass.ds(j, 1), :],
                                         k.cache_cmp[bass.ds(pg, 1), :, :].rearrange("a p n -> p a n"))\
                              .then_inc(page_in[s], 16)
                wait(sp, const_in, 16)
                wait(sp, w_in, 16 * 16)

            @block.gpsimd
            def _(pool):
                for v in range(2):
                    nc.gpsimd.memset(w1[0:64, v, :, 64:128], 0.0)
                    nc.gpsimd.memset(w1[64:128, v, :, 0:64], 0.0)
                    nc.gpsimd.memset(k.w2b[0:64, v, 64:128], 0.0)
                    nc.gpsimd.memset(k.w2b[64:128, v, 0:64], 0.0).then_inc(w_zero, 1)
                wait(pool, w_zero, 2)
                wait(pool, pe_in, 32)
                for s in range(2):
                    for g in range(2):
                        dst = page[s][:, PAGES, :].rearrange("p (v g d) -> p v g d", v=2, g=2)[:, :, g, :]
                        nc.gpsimd.tensor_copy(dst, pe[:, :, :]).then_inc(pe_placed, 1)

            @block.tensor
            def _(te):
                wait(te, w_in, 16 * 16)
                wait(te, w_zero, 2)
                wait(te, pe_placed, 4)
                with te.Fori(0, NB // 2) as pair:
                    for s in range(2):
                        wait(te, page_in[s], pair * (16 * PAGES) + 16 * PAGES)
                        wait(te, z_done, pair * 4 + 2 * s)
                        rows = page[s][:, :, :].rearrange("p n (v g d) -> p v d g n", v=2, g=2)
                        for v in range(2):
                            for d in range(HD):
                                last = nc.tensor.matmul(hp[:, v], w1[:, v, d, :], rows[:, v, d],
                                                        start=d == 0, stop=d == HD - 1)
                        last.then_inc(page_free[s], 1)
                        wait(te, h_done, pair * 2 + s + 1)
                        wait(te, blocks_out, pair * 4 + 2 * s)
                        nc.tensor.matmul(ps[1][:, 0:64], k.w2b[:, 0, :], hid[:, 0, :, :].rearrange("p g n -> p (g n)"),
                                         start=True, stop=True)
                        nc.tensor.matmul(ps[2][0:64, 0:128], hid[:, 1, :, :].rearrange("p g n -> p (g n)"),
                                         k.w2b[:, 1, :], start=True, stop=True).then_inc(blocks_done, 1)

            @block.vector
            def _(ve):
                with ve.Fori(0, NB // 2) as pair:
                    for s in range(2):
                        wait(ve, page_free[s], pair + 1)
                        nc.vector.tensor_copy(k.pebias[:, :], hp[:, :, 0, PAGES]).then_inc(act_bias, 1)
                        wait(ve, act_bias, pair * 2 + s + 1)
                        for v in range(2):
                            nc.vector.tensor_scalar(z[:, v], hp[:, v], k.pebias[:, v:v + 1], None, ALU.add).then_inc(z_done, 1)
                        wait(ve, e_done, pair * 4 + 2 * s + 1)
                        nc.vector.tensor_scalar_add(ez[:, :, :, :], ez[:, :, :, :], 1.0).then_inc(e_done, 1)
                        wait(ve, e_done, pair * 4 + 2 * s + 2)
                        nc.vector.reciprocal(ez[:, :, :, :], ez[:, :, :, :]).then_inc(h_free, 1)
                        wait(ve, h_free, pair * 2 + s + 1)
                        wait(ve, blocks_done, pair * 2 + s)
                        nc.vector.tensor_tensor(hid[:, :, :, :], z[:, :, :, 0:PAGES], ez[:, :, :, 0:PAGES],
                                                ALU.mult).then_inc(h_done, 1)

            @block.scalar
            def _(sc):
                with sc.Fori(0, NB // 2) as pair:
                    for s in range(2):
                        wait(sc, z_done, pair * 4 + 2 * s + 2)
                        wait(sc, h_done, pair * 2 + s)
                        nc.scalar.activation(ez[:, :, :, :], z[:, :, :, :], ACT.Exp, scale=-1.0).then_inc(e_done, 1)
                        wait(sc, blocks_done, pair * 2 + s + 1)
                        nc.scalar.activation(k.kcb[:, bass.ds(pair * 2 + s, 1), :], ps[1][:, 0:64].unsqueeze(1), ACT.Copy).then_inc(blocks_out, 1)
                        nc.scalar.activation(k.vcb[:, bass.ds(pair * 2 + s, 1), :], ps[2][0:64, 0:128].unsqueeze(1), ACT.Copy).then_inc(blocks_out, 1)


def forget(k):
    nc, ps = k.nc, k.ps
    with ExitStack() as cx:
        sb, sem = k.makers(cx)
        logf = sb("g_logf", [P, 2, P * H])
        rows = sb("g_rows", [P, 2, H, P])
        total = sb("g_total", [P, 2, P])
        idx = sb("g_idx", [P, 2], I32)
        idx_in, logf_in = sem("g_idx_in"), k.logf_in
        turned, rows_out, tot_done, tot_out, sum_done, sum_out = (sem(n) for n in (
            "g_turned", "g_rows_out", "g_tot_done", "g_tot_out", "g_sum_done", "g_sum_out"))
        r = k.rpast[:, :, :].rearrange("p (a c n) h -> p a h c n", a=2, n=PAGES)
        with nc.Block() as block:
            @block.sync
            def _(sp):
                for a in range(2):
                    sp.dma_start(idx[:, a:a + 1], k.page_table.rearrange("(a c) n -> a (c n)", a=2)[a].unsqueeze(1))\
                      .then_inc(idx_in, 16)
                sp.wait_ge(idx_in, 32)

            @block.gpsimd
            def _(pool):
                pool.wait_ge(idx_in, 32)
                for a in range(2):
                    nc.gpsimd.indirect_dma_start(
                        out=logf[:, a, :], out_offset=None, in_=k.cache_logf,
                        in_offset=bass.IndirectOffsetOnAxis(ap=idx[:, a:a + 1].bitcast(U32), axis=0),
                        bounds_check=POOL - 1, oob_is_err=False).then_inc(logf_in[a], 16)

            @block.tensor
            def _(te):
                for a in range(2):
                    te.wait_ge(logf_in[a], 16)
                    for hh in range(2):
                        for h in range(4):
                            src = logf[:, a, :].rearrange("p (r h) -> p h r", h=H)[:, 4 * hh + h]
                            last = nc.tensor.transpose(ps[2 * a + hh][:, h * P:(h + 1) * P], src, k.ident)
                        last.then_inc(turned, 1)
                for n in range(2 * H):
                    a, h = n // H, n % H
                    te.wait_ge(rows_out, n // 4 + 1)
                    if n >= 2:
                        te.wait_ge(tot_out, n - 1)
                    nc.tensor.matmul(ps[4 + n % 2][:, 0:P], rows[:, a, h, :], k.ones, start=True, stop=True).then_inc(tot_done, 1)
                    if n >= 2:
                        te.wait_ge(sum_out, n - 1)
                    te.wait_ge(tot_out, n + 1)
                    nc.tensor.matmul(ps[6 + n % 2][:, 0:P], k.later, rows[:, a, h, :], start=True, stop=False)
                    nc.tensor.matmul(ps[6 + n % 2][:, 0:P], total[:, n % 2, :], k.wsuf, start=False, stop=True).then_inc(sum_done, 1)

            @block.scalar
            def _(sc):
                for n in range(4):
                    sc.wait_ge(turned, n + 1)
                    nc.scalar.activation(rows[:, n // 2, 4 * (n % 2):4 * (n % 2) + 4, :],
                                         ps[n][:, :].rearrange("p (h n) -> p h n", h=4), ACT.Copy).then_inc(rows_out, 1)
                for n in range(2 * H):
                    sc.wait_ge(tot_done, n + 1)
                    if n >= 2:
                        sc.wait_ge(sum_done, n - 1)
                    nc.scalar.activation(total[:, n % 2, :], ps[4 + n % 2][:, 0:P], ACT.Copy).then_inc(tot_out, 1)

            @block.vector
            def _(ve):
                for n in range(2 * H):
                    ve.wait_ge(sum_done, n + 1)
                    nc.vector.tensor_copy(r[:, n // H, n % H], ps[6 + n % 2][:, 0:P].rearrange("p (c n) -> p c n", c=4)).then_inc(sum_out, 1)


def norm(k):
    nc, ps = k.nc, k.ps
    with ExitStack() as cx:
        sb, sem = k.makers(cx)
        NX, NMT = NT + 1, NM // P
        x = sb("n_x", [P, NX + NMT, D])
        gb = sb("n_g", [P, 2, D])
        sq = sb("n_sq", [P, D])
        ss = sb("n_ss", [P, NX + NMT])
        x_in = [sem(f"n_x_in{i}") for i in range(NX + NMT)]
        g_in, sq_done, rstd_done, act_rstd, scaled, turned, placed, ss_set = (sem(n) for n in (
            "n_g_in", "n_sq_done", "n_rstd_done", "n_act_rstd", "n_scaled", "n_turned", "n_placed", "n_ss_set"))
        wide = [P] * NT + [NB] + [P] * NMT

        with nc.Block() as block:
            @block.sync
            def _(sp):
                for t in range(NT):
                    sp.dma_start(x[:, t, :], k.x_prompt[t * P:(t + 1) * P, :]).then_inc(x_in[t], 16)
                sp.dma_start(x[0:NB, NT, :], k.x_sample).then_inc(x_in[NT], 16)
                for i, g in enumerate((k.g_pre, k.g_mem)):
                    sp.dma_start(gb[:, i, :], g[0].partition_broadcast(P)).then_inc(g_in, 16)
                for t in range(NMT):
                    sp.dma_start(x[:, NX + t, :], k.mem_prompt[t * P:(t + 1) * P, :]).then_inc(x_in[NX + t], 16)

            @block.scalar
            def _(sc):
                sc.wait_ge(ss_set, 1)
                for t, w in enumerate(wide):
                    sc.wait_ge(x_in[t], 16)
                    if t:
                        sc.wait_ge(sq_done, t)
                    nc.scalar.activation(sq[0:w, :], x[0:w, t, :], ACT.Square, accum_out=ss[0:w, t:t + 1]).then_inc(sq_done, 1)
                sc.wait_ge(rstd_done, 1)
                nc.scalar.activation(ss[:, :], ss[:, :], ACT.Ln).then_inc(act_rstd, 1)
                sc.wait_ge(act_rstd, 1)
                nc.scalar.activation(ss[:, :], ss[:, :], ACT.Exp, scale=-0.5).then_inc(act_rstd, 1)
                for t, w in enumerate(wide):
                    for half in range(2):
                        n = 2 * t + half
                        sc.wait_ge(turned, n + 1)
                        src = ps[n % 4][:, :].rearrange("p (c n) -> p c n", c=4)[:, :, 0:w]
                        if t < NX:
                            dst = k.xnT[:, 4 * half:4 * half + 4, t * P:t * P + w]
                        else:
                            dst = k.mnT[:, 4 * half:4 * half + 4, (t - NX) * P:(t - NX + 1) * P]
                        nc.scalar.activation(dst, src, ACT.Copy).then_inc(placed, 1)

            @block.vector
            def _(ve):
                ve.wait_ge(sq_done, NX + NMT)
                nc.vector.tensor_scalar(ss[:, :], ss[:, :], 1.0 / D, EPS, ALU.mult, ALU.add).then_inc(rstd_done, 1)
                ve.wait_ge(act_rstd, 2)
                ve.wait_ge(g_in, 32)
                for t, w in enumerate(wide):
                    nc.vector.scalar_tensor_tensor(out=x[0:w, t, :], in0=x[0:w, t, :], scalar=ss[0:w, t:t + 1],
                                                   in1=gb[0:w, int(t >= NX), :], op0=ALU.mult, op1=ALU.mult).then_inc(scaled, 1)

            @block.gpsimd
            def _(pool):
                nc.gpsimd.memset(ss[:, :], 1.0).then_inc(ss_set, 1)

            @block.tensor
            def _(te):
                for t, w in enumerate(wide):
                    te.wait_ge(scaled, t + 1)
                    for half in range(2):
                        n = 2 * t + half
                        if n >= 4:
                            te.wait_ge(placed, n - 3)
                        for c in range(4):
                            f = 4 * half + c
                            last = nc.tensor.transpose(ps[n % 4][:, c * P:c * P + w], x[0:w, t, f * P:(f + 1) * P], k.ident[0:w, 0:w])
                        last.then_inc(turned, 1)


def project(k):
    nc, ps = k.nc, k.ps
    chunks = []

    def add(col, w=P, mem=False, store=None, rope=False, turn=None, dup=None):
        chunks.append(Chunk(col=col, w=w, mem=mem, store=store, rope=rope, turn=turn, dup=dup))

    for c in range(4):
        add(C_Q + c * P, store=("fm", K_Q + c), rope=True)
    add(C_CMP, rope=True, turn=M_CMP)
    add(C_CMP + P, turn=M_CMP + P)
    add(C_SLC, rope=True, turn=M_SLC, dup=K_KD)
    add(C_SLC + P, turn=M_SLC + P)
    add(C_WIN, rope=True, turn=M_WIN, dup=K_KD + 2)
    add(C_WIN + P, turn=M_WIN + P)
    add(C_GATE, 24, store=("gate", 0))
    for c in range(4):
        add(C_FQ + c * P, store=("fm", K_FQ + c))
    for c in range(4):
        add(C_FKV + c * P, store=("fm", K_FK + c), turn=M_FK + c * P)
    for c in range(4):
        add(C_FKV + BRW + c * P, turn=M_FV + c * P)
    add(C_FLOG, 8, store=("logf", 0))
    for c in range(4):
        add(C_MQ + c * P, store=("fm", K_MQ + c))
    for c in range(4):
        add(c * P, mem=True, store=("memk", c), turn=c * P)
    for c in range(4):
        add(BRW + c * P, mem=True, turn=BRW + c * P)

    loads = []
    for n, ch in enumerate(chunks):
        prev = loads[-1] if loads else None
        if prev and prev.chunks == 1 and prev.mem == ch.mem and prev.col + P == ch.col and prev.w == P and ch.w == P:
            prev.w, prev.chunks, prev.last = 2 * P, 2, n
        else:
            loads.append(Chunk(col=ch.col, w=ch.w, mem=ch.mem, chunks=1, last=n))
        ch.load, ch.off = len(loads) - 1, ch.col - loads[-1].col
    ropes = turns = dups = 0
    for ch in chunks:
        ch.rope_no = ropes = ropes + bool(ch.rope)
        ch.turn_no = turns = turns + (ch.turn is not None)
        ch.dup_no = dups = dups + (ch.dup is not None)
    RING, STG = 2, 3

    with ExitStack() as cx:
        sb, sem = k.makers(cx)
        ring = [sb(f"p_w{i}", [P, DC, 2 * P]) for i in range(RING)]
        stg = [sb(f"p_stg{i}", [P, 2, TH]) for i in range(STG)]
        t1, t2 = sb("p_t1", [P, 2, TH]), sb("p_t2", [P, 2, TH])
        w_in = [sem(f"p_w_in{i}") for i in range(RING)]
        (proj_done, stg_ready, swap_done, t1_done, t2_done, rope_done, turned, placed, dup_done, dup_out) = (
            sem("p_" + n) for n in ("proj_done", "stg_ready", "swap_done", "t1_done", "t2_done", "rope_done",
                                    "turned", "placed", "dup_done", "dup_out"))
        pj = [[ps[0], ps[1]], [ps[2], ps[3]]]
        rp, tp, tsp = [ps[4], ps[5]], ps[6], ps[7]
        halves = lambda a: a.rearrange("p (i n) -> p i n", i=2)

        def place(ch):
            kind, i = ch.store if ch.store else ("stg", 0)
            if kind == "fm":
                return halves(k.fm[:, i, :])
            if kind == "gate":
                return halves(k.gate[:, :])
            if kind == "logf":
                return halves(k.logf[:, :])
            if kind == "memk":
                return k.mkT[:, i, :]
            s = stg[ch.n % STG]
            return s[:, 0, 0:NM] if ch.mem else s[:, :, :]

        for n, ch in enumerate(chunks):
            ch.n = n
            ch.first = stg[n % STG][:, :, :] if ch.rope else place(ch)
            ch.final = place(ch)
            ch.uses_stg = ch.store is None or ch.rope

        def free_of(ch, engine):
            if ch.dup is not None:
                engine.wait_ge(dup_done, 2 * ch.dup_no)
            elif ch.turn is not None:
                engine.wait_ge(turned, ch.turn_no)
            if ch.rope:
                engine.wait_ge(rope_done, ch.rope_no)

        with nc.Block() as block:
            @block.sync
            def _(sp):
                for i, ld in enumerate(loads):
                    if i >= RING:
                        sp.wait_ge(proj_done, loads[i - RING].last + 1)
                    src = (k.w_mem if ld.mem else k.w_in)[:, ld.col:ld.col + ld.w]
                    sp.dma_start(ring[i % RING][:, :, 0:ld.w], src.rearrange("(c p) n -> p c n", p=P)).then_inc(w_in[i % RING], 16)

            @block.tensor
            def _(te):
                def product(ch):
                    te.wait_ge(w_in[ch.load % RING], 16 * (ch.load // RING + 1))
                    if ch.n >= 2:
                        te.wait_ge(stg_ready, ch.n - 1)
                    w = ring[ch.load % RING]
                    for i in range(1 if ch.mem else 2):
                        for c in range(DC):
                            rhs = k.mnT[:, c, :] if ch.mem else k.xnT[:, c, i * TH:(i + 1) * TH]
                            last = nc.tensor.matmul(pj[ch.n % 2][i][0:ch.w, 0:NM if ch.mem else TH],
                                                    w[:, c, ch.off:ch.off + ch.w], rhs, start=c == 0, stop=c == DC - 1)
                    last.then_inc(proj_done, 1)

                def swap(ch):
                    te.wait_ge(stg_ready, ch.n + 1)
                    te.wait_ge(t1_done, ch.rope_no - 1)
                    if ch.dup_no - (ch.dup is not None):
                        te.wait_ge(dup_out, 2 * (ch.dup_no - (ch.dup is not None)))
                    for i in range(2):
                        last = nc.tensor.matmul(rp[i][:, 0:TH], k.swap, ch.first[:, i, :], start=True, stop=True)
                    last.then_inc(swap_done, 1)

                def turn(ch):
                    te.wait_ge(stg_ready, ch.n + 1)
                    if ch.rope:
                        te.wait_ge(rope_done, ch.rope_no)
                    if ch.turn_no > 1:
                        te.wait_ge(placed, 2 * (ch.turn_no - 1))
                    src = ch.final if ch.mem else ch.final
                    flat = src if ch.mem else src.rearrange("p i n -> p (i n)")
                    for t in range(NM // P if ch.mem else NT):
                        last = nc.tensor.transpose(tp[:, t * P:(t + 1) * P], flat[:, t * P:(t + 1) * P], k.ident)
                    if not ch.mem:
                        last = nc.tensor.transpose(tsp[0:NB, 0:P], flat[:, T:TT], k.ident)
                    last.then_inc(turned, 1)
                    if ch.dup is not None:
                        for g in range(2):
                            te.wait_ge(t1_done, ch.rope_no)
                            if ch.dup_no > 1 or g:
                                te.wait_ge(dup_out, 2 * (ch.dup_no - 1) + g)
                            for i in range(2):
                                last = nc.tensor.matmul(rp[i][:, 0:TH], k.dup[:, g * P:(g + 1) * P], ch.final[:, i, :], start=True, stop=True)
                            last.then_inc(dup_done, 1)

                for n in range(len(chunks) + 2):
                    if n < len(chunks):
                        product(chunks[n])
                    if 1 <= n <= len(chunks) and chunks[n - 1].rope:
                        swap(chunks[n - 1])
                    if n >= 2 and chunks[n - 2].turn is not None:
                        turn(chunks[n - 2])

            @block.scalar
            def _(sc):
                def copies(ch):
                    for g in range(2):
                        sc.wait_ge(dup_done, 2 * (ch.dup_no - 1) + g + 1)
                        for i in range(2):
                            last = nc.scalar.activation(halves(k.fm[:, ch.dup + g, :])[:, i, :], rp[i][:, 0:TH], ACT.Copy)
                        last.then_inc(dup_out, 1)

                for n in range(len(chunks) + 3):
                    if n < len(chunks):
                        ch = chunks[n]
                        sc.wait_ge(proj_done, n + 1)
                        if n >= STG and ch.uses_stg:
                            for old in range(n - STG, -1, -STG):
                                if chunks[old].uses_stg:
                                    free_of(chunks[old], sc)
                                    break
                        if ch.mem:
                            nc.scalar.activation(ch.first, pj[n % 2][0][:, 0:NM], ACT.Copy).then_inc(stg_ready, 1)
                        else:
                            nc.scalar.activation(ch.first[0:ch.w, 0, :], pj[n % 2][0][0:ch.w, 0:TH], ACT.Copy)
                            nc.scalar.activation(ch.first[0:ch.w, 1, :], pj[n % 2][1][0:ch.w, 0:TH], ACT.Copy).then_inc(stg_ready, 1)
                    if n >= 2 and n - 2 < len(chunks) and chunks[n - 2].dup is not None:
                        copies(chunks[n - 2])

            @block.gpsimd
            def _(pool):
                for ch in chunks:
                    if ch.rope:
                        pool.wait_ge(stg_ready, ch.n + 1)
                        if ch.rope_no > 1:
                            pool.wait_ge(rope_done, ch.rope_no - 1)
                        nc.gpsimd.tensor_tensor(t2[:, :, :], ch.first, halves(k.ropec), ALU.mult).then_inc(t2_done, 1)

            @block.vector
            def _(ve):
                def rope(ch):
                    ve.wait_ge(swap_done, ch.rope_no)
                    if ch.rope_no > 1:
                        ve.wait_ge(rope_done, ch.rope_no - 1)
                    for i in range(2):
                        last = nc.vector.tensor_tensor(t1[:, i, :], rp[i][:, 0:TH], halves(k.ropes)[:, i, :], ALU.mult)
                    last.then_inc(t1_done, 1)
                    ve.wait_ge(t1_done, ch.rope_no)
                    ve.wait_ge(t2_done, ch.rope_no)
                    nc.vector.tensor_tensor(ch.final, t1[:, :, :], t2[:, :, :], ALU.add).then_inc(rope_done, 1)

                def row(ch):
                    ve.wait_ge(turned, ch.turn_no)
                    if ch.mem:
                        nc.vector.tensor_copy(k.mrow[:, 0, ch.turn:ch.turn + P], tp[:, 0:P]).then_inc(placed, 1)
                        nc.vector.tensor_copy(k.mrow[:, 1, ch.turn:ch.turn + P], tp[:, P:2 * P]).then_inc(placed, 1)
                    else:
                        nc.vector.tensor_copy(k.row[:, :, ch.turn:ch.turn + P], tp[:, :].rearrange("p (t n) -> p t n", t=NT)).then_inc(placed, 1)
                        nc.vector.tensor_copy(k.srow[:, ch.turn:ch.turn + P], tsp[0:NB, 0:P]).then_inc(placed, 1)

                for n in range(len(chunks) + 2):
                    if 1 <= n <= len(chunks) and chunks[n - 1].rope:
                        rope(chunks[n - 1])
                    if n >= 2 and chunks[n - 2].turn is not None:
                        row(chunks[n - 2])


def gates(k):
    nc, ps = k.nc, k.ps
    with ExitStack() as cx:
        sb, sem = k.makers(cx)
        e8 = sb("a_e8", [H, TT])
        m8 = sb("a_m8", [H, TT])
        bf = sb("a_bf", [H, 1])
        lrow = sb("a_lrow", [P, NT, H])
        qs = sb("a_qs", [P, 8, NB])
        gsig = sb("a_gsig", [24, TT])
        gsel = sb("a_gsel", [24, 12 * P])
        b_in, gsel_in, out_done = sem("a_b_in"), sem("a_gsel_in"), sem("a_out_done")
        va, vb, vc = sem("a_vector_step"), sem("a_scalar_step"), sem("a_scalar_gate")
        qs_done, q_up, row_done, row_out, cum_done, gate_row, gate_out, new_done, pool_zero, dup_done, scl = (
            sem("a_" + n) for n in ("qs_done", "q_up", "lrow_done", "lrow_out", "cum_done", "gate_row",
                                    "gate_out", "new_done", "pool_zero", "qdup_done", "last"))
        with nc.Block() as block:
            @block.sync
            def _(sp):
                sp.dma_start(bf[:, :], k.b_fgate.rearrange("a h -> h a")).then_inc(b_in, 16)
                sp.dma_start(gsel[:, :], k.selectors[:, 0:12 * P]).then_inc(gsel_in, 16)
                rows = lambda a: a.rearrange("(t p) n -> p t n", p=P)
                outs = [(rows(k.o_cmp_p), k.row[:, :, M_CMP:M_CMP + 256]), (rows(k.o_slc_p), k.row[:, :, M_SLC:M_SLC + 256]),
                        (rows(k.o_win_p), k.row[:, :, M_WIN:M_WIN + 256]), (rows(k.o_fkv_p), k.row[:, :, M_FK:M_ALL]),
                        (rows(k.o_mem_p), k.mrow[:, :, :]),
                        (k.o_cmp_s, k.srow[:, M_CMP:M_CMP + 256]), (k.o_slc_s, k.srow[:, M_SLC:M_SLC + 256]),
                        (k.o_win_s[:, WIN - 1, :], k.srow[:, M_WIN:M_WIN + 256]), (k.o_fkv_s, k.srow[:, M_FK:M_ALL]),
                        (k.o_win_s[:, 0:WIN - 1, :], k.state_win[:, 1:WIN, :])]
                for dst, src in outs:
                    sp.dma_start(dst, src).then_inc(out_done, 16)
                sp.wait_ge(row_out, 2)
                sp.dma_start(rows(k.o_logf_p), lrow[:, :, :]).then_inc(out_done, 16)
                sp.dma_start(k.o_logf_s, k.slrow[:, :]).then_inc(out_done, 16)
                sp.wait_ge(out_done, 16 * (len(outs) + 2))

            @block.vector
            def _(ve):
                ve.wait_ge(b_in, 16)
                nc.vector.tensor_scalar(k.logf[:, :], k.logf[:, :], bf[:, 0:1], None, ALU.add).then_inc(va, 1)
                ve.wait_ge(va, 1)
                nc.vector.tensor_scalar(m8[:, :], k.logf[:, :], -1.0, None, ALU.mult).then_inc(va, 1)
                ve.wait_ge(va, 2)
                nc.vector.tensor_tensor(m8[:, :], m8[:, :], k.logf[:, :], ALU.min).then_inc(va, 1)
                ve.wait_ge(vb, 1)
                nc.vector.tensor_scalar_add(e8[:, :], e8[:, :], 1.0).then_inc(va, 1)
                ve.wait_ge(vb, 2)
                nc.vector.tensor_scalar(k.logf[:, :], k.logf[:, :], 0.0, None, ALU.min).then_inc(va, 1)
                ve.wait_ge(va, 5)
                nc.vector.tensor_tensor(k.logf[:, :], k.logf[:, :], e8[:, :], ALU.subtract).then_inc(va, 1)
                nc.vector.tensor_scalar(qs[:, :, :], k.fm[:, K_Q:K_Q + 8, T:TT], SCALE, None, ALU.mult).then_inc(qs_done, 1)
                nc.vector.tensor_scalar(k.mq[:, :, :], k.fm[:, K_MQ:K_MQ + 4, T:TT].rearrange("p c b -> p b c"), MSCALE, None, ALU.mult)
                ve.wait_ge(row_done, 1)
                nc.vector.tensor_copy(lrow[:, :, :], ps[0][:, 0:NT * H].rearrange("p (t h) -> p t h", t=NT)).then_inc(row_out, 1)
                nc.vector.tensor_copy(k.slrow[:, :], ps[1][0:NB, 0:H]).then_inc(row_out, 1)
                ve.wait_ge(cum_done, 1)
                nc.vector.tensor_scalar(k.ncum[:, :], ps[2][0:H, :], -1.0, None, ALU.mult)
                ve.wait_ge(vc, 1)
                nc.vector.tensor_scalar_add(gsig[:, :], gsig[:, :], 1.0).then_inc(gate_row, 1)
                ve.wait_ge(gate_row, 1)
                nc.vector.reciprocal(gsig[:, :], gsig[:, :]).then_inc(gate_row, 1)
                ve.wait_ge(gate_out, 1)
                nc.vector.tensor_copy(k.grow[:, :, :], ps[3][:, 0:NT * 24].rearrange("p (t h) -> p t h", t=NT))
                nc.vector.tensor_copy(k.sg[:, :, :], ps[4][:, 0:12 * NB].rearrange("p (c b) -> p c b", c=12))
                ve.wait_ge(dup_done, 1)
                ve.wait_ge(pool_zero, 1)
                for q in range(2):
                    src = ps[5][:, q * 32:(q + 1) * 32].rearrange("p (c b) -> p b c", c=4)
                    nc.vector.tensor_copy(k.qd[:, :, :].rearrange("p b (c q) -> p q b c", q=2)[:, q], src)
                    for g in range(2):
                        rows = slice(64 * g, 64 * g + 64)
                        nc.vector.tensor_copy(k.qg[rows, :, 4 * g:4 * g + 4].rearrange("p b (c q) -> p q b c", q=2)[:, q],
                                              src[rows, :, 2 * g:2 * g + 2])
                for c in range(4):
                    for q in range(2):
                        rows = slice(64 * q, 64 * q + 64)
                        nc.vector.tensor_copy(k.qz[rows, :, c, q], qs[rows, 4 + c, :])
                ve.wait_ge(new_done, 1)
                ve.wait_ge(pool_zero, 2)
                diag = k.diag[0:NB, :].unsqueeze(1).to_broadcast([NB, 4, NB])
                for br in range(3):
                    for j in range(2):
                        sc = ps[6 + j][0:NB, br * 32:(br + 1) * 32].rearrange("p (c b) -> p c b", c=4)
                        nc.vector.tensor_tensor(k.snew[0:NB, br, :, :].rearrange("p b (c j) -> p j c b", j=2)[:, j], sc, diag, ALU.add).then_inc(scl, 1)
                ve.wait_ge(scl, 6)
                ve.wait_ge(row_out, 2)
                nc.vector.tensor_tensor(k.snew[0:NB, 0, :, :], k.snew[0:NB, 0, :, :],
                                        k.slrow[:, :].unsqueeze(1).to_broadcast([NB, NB, H]), ALU.subtract)

            @block.scalar
            def _(sc):
                sc.wait_ge(va, 3)
                nc.scalar.activation(e8[:, :], m8[:, :], ACT.Exp).then_inc(vb, 1)
                nc.scalar.activation(gsig[:, :], k.gate[:, :], ACT.Exp, scale=-1.0).then_inc(vc, 1)
                sc.wait_ge(va, 4)
                nc.scalar.activation(e8[:, :], e8[:, :], ACT.Ln).then_inc(vb, 1)

            @block.gpsimd
            def _(pool):
                nc.gpsimd.memset(k.qz[:, :, :, :], 0.0)
                nc.gpsimd.memset(k.qg[:, :, :], 0.0).then_inc(pool_zero, 1)
                nc.gpsimd.memset(k.snew[:, :, :, :], NEG).then_inc(pool_zero, 1)
                nc.gpsimd.tensor_scalar(k.fm[:, K_Q:K_MQ, 0:T], k.fm[:, K_Q:K_MQ, 0:T], SCALE, None, ALU.mult)
                nc.gpsimd.tensor_scalar(k.fm[:, K_MQ:K_FK, 0:T], k.fm[:, K_MQ:K_FK, 0:T], MSCALE, None, ALU.mult)

            @block.tensor
            def _(te):
                te.wait_ge(va, 6)
                for t in range(NT):
                    nc.tensor.transpose(ps[0][:, t * H:(t + 1) * H], k.logf[:, t * P:(t + 1) * P], k.ident[0:H, 0:H])
                nc.tensor.transpose(ps[1][0:NB, 0:H], k.logf[:, T:TT], k.ident[0:H, 0:H]).then_inc(row_done, 1)
                te.wait_ge(row_out, 1)
                for t in range(NT):
                    last = nc.tensor.matmul(ps[2][0:H, t * P:T], lrow[:, t, :], k.cum[:, 0:T - t * P],
                                            start=t == 0, stop=t == NT - 1, skip_group_check=True)
                last.then_inc(cum_done, 1)
                te.wait_ge(gate_row, 2)
                te.wait_ge(gsel_in, 16)
                for t in range(NT):
                    nc.tensor.transpose(ps[3][:, t * 24:(t + 1) * 24], gsig[:, t * P:(t + 1) * P], k.ident[0:24, 0:24])
                for n in range(12):
                    last = nc.tensor.matmul(ps[4][:, n * NB:(n + 1) * NB], gsel[:, n * P:(n + 1) * P], gsig[:, T:TT], start=True, stop=True)
                last.then_inc(gate_out, 1)
                te.wait_ge(qs_done, 1)
                for q in range(2):
                    last = nc.tensor.matmul(ps[5][:, q * 32:(q + 1) * 32], k.dup[:, q * P:(q + 1) * P],
                                            qs[:, 0:4, :].rearrange("p c b -> p (c b)"), start=True, stop=True)
                last.then_inc(dup_done, 1)
                for br in range(3):
                    for h in range(H):
                        c, rows = h // 2, slice(64 * (h % 2), 64 * (h % 2) + 64)
                        place = K_FK + c if br == 0 else K_KD + 2 * (br - 1) + h // R
                        last = nc.tensor.matmul(ps[6 + h % 2][0:NB, (br * 4 + c) * NB:(br * 4 + c + 1) * NB], k.fm[rows, place, T:TT],
                                                qs[rows, (4 if br == 0 else 0) + c, :], start=True, stop=True)
                last.then_inc(new_done, 1)


def prompt_compressed(k):
    nc, ps = k.nc, k.ps
    with ExitStack() as cx:
        sb, sem = k.makers(cx)
        w1 = sb("b_w1", [P, CB, P])
        z = sb("b_z", [P, 2, 8])
        ez = sb("b_ez", [P, 2, 8])
        hid = sb("b_hid", [P, 2, 8])
        hv = sb("b_hv", [P, H, 2, NT])
        kp = sb("b_kp", [P, G, 2, NT])
        vbd = sb("b_vbd", [64, H, HD])
        s = sb("b_s", [P, NT, H, 8])
        m, den = sb("b_m", [P, NT, H]), sb("b_den", [P, NT, H])
        pt = w1[0:64, 0:NT, :]
        w_in, zeroed, hid_done, z_done, e_done, h_done, step, hv_done, kp_done, kp_out, v_done, vbd_done = (
            sem("b_" + n) for n in ("w_in", "zeroed", "hid_done", "z_done", "e_done", "h_done", "step", "hv_done",
                                    "kp_done", "kp_out", "v_done", "vbd_done"))
        q_done, s_done, x_step, exp_done, turned, pt_out, o_done, o_out = (
            sem("b_" + n) for n in ("q_done", "s_done", "x_step", "exp_done", "turned", "pt_out", "o_done", "o_out"))
        masked = sem("b_masked")
        hp = ps[0][:, 0:16].rearrange("p (v n) -> p v n", v=2)
        with nc.Block() as block:
            @block.sync
            def _(sp):
                sp.wait_ge(zeroed, 1)
                for v in range(2):
                    if v:
                        sp.wait_ge(hid_done, 1)
                    for half in range(2):
                        rows = slice(64 * half, 64 * half + 64)
                        sp.dma_start(w1[rows, :, rows], k.w_cmp1[0, v]).then_inc(w_in, 16)

            @block.gpsimd
            def _(pool):
                nc.gpsimd.memset(w1[0:64, :, 64:128], 0.0)
                nc.gpsimd.memset(w1[64:128, :, 0:64], 0.0).then_inc(zeroed, 1)
                pool.wait_ge(zeroed, 1)
                nc.gpsimd.memset(hv[:, :, :, :], 0.0).then_inc(zeroed, 1)

            @block.tensor
            def _(te):
                te.wait_ge(zeroed, 1)
                for v in range(2):
                    te.wait_ge(w_in, 32 * (v + 1))
                    rows = k.row[:, :, M_CMP + 128 * v:M_CMP + 128 * v + 128].rearrange("p t (g d) -> p d g t", g=2)
                    for d in range(HD):
                        last = nc.tensor.matmul(hp[:, v], w1[:, d, :], rows[:, d], start=d == 0, stop=d == HD - 1)
                    last.then_inc(hid_done, 1)
                te.wait_ge(h_done, 1)
                for half in range(2):
                    rows = slice(64 * half, 64 * half + 64)
                    last = nc.tensor.matmul(ps[1 + half][:, 0:8], k.w2d[rows, 0, :], hid[rows, 0, :], start=True, stop=True)
                last.then_inc(kp_done, 1)
                te.wait_ge(hv_done, 4)
                nc.tensor.matmul(ps[3][0:64, 0:HD], hv[:, :, :, :].rearrange("p h a t -> p (h a t)"), k.w2d[:, 1, 0:HD],
                                 start=True, stop=True).then_inc(v_done, 1)
                te.wait_ge(kp_out, 2)
                for t in range(NT):
                    for h in range(H):
                        c, rows = h // 2, slice(64 * (h % 2), 64 * (h % 2) + 64)
                        last = nc.tensor.matmul(ps[1 + h % 2][:, (t * 4 + c) * 8:(t * 4 + c + 1) * 8], k.fm[rows, K_Q + c, t * P:(t + 1) * P],
                                                kp[rows, h // R, :, :].rearrange("p a t -> p (a t)"), start=True, stop=True)
                last.then_inc(s_done, 1)
                te.wait_ge(x_step, 5)
                for t in range(NT):
                    last = nc.tensor.transpose(ps[5][0:64, t * P:(t + 1) * P], s[:, t, :, :].rearrange("p h n -> p (h n)"), k.ident)
                last.then_inc(turned, 1)
                te.wait_ge(pt_out, 1)
                te.wait_ge(vbd_done, 1)
                for t in range(NT):
                    if t >= 2:
                        te.wait_ge(o_out, t - 1)
                    nc.tensor.matmul(ps[6 + t % 2][:, :], pt[:, t, :], vbd[:, :, :].rearrange("p h d -> p (h d)"),
                                     start=True, stop=True).then_inc(o_done, 1)

            @block.scalar
            def _(sc):
                sc.wait_ge(z_done, 2)
                nc.scalar.activation(ez[:, :, :], z[:, :, :], ACT.Exp, scale=-1.0).then_inc(e_done, 1)
                sc.wait_ge(x_step, 2)
                nc.scalar.activation(s[:, :, :, :], s[:, :, :, :], ACT.Exp).then_inc(exp_done, 1)

            @block.vector
            def _(ve):
                ve.wait_ge(hid_done, 2)
                for v in range(2):
                    nc.vector.tensor_scalar(z[:, v], hp[:, v], k.pebias[:, v:v + 1], None, ALU.add).then_inc(z_done, 1)
                ve.wait_ge(e_done, 1)
                nc.vector.tensor_scalar_add(ez[:, :, :], ez[:, :, :], 1.0).then_inc(step, 1)
                ve.wait_ge(step, 1)
                nc.vector.reciprocal(ez[:, :, :], ez[:, :, :]).then_inc(step, 1)
                ve.wait_ge(step, 2)
                nc.vector.tensor_tensor(hid[:, :, :], z[:, :, :], ez[:, :, :], ALU.mult).then_inc(h_done, 1)
                ve.wait_ge(h_done, 1)
                ve.wait_ge(zeroed, 2)
                for half in range(2):
                    rows = slice(64 * half, 64 * half + 64)
                    for g in range(G):
                        src = hid[rows, 1, g * NT:(g + 1) * NT].unsqueeze(1).to_broadcast([64, R, NT])
                        nc.vector.tensor_copy(hv[rows, g * R:(g + 1) * R, half, :], src).then_inc(hv_done, 1)
                ve.wait_ge(kp_done, 1)
                for half in range(2):
                    nc.vector.tensor_copy(kp[:, :, half, :], ps[1 + half][:, 0:8].rearrange("p (g t) -> p g t", g=2)).then_inc(kp_out, 1)
                ve.wait_ge(v_done, 1)
                nc.vector.tensor_tensor(vbd[:, :, :], ps[3][0:64, 0:HD].unsqueeze(1).to_broadcast([64, H, HD]),
                                        k.headrow[0:64, :].unsqueeze(2).to_broadcast([64, H, HD]), ALU.mult).then_inc(vbd_done, 1)
                ve.wait_ge(s_done, 1)
                per = lambda a: a.rearrange("p (t n) -> p t n", t=NT).unsqueeze(2).to_broadcast([P, NT, H, 8])
                wide = lambda a: a[:, :, :].unsqueeze(3).to_broadcast([P, NT, H, 8])
                for j in range(2):
                    for t in range(NT):
                        nc.vector.tensor_tensor(s[:, t, :, :].rearrange("p (c j) n -> p j c n", j=2)[:, j],
                                                ps[1 + j][:, t * 32:(t + 1) * 32].rearrange("p (c n) -> p c n", c=4),
                                                k.cneg[:, t * 8:(t + 1) * 8].unsqueeze(1).to_broadcast([P, 4, 8]), ALU.add).then_inc(masked, 1)
                ve.wait_ge(masked, 2 * NT)
                nc.vector.tensor_reduce(m[:, :, :], s[:, :, :, :], AX, ALU.max).then_inc(x_step, 1)
                ve.wait_ge(x_step, 1)
                nc.vector.tensor_tensor(s[:, :, :, :], s[:, :, :, :], wide(m), ALU.subtract).then_inc(x_step, 1)
                ve.wait_ge(exp_done, 1)
                nc.vector.tensor_tensor(s[:, :, :, :], s[:, :, :, :], per(k.c01), ALU.mult).then_inc(x_step, 1)
                ve.wait_ge(x_step, 3)
                nc.vector.tensor_reduce(den[:, :, :], s[:, :, :, :], AX, ALU.add).then_inc(step, 1)
                ve.wait_ge(step, 3)
                nc.vector.tensor_scalar(den[:, :, :], den[:, :, :], TINY, None, ALU.max).then_inc(step, 1)
                ve.wait_ge(step, 4)
                nc.vector.reciprocal(den[:, :, :], den[:, :, :]).then_inc(x_step, 1)
                ve.wait_ge(x_step, 4)
                nc.vector.tensor_tensor(s[:, :, :, :], s[:, :, :, :], wide(den), ALU.mult).then_inc(x_step, 1)
                ve.wait_ge(turned, 1)
                nc.vector.tensor_copy(pt[:, :, :], ps[5][0:64, :].rearrange("p (t n) -> p t n", t=NT)).then_inc(pt_out, 1)
                for t in range(NT):
                    ve.wait_ge(o_done, t + 1)
                    gate = k.grow[:, t, 0:H].unsqueeze(2).to_broadcast([P, H, HD])
                    nc.vector.tensor_tensor(k.o[:, t, 0:BRW].rearrange("p (h d) -> p h d", h=H),
                                            ps[6 + t % 2][:, :].rearrange("p (h d) -> p h d", h=H), gate, ALU.mult).then_inc(o_out, 1)


def sample_compressed(k):
    nc, ps = k.nc, k.ps
    NG = NB * G
    with ExitStack() as cx:
        sb, sem = k.makers(cx)
        s = sb("s_s", [R, NG, NBLK])
        m, den = sb("s_m", [R, NG]), sb("s_den", [R, NG])
        pt = sb("s_pt", [64, NB, 2, R])
        flat = sb("s_flat", [1, NG * NBLK])
        imp, imp2 = sb("s_imp", [NG, NBLK]), sb("s_imp2", [NG, NBLK])
        mx = sb("s_mx", [NG, 16])
        ix = sb("s_ix", [NG, 16], U32)
        ixf = sb("s_ixf", [NG, 16])
        tab_i = sb("s_tab_i", [NG, PAGES], I32)
        tab_f = sb("s_tab_f", [NG, PAGES])
        tab = sb("s_tab", [NG, PAGES, 2])
        hot = sb("s_hot", [NG, 16, NBLK])
        first = sb("s_first", [NG, 16])
        firstT = sb("s_firstT", [16, NG])
        spread = sb("s_spread", [16, NG, 8])
        rowf = sb("s_rowf", [P, NG * 8])
        s_done, x, exp_done, imp_done, imp_out, imp_in, tab_in, t, first_turned, spread_done, rows_done, p_turned, pt_out, o_done, top = (
            sem("s_" + n) for n in ("s_done", "x", "exp_done", "imp_done", "imp_out", "imp_in", "tab_in", "t",
                                    "first_turned", "spread_done", "rows_done", "p_turned", "pt_out", "o_done", "top"))
        with nc.Block() as block:
            @block.sync
            def _(sp):
                for g in range(G):
                    for b in range(NB):
                        sp.dma_start(tab_i[b * G + g:b * G + g + 1, :], k.page_table[b:b + 1, :]).then_inc(tab_in, 16)
                sp.wait_ge(imp_out, 2)
                sp.dma_start(imp[:, :], flat[0:1, :].rearrange("o (n b) -> o n b", n=NG)).then_inc(imp_in, 16)

            @block.tensor
            def _(te):
                for b in range(NB):
                    for g in range(G):
                        n = b * G + g
                        for half in range(2):
                            rows = slice(64 * half, 64 * half + 64)
                            last = nc.tensor.matmul(ps[half][0:R, n * PAGES:(n + 1) * PAGES], k.qd[rows, b, g * R:(g + 1) * R],
                                                    k.kcb[rows, b, g * PAGES:(g + 1) * PAGES], start=True, stop=True)
                last.then_inc(s_done, 1)
                te.wait_ge(x, 7)
                for i in range(2):
                    nc.tensor.matmul(ps[2 + i][0:1, :], k.ones[0:R, 0:1], s[:, 8 * i:8 * i + 8, :].rearrange("p n b -> p (n b)"),
                                     start=True, stop=True).then_inc(imp_done, 1)
                for b in range(NB):
                    for half in range(2):
                        src = s[:, 2 * b:2 * b + 2, :].rearrange("p g (n a) -> p a (g n)", a=2)[:, half]
                        last = nc.tensor.transpose(ps[4][0:64, (b * 2 + half) * R:(b * 2 + half + 1) * R], src, k.ident[0:R, 0:R])
                last.then_inc(p_turned, 1)
                te.wait_ge(pt_out, 1)
                for b in range(NB):
                    for g in range(G):
                        rows = slice(32 * g, 32 * g + 32)
                        for half in range(2):
                            last = nc.tensor.matmul(ps[5 + g][0:64, b * R:(b + 1) * R], k.vcb[rows, b, 64 * half:64 * half + 64],
                                                    pt[rows, b, half, :], start=half == 0, stop=half == 1, skip_group_check=True)
                last.then_inc(o_done, 1)
                te.wait_ge(t, 4)
                nc.tensor.transpose(ps[2][0:16, 0:NG], first[:, :], k.ident[0:NG, 0:NG]).then_inc(first_turned, 1)
                te.wait_ge(spread_done, 1)
                nc.tensor.matmul(ps[3][:, 0:NG * 8], k.epart[0:16, :], spread[:, :, :].rearrange("p n j -> p (n j)"),
                                 start=True, stop=True).then_inc(rows_done, 1)

            @block.scalar
            def _(sc):
                sc.wait_ge(x, 4)
                nc.scalar.activation(s[:, :, :], s[:, :, :], ACT.Exp).then_inc(exp_done, 1)

            @block.gpsimd
            def _(pool):
                pass

            @block.vector
            def _(ve):
                wide = lambda a: a[:, :].unsqueeze(2).to_broadcast([R, NG, NBLK])
                ve.wait_ge(s_done, 1)
                for half in range(2):
                    nc.vector.tensor_copy(s[:, :, :].rearrange("p n (b a) -> p a n b", a=2)[:, half],
                                          ps[half][0:R, :].rearrange("p (n b) -> p n b", n=NG)).then_inc(x, 1)
                ve.wait_ge(x, 2)
                nc.vector.tensor_reduce(m[:, :], s[:, :, :], AX, ALU.max).then_inc(x, 1)
                ve.wait_ge(x, 3)
                nc.vector.tensor_tensor(s[:, :, :], s[:, :, :], wide(m), ALU.subtract).then_inc(x, 1)
                ve.wait_ge(exp_done, 1)
                nc.vector.tensor_reduce(den[:, :], s[:, :, :], AX, ALU.add).then_inc(x, 1)
                ve.wait_ge(x, 5)
                nc.vector.reciprocal(den[:, :], den[:, :]).then_inc(x, 1)
                ve.wait_ge(x, 6)
                nc.vector.tensor_tensor(s[:, :, :], s[:, :, :], wide(den), ALU.mult).then_inc(x, 1)
                ve.wait_ge(imp_done, 2)
                for i in range(2):
                    nc.vector.tensor_copy(flat[0:1, 512 * i:512 * i + 512], ps[2 + i][0:1, :]).then_inc(imp_out, 1)
                ve.wait_ge(tab_in, 16 * NG)
                nc.vector.tensor_copy(tab_f[:, :], tab_i[:, :]).then_inc(t, 1)
                ve.wait_ge(t, 1)
                nc.vector.tensor_scalar(tab_f[:, :], tab_f[:, :], float(P), None, ALU.mult).then_inc(t, 1)
                ve.wait_ge(t, 2)
                nc.vector.tensor_tensor(tab[:, :, :], tab_f[:, :].unsqueeze(2).to_broadcast([NG, PAGES, 2]),
                                        k.blkrow[0:NG, :].rearrange("p (n a) -> p n a", a=2), ALU.add).then_inc(t, 1)
                ve.wait_ge(p_turned, 1)
                nc.vector.tensor_copy(pt[:, :, :, :], ps[4][0:64, 0:NB * 2 * R].rearrange("p (b a r) -> p b a r", b=NB, a=2)).then_inc(pt_out, 1)
                ve.wait_ge(imp_in, 16)
                nc.vector.max(out=mx[:, 0:8], in_=imp[:, :]).then_inc(top, 1)
                ve.wait_ge(top, 1)
                nc.vector.max_index(out=ix[:, 0:8], in_max=mx[:, 0:8], in_values=imp[:, :]).then_inc(top, 1)
                nc.vector.match_replace(out=imp2[:, :], in_to_replace=mx[:, 0:8], in_values=imp[:, :], imm_value=NEG).then_inc(top, 1)
                ve.wait_ge(top, 3)
                nc.vector.max(out=mx[:, 8:16], in_=imp2[:, :]).then_inc(top, 1)
                ve.wait_ge(top, 4)
                nc.vector.max_index(out=ix[:, 8:16], in_max=mx[:, 8:16], in_values=imp2[:, :]).then_inc(top, 1)
                ve.wait_ge(top, 5)
                nc.vector.tensor_copy(ixf[:, :], ix[:, :]).then_inc(top, 1)
                ve.wait_ge(top, 6)
                nc.vector.tensor_tensor(hot[:, :, :], ixf[:, :].unsqueeze(2).to_broadcast([NG, 16, NBLK]),
                                        k.blk[0:NG, :].unsqueeze(1).to_broadcast([NG, 16, NBLK]), ALU.is_equal).then_inc(top, 1)
                ve.wait_ge(top, 7)
                ve.wait_ge(t, 3)
                nc.vector.tensor_tensor(hot[:, :, :], hot[:, :, :],
                                        tab[:, :, :].rearrange("p n a -> p (n a)").unsqueeze(1).to_broadcast([NG, 16, NBLK]), ALU.mult).then_inc(top, 1)
                ve.wait_ge(top, 8)
                nc.vector.tensor_reduce(first[:, :], hot[:, :, :], AX, ALU.add).then_inc(t, 1)
                ve.wait_ge(first_turned, 1)
                nc.vector.tensor_copy(firstT[:, :], ps[2][0:16, 0:NG]).then_inc(top, 1)
                ve.wait_ge(top, 9)
                nc.vector.tensor_tensor(spread[:, :, :], firstT[:, :].unsqueeze(2).to_broadcast([16, NG, 8]),
                                        k.jmask[0:16, :].unsqueeze(1).to_broadcast([16, NG, 8]), ALU.mult).then_inc(spread_done, 1)
                ve.wait_ge(rows_done, 1)
                nc.vector.tensor_scalar(rowf[:, :], ps[3][:, 0:NG * 8], k.lcol, None, ALU.add).then_inc(top, 1)
                ve.wait_ge(top, 10)
                nc.vector.tensor_copy(k.selrow[:, :], rowf[:, :])
                ve.wait_ge(o_done, 1)
                for g in range(G):
                    nc.vector.tensor_copy(k.oc[:, :, g * R:(g + 1) * R], ps[5 + g][0:64, 0:NB * R].rearrange("p (b r) -> p b r", b=NB))


def attention(k, name, pairs, units, keys, vwide, loops, addresses, mask, forget_sums, place):
    nc, ps, wait = k.nc, k.ps, k.wait
    U = len(units)
    with ExitStack() as cx:
        sb, sem = k.makers(cx)
        q, kk = sb(name + "_q", [P, T]), sb(name + "_k", [P, T])
        hs = sb(name + "_hs", [H, 2, P])
        hsel = sb(name + "_hsel", [H, H, P])
        e = [sb(f"{name}_e{i}", [P, T]) for i in range(2)]
        pt = [sb(f"{name}_pt{i}", [P, T]) for i in range(2)]
        nm, su, rc = sb(name + "_nm", [P, U]), sb(name + "_su", [P, U]), sb(name + "_rc", [P, U])
        staged, s_done, m_done, e_done, turned, pt_out, o_done, rc_done, o_out, gr_done = (
            sem(name + "_" + n) for n in ("staged", "s_done", "m_done", "e_done", "turned", "pt_out", "o_done", "rc_done", "o_out", "gr_done"))
        kw = keys(NT - 1)
        STAGES = 3 if forget_sums else 2

        def every(engine, body):
            def nest(idx, n, rest):
                if not rest:
                    body(n, idx)
                    return
                with engine.Fori(0, rest[0]) as i:
                    nest(idx + [i], n * rest[0] + i if idx else i, rest[1:])
            nest([], 0, list(loops))

        hsel_in = sem(name + "_hsel_in")
        k.prime(s_done, e_done, turned, pt_out, o_done, o_out)
        with nc.Block() as block:
            @block.sync
            def _(sp):
                if forget_sums:
                    sp.dma_start(hsel[:, :, :], k.selectors[0:H, 12 * P:].rearrange("k (h n) -> k h n", h=H)).then_inc(hsel_in, 16)

            @block.gpsimd
            def _(pool):
                def body(it, idx):
                    qc, kc, _, _ = addresses(idx)
                    wait(pool, s_done, it * U)
                    nc.gpsimd.tensor_copy(q[:, :].unsqueeze(1), k.fm[:, bass.ds(qc, 1), 0:T]).then_inc(staged, 1)
                    src = k.fm if kc[0] == "fm" else k.mkT
                    nc.gpsimd.tensor_copy(kk[:, 0:kw].unsqueeze(1), src[:, bass.ds(kc[1], 1), 0:kw]).then_inc(staged, 1)
                    if forget_sums:
                        nc.gpsimd.tensor_copy(hs[:, :, :], hsel[:, bass.ds(idx[-1] * 2, 2), :]).then_inc(staged, 1)
                if forget_sums:
                    wait(pool, hsel_in, 16)
                every(pool, body)

            @block.tensor
            def _(te):
                def body(it, idx):
                    _, _, vc, vstep = addresses(idx)

                    def scores(u):
                        rows, t = units[u]
                        n = keys(t)
                        wait(te, e_done, it * U + u - 1) if u else wait(te, e_done, it * U)
                        parts = [(q[rows, t * P:(t + 1) * P], kk[rows, 0:n], slice(0, n))]
                        if forget_sums:
                            parts.append((hs[:, rows.start // 64, :], k.ncum[:, 0:n], slice(0, n)))
                        if mask:
                            parts.append((k.ident, k.causal, slice(t * P, n)))
                        for i, (left, right, cols) in enumerate(parts):
                            last = nc.tensor.matmul(ps[u % 2][:, cols], left, right, start=i == 0, stop=i == len(parts) - 1,
                                                    skip_group_check=True)
                        last.then_inc(s_done, 1)

                    def values(u):
                        rows, t = units[u]
                        n = keys(t)
                        wait(te, e_done, it * U + u + 1)
                        wait(te, pt_out, it * U + u - 1) if u else wait(te, pt_out, it * U)
                        for j in range(n // P):
                            last = nc.tensor.transpose(ps[2 + u % 2][:, j * P:(j + 1) * P], e[u % 2][:, j * P:(j + 1) * P], k.ident)
                        last.then_inc(turned, 1)

                    def sums(u):
                        rows, t = units[u]
                        n = keys(t)
                        wait(te, pt_out, it * U + u + 1)
                        wait(te, o_out, it * U + u - 1) if u else wait(te, o_out, it * U)
                        src = k.mrow if kc_mem else k.row
                        for j in range(n // P):
                            last = nc.tensor.matmul(ps[4 + u % 2][:, 0:vwide], pt[u % 2][:, j * P:(j + 1) * P],
                                                    src[:, j, bass.ds(vc + vstep * (rows.start // 64), vwide)],
                                                    start=j == 0, stop=j == n // P - 1)
                        last.then_inc(o_done, 1)

                    kc_mem = addresses(idx)[1][0] != "fm"
                    wait(te, staged, it * STAGES + STAGES)
                    scores(0)
                    for u in range(U):
                        if u + 1 < U:
                            scores(u + 1)
                        values(u)
                        if u:
                            sums(u - 1)
                    sums(U - 1)
                every(te, body)

            @block.vector
            def _(ve):
                def body(it, idx):
                    def finish(u):
                        rows, t = units[u]
                        wait(ve, o_done, it * U + u + 1)
                        col, gate, add = place(idx, rows.start // 64)
                        dst = k.o[:, t, bass.ds(col, vwide)]
                        src = ps[4 + u % 2][:, 0:vwide]
                        nc.vector.reciprocal(rc[:, u:u + 1], su[:, u:u + 1]).then_inc(rc_done, 1)
                        wait(ve, rc_done, it * U + u + 1)
                        if gate is not None:
                            nc.vector.tensor_tensor(rc[:, u:u + 1], rc[:, u:u + 1], k.grow[:, t, bass.ds(gate, 1)], ALU.mult).then_inc(gr_done, 1)
                            wait(ve, gr_done, it * U + u + 1)
                        if add:
                            nc.vector.scalar_tensor_tensor(out=dst, in0=src, scalar=rc[:, u:u + 1], in1=dst, op0=ALU.mult, op1=ALU.add).then_inc(o_out, 1)
                        else:
                            nc.vector.tensor_scalar(dst, src, rc[:, u:u + 1], None, ALU.mult).then_inc(o_out, 1)

                    def maximum(u):
                        rows, t = units[u]
                        wait(ve, s_done, it * U + u + 1)
                        nc.vector.tensor_reduce(nm[:, u:u + 1], ps[u % 2][:, 0:keys(t)], AX, ALU.max, negate=True).then_inc(m_done, 1)

                    maximum(0)
                    for u in range(U):
                        if u + 1 < U:
                            maximum(u + 1)
                        rows, t = units[u]
                        wait(ve, turned, it * U + u + 1)
                        wait(ve, o_done, it * U + u - 1) if u else wait(ve, o_done, it * U)
                        nc.vector.tensor_copy(pt[u % 2][:, 0:keys(t)], ps[2 + u % 2][:, 0:keys(t)]).then_inc(pt_out, 1)
                        if u:
                            finish(u - 1)
                    finish(U - 1)
                every(ve, body)

            @block.scalar
            def _(sc):
                def body(it, idx):
                    for u, (rows, t) in enumerate(units):
                        wait(sc, m_done, it * U + u + 1)
                        wait(sc, turned, it * U + u - 1) if u else wait(sc, turned, it * U)
                        nc.scalar.activation(e[u % 2][:, 0:keys(t)], ps[u % 2][:, 0:keys(t)], ACT.Exp, bias=nm[:, u:u + 1],
                                             accum_out=su[:, u:u + 1]).then_inc(e_done, 1)
                every(sc, body)


def prompt(k):
    two = [(slice(64 * j, 64 * j + 64), t) for t in range(NT) for j in range(2)]
    one = [(slice(0, P), t) for t in range(NT)]
    causal = lambda t: (t + 1) * P
    attention(k, "f", None, two, causal, HD, [4],
              lambda i: (K_FQ + i[0], ("fm", K_FK + i[0]), M_FV + i[0] * P, HD), True, True,
              lambda i, j: (BRW + i[0] * P + j * HD, None, False))
    attention(k, "m", None, one, lambda t: NM, P, [4],
              lambda i: (K_MQ + i[0], ("mem", i[0]), BRW + i[0] * P, 0), False, False,
              lambda i, j: (2 * BRW + i[0] * P, None, False))
    attention(k, "w", None, two, causal, HD, [2, G, 2],
              lambda i: (K_Q + i[1] * 2 + i[2], ("fm", K_KD + i[0] * 2 + i[1]), M_SLC + P + i[0] * 256 + i[1] * HD, 0),
              True, False,
              lambda i, j: (i[1] * 256 + i[2] * P + j * HD, (i[0] + 1) * 8 + i[1] * 4 + i[2] * 2 + j, True))


def sample(k):
    nc, ps, wait = k.nc, k.ps, k.wait
    KR = 4
    SLOTS = 2 * KR
    ROUNDS = PAGES // SLOTS
    NSLC, NWIN, NMEM = 16, WIN // P, NM // P
    FT, ST, WT = PAGES + 1, NSLC // 2 + 1, NWIN + 1
    small = [("slc", n) for n in range(4)] + [("win", 0)] + [("mem", n) for n in range(NMEM)]
    TURNS = PAGES + len(small)
    NS = H + H + H + MH
    with ExitStack() as cx:
        sb, sem = k.makers(cx)
        kpage = sb("d_kpage", [P, SLOTS, BRW])
        vpage = sb("d_vpage", [P, SLOTS, BRW])
        slc = sb("d_slc", [P, NSLC, 256])
        win = sb("d_win", [P, NWIN, 256])
        mem = sb("d_mem", [P, NMEM, 2 * BRW])
        kT = [sb(f"d_kT{i}", [P, 4 * P]) for i in range(2)]
        sf = sb("d_sf", [P, FT, H])
        pf = sb("d_pf", [P, FT, H])
        ss = sb("d_ss", [P, ST + WT, H])
        sm = sb("d_sm", [P, NMEM, MH])
        mx, den, rden = sb("d_mx", [P, NS]), sb("d_den", [P, NS]), sb("d_rden", [P, NS])
        col, dia = sb("d_col", [NS, 1]), sb("d_dia", [NS, NS])

        k_in = [sem(f"d_k_in{i}") for i in range(SLOTS)]
        v_in = [sem(f"d_v_in{i}") for i in range(SLOTS)]
        k_free, v_free, sc_out = ([sem(f"d_{n}{i}") for i in range(2)] for n in ("k_free", "v_free", "sc_out"))
        slc_in = k.slc_in
        win_in, mem_in, small_free = (sem("d_" + n) for n in ("win_in", "mem_in", "small_free"))
        turned, kT_out, used, small_out = (sem("d_" + n) for n in ("turned", "kT_out", "used", "small_out"))
        mx_done, mx_turned, col_done, dia_done, mx_spread, shifted, exp_done = (
            sem("d_" + n) for n in ("mx_done", "mx_turned", "col_done", "dia_done", "mx_spread", "shifted", "exp_done"))
        den_done, den_spread, rden_done, p_done, pf_done, of_out, os_out, zero = (
            sem("d_" + n) for n in ("den_done", "den_spread", "rden_done", "p_done", "pf_done", "of_out", "os_out", "zero"))
        late_masked, new_in = sem("d_late_masked"), sem("d_new_in")
        turn_bank, small_bank, page_bank, stat_bank, sv_bank, fv_bank = ps[0:2], ps[2], ps[3:5], ps[5], ps[6], ps[7]

        k.prime(*k_free, *v_free, *sc_out, small_free, kT_out, used, small_out, of_out, os_out, pf_done)
        with nc.Block() as block:
            @block.sync
            def _(sp):
                def pages(b, which):
                    buf, arrive = ((kpage, k_in), (vpage, v_in))[which]
                    with sp.Fori(0, ROUNDS) as st:
                        for half in range(2):
                            wait(sp, (k_free, v_free)[which][half], b * ROUNDS + st)
                            for slot in range(half * KR, half * KR + KR):
                                pg = sp.value_load(k.table[0:1, bass.ds(b * PAGES + st * SLOTS + slot, 1)], min_val=0, max_val=POOL - 1)
                                sp.dma_start(buf[:, slot, :].unsqueeze(1),
                                             k.cache_fox[bass.ds(pg, 1), :, which, :].rearrange("a p n -> p a n")).then_inc(arrive[slot], 16)

                def others(b):
                    wait(sp, small_free, b)
                    for t in range(NWIN):
                        sp.dma_start(win[:, t, :].unsqueeze(1), k.state_win[bass.ds(b, 1), t * P:(t + 1) * P, :].rearrange("a p n -> p a n")).then_inc(win_in, 16)
                    for t in range(NMEM):
                        sp.dma_start(mem[:, t, :].unsqueeze(1), k.cache_mem[bass.ds(b, 1), t * P:(t + 1) * P, :].rearrange("a p n -> p a n")).then_inc(mem_in, 16)

                pages(0, 0)
                others(0)
                with sp.Fori(1, NB) as b:
                    pages(b, 0)
                    others(b)
                    pages(b - 1, 1)
                pages(NB - 1, 1)

            @block.gpsimd
            def _(pool):
                nc.gpsimd.memset(k.ow[:, :, :, :], 0.0).then_inc(zero, 1)
                for b in range(NB):
                    if b:
                        wait(pool, small_free, b)
                    for n in range(NSLC):
                        at = b * NSLC + n
                        nc.gpsimd.indirect_dma_start(
                            out=slc[:, n, :], out_offset=None, in_=k.cache_slc,
                            in_offset=bass.IndirectOffsetOnAxis(ap=k.selrow[:, at:at + 1].bitcast(U32), axis=0),
                            bounds_check=POOL * P - 1, oob_is_err=False).then_inc(slc_in, 16)

            @block.tensor
            def _(te):
                def page_keys(b):
                    def score(st, slot):
                        half, i = slot // KR, slot % KR
                        wait(te, kT_out, b * TURNS + st * SLOTS + slot + 1)
                        if i == 0:
                            wait(te, sc_out[half], b * ROUNDS + st)
                        for c in range(4):
                            last = nc.tensor.matmul(page_bank[half][:, i * H + 2 * c:i * H + 2 * c + 2], kT[slot % 2][:, c * P:(c + 1) * P],
                                                    k.qz[:, bass.ds(b, 1), c, :].rearrange("p a n -> p (a n)"), start=True, stop=True)
                            if c == 0 and i == KR - 1:
                                last.then_inc(k_free[half], 1)
                        last.then_inc(used, 1)

                    with te.Fori(0, ROUNDS) as st:
                        for slot in range(SLOTS):
                            wait(te, k_in[slot], (b * ROUNDS + st) * 16 + 16)
                            wait(te, kT_out, b * TURNS + st * SLOTS + max(slot - 1, 0))
                            for c in range(4):
                                last = nc.tensor.transpose(turn_bank[slot % 2][:, c * P:(c + 1) * P], kpage[:, slot, c * P:(c + 1) * P], k.ident)
                            last.then_inc(turned, 1)
                            if slot:
                                score(st, slot - 1)
                        score(st, SLOTS - 1)

                def small_keys(b):
                    wait(te, slc_in, b * (16 * NSLC) + 16 * NSLC)
                    wait(te, win_in, b * (16 * NWIN) + 16 * NWIN)
                    wait(te, mem_in, b * (16 * NMEM) + 16 * NMEM)
                    wait(te, small_out, b * 3)

                    def turn(no):
                        kind, n = small[no]
                        wait(te, kT_out, b * TURNS + PAGES + max(no - 1, 0))
                        for i in range(4):
                            src = {"slc": slc[:, (4 * n + i) % NSLC, 0:P], "win": win[:, i, 0:P], "mem": mem[:, n % NMEM, i * P:(i + 1) * P]}[kind]
                            last = nc.tensor.transpose(turn_bank[no % 2][:, i * P:(i + 1) * P], src, k.ident)
                        last.then_inc(turned, 1)

                    def score(no):
                        kind, n = small[no]
                        wait(te, kT_out, b * TURNS + PAGES + no + 1)
                        for i in range(4):
                            if kind == "slc":
                                tile = 4 * n + i
                                out, right = small_bank[:, tile * R:(tile + 1) * R], k.qg[:, bass.ds(b, 1), (tile // 8) * R:(tile // 8 + 1) * R]
                            elif kind == "win":
                                out, right = small_bank[:, 64 + i * H:64 + (i + 1) * H], k.qg[:, bass.ds(b, 1), :]
                            else:
                                out, right = small_bank[:, 96 + n * MH + i:97 + n * MH + i], k.mq[:, bass.ds(b, 1), i:i + 1]
                            last = nc.tensor.matmul(out, kT[no % 2][:, i * P:(i + 1) * P], right.rearrange("p a n -> p (a n)"), start=True, stop=True)
                        last.then_inc(used, 1)

                    turn(0)
                    for no in range(len(small)):
                        if no + 1 < len(small):
                            turn(no + 1)
                        score(no)

                def softmax_step(b, i):
                    if i == 0:
                        wait(te, mx_done, b * 4 + 4)
                        nc.tensor.transpose(stat_bank[0:NS, 0:P], mx[:, :], k.ident).then_inc(mx_turned, 1)
                    elif i == 1:
                        wait(te, dia_done, b + 1)
                        nc.tensor.matmul(stat_bank[:, P:P + NS], k.ones[0:NS, :], dia[:, :], start=True, stop=True).then_inc(mx_spread, 1)
                    else:
                        wait(te, den_done, b * 4 + 4)
                        nc.tensor.matmul(stat_bank[:, 2 * P:2 * P + NS], k.ones, den[:, :], start=True, stop=True).then_inc(den_spread, 1)

                def page_values(b, st):
                    if st == 0:
                        wait(te, pf_done, b + 1)
                        wait(te, of_out, b * 2)
                        for c in range(4):
                            nc.tensor.matmul(fv_bank[:, 2 * c:2 * c + 2], k.srow[:, M_FV + c * P:M_FV + (c + 1) * P],
                                             pf[0:NB, FT - 1, 2 * c:2 * c + 2], start=c == 0, stop=False, skip_group_check=True)
                    for slot in range(SLOTS):
                        wait(te, v_in[slot], (b * ROUNDS + st) * 16 + 16)
                        for c in range(4):
                            last = nc.tensor.matmul(fv_bank[:, 2 * c:2 * c + 2], vpage[:, slot, c * P:(c + 1) * P],
                                                    pf[:, st * SLOTS + slot, 2 * c:2 * c + 2], start=False,
                                                    stop=st == ROUNDS - 1 and slot == SLOTS - 1, skip_group_check=True)
                        if slot % KR == KR - 1:
                            last.then_inc(v_free[slot // KR], 1)

                def small_values(b):
                    wait(te, p_done, b * 3 + 3)
                    wait(te, os_out, b * 3)
                    parts = []
                    for n in range(NSLC):
                        g = n // 8
                        parts.append((slice(g * R, (g + 1) * R), slc[:, n, P:2 * P], ss[:, n % 8, g * R:(g + 1) * R]))
                    parts.append((slice(0, H), k.srow[:, M_SLC + P:M_SLC + 2 * P], ss[0:NB, ST - 1, :]))
                    for n in range(NWIN):
                        parts.append((slice(H, 2 * H), win[:, n, P:2 * P], ss[:, ST + n, :]))
                    parts.append((slice(H, 2 * H), k.srow[:, M_WIN + P:M_WIN + 2 * P], ss[0:NB, ST + WT - 1, :]))
                    for n in range(NMEM):
                        for c in range(MH):
                            parts.append((slice(2 * H + c, 2 * H + c + 1), mem[:, n, BRW + c * P:BRW + (c + 1) * P], sm[:, n, c:c + 1]))
                    for i, (cols, left, right) in enumerate(parts):
                        last = nc.tensor.matmul(sv_bank[:, cols], left, right, start=i == 0, stop=i == len(parts) - 1, skip_group_check=True)
                    last.then_inc(small_free, 1)

                def keys(b):
                    page_keys(b)
                    small_keys(b)

                keys(0)
                for i in range(3):
                    softmax_step(0, i)
                small_values(0)
                with te.Fori(1, NB) as b:
                    keys(b)
                    for st in range(ROUNDS):
                        page_values(b - 1, st)
                        if st < 3:
                            softmax_step(b, st)
                    small_values(b)
                for st in range(ROUNDS):
                    page_values(NB - 1, st)

            @block.scalar
            def _(sc):
                with sc.Fori(0, NB) as b:
                    def copy(base, no):
                        wait(sc, turned, base + no + 1)
                        wait(sc, used, base + max(no - 1, 0))
                        nc.scalar.activation(kT[no % 2][:, :], turn_bank[no % 2][:, :], ACT.Copy).then_inc(kT_out, 1)

                    with sc.Fori(0, ROUNDS) as st:
                        for slot in range(SLOTS):
                            copy(b * TURNS + st * SLOTS, slot)
                    for no in range(len(small)):
                        copy(b * TURNS + PAGES, no)
                    for i, s in enumerate((ss, sm, sf)):
                        wait(sc, shifted, b * 4 + (2, 3, 4)[i])
                        nc.scalar.activation(s[:, :, :], s[:, :, :], ACT.Exp).then_inc(exp_done, 1)

            @block.vector
            def _(ve):
                kinds = [(ss, slice(0, ST), H, H), (ss, slice(ST, ST + WT), H, 2 * H), (sm, slice(0, NMEM), MH, 3 * H),
                         (sf, slice(0, FT), H, 0)]

                def spread(cols, tiles, heads, at):
                    return cols[:, at:at + heads].unsqueeze(1).to_broadcast([P, tiles.stop - tiles.start, heads])

                def scores(b):
                    wait(ve, pf_done, b)
                    wait(ve, small_free, b)
                    nc.vector.tensor_copy(sf[:, FT - 1, :].unsqueeze(1), k.snew[:, 0, bass.ds(b, 1), :]).then_inc(new_in, 1)
                    nc.vector.tensor_copy(ss[:, ST - 1, :].unsqueeze(1), k.snew[:, 1, bass.ds(b, 1), :]).then_inc(new_in, 1)
                    nc.vector.tensor_copy(ss[:, ST + WT - 1, :].unsqueeze(1), k.snew[:, 2, bass.ds(b, 1), :]).then_inc(new_in, 1)
                    with ve.Fori(0, ROUNDS) as st:
                        for half in range(2):
                            wait(ve, used, b * TURNS + st * SLOTS + (half + 1) * KR)
                            at = st * SLOTS + half * KR
                            nc.vector.tensor_tensor(sf[:, bass.ds(at, KR), :], page_bank[half][:, 0:KR * H].rearrange("p (n h) -> p n h", h=H),
                                                    k.rpast[:, bass.ds(b * PAGES + at, KR), :], ALU.add).then_inc(sc_out[half], 1)
                    wait(ve, used, b * TURNS + TURNS)
                    nc.vector.tensor_copy(ss[:, 0:8, :].rearrange("p j (g r) -> p g j r", g=G),
                                          small_bank[:, 0:64].rearrange("p (g j r) -> p g j r", g=G, r=R)).then_inc(small_out, 1)
                    nc.vector.tensor_copy(ss[:, ST:ST + NWIN, :], small_bank[:, 64:96].rearrange("p (n h) -> p n h", h=H)).then_inc(small_out, 1)
                    nc.vector.tensor_copy(sm[:, :, :], small_bank[:, 96:96 + NMEM * MH].rearrange("p (n h) -> p n h", h=MH)).then_inc(small_out, 1)
                    wait(ve, small_out, b * 3 + 3)
                    nc.vector.tensor_scalar(ss[:, 7, :], ss[:, 7, :], k.newneg, None, ALU.add).then_inc(late_masked, 1)
                    wait(ve, late_masked, b + 1)

                def softmax(b):
                    wait(ve, new_in, b * 3 + 3)
                    for half in range(2):
                        wait(ve, sc_out[half], b * ROUNDS + ROUNDS)
                    for s, tiles, heads, at in kinds:
                        nc.vector.tensor_reduce(mx[:, at:at + heads], s[:, tiles, :].rearrange("p n h -> p h n"), AX, ALU.max).then_inc(mx_done, 1)
                    wait(ve, mx_turned, b + 1)
                    nc.vector.tensor_reduce(col[:, :], stat_bank[0:NS, 0:P], AX, ALU.max).then_inc(col_done, 1)
                    wait(ve, col_done, b + 1)
                    nc.vector.tensor_scalar(dia[:, :], k.ident[0:NS, 0:NS], col[:, 0:1], None, ALU.mult).then_inc(dia_done, 1)
                    wait(ve, mx_spread, b + 1)
                    for s, tiles, heads, at in kinds:
                        nc.vector.tensor_tensor(s[:, tiles, :], s[:, tiles, :], spread(stat_bank[:, P:P + NS], tiles, heads, at), ALU.subtract).then_inc(shifted, 1)
                    wait(ve, exp_done, b * 3 + 3)
                    for s, tiles, heads, at in kinds:
                        nc.vector.tensor_reduce(den[:, at:at + heads], s[:, tiles, :].rearrange("p n h -> p h n"), AX, ALU.add).then_inc(den_done, 1)
                    wait(ve, den_spread, b + 1)
                    nc.vector.reciprocal(rden[:, :], stat_bank[:, 2 * P:2 * P + NS]).then_inc(rden_done, 1)
                    wait(ve, rden_done, b + 1)
                    for s, tiles, heads, at in kinds[:3]:
                        nc.vector.tensor_tensor(s[:, tiles, :], s[:, tiles, :], spread(rden, tiles, heads, at), ALU.mult).then_inc(p_done, 1)

                def page_sums(b):
                    wait(ve, v_free[1], b * ROUNDS + ROUNDS)
                    for j in range(2):
                        rows = slice(64 * j, 64 * j + 64)
                        nc.vector.tensor_copy(k.of[rows, :, bass.ds(b, 1)],
                                              fv_bank[rows, 0:8].rearrange("p (c j) -> p c j", j=2)[:, :, j:j + 1]).then_inc(of_out, 1)

                def probabilities(b):
                    s, tiles, heads, at = kinds[3]
                    nc.vector.tensor_tensor(pf[:, :, :], sf[:, :, :], spread(rden, tiles, heads, at), ALU.mult).then_inc(pf_done, 1)

                def small_sums(b):
                    wait(ve, small_free, b + 1)
                    for g in range(G):
                        rows = slice(64 * g, 64 * g + 64)
                        nc.vector.tensor_copy(k.ow[rows, :, bass.ds(b, 1), g * R:(g + 1) * R],
                                              sv_bank[rows, 0:2 * H].rearrange("p (i a h) -> p i a h", i=2, a=1)[:, :, :, g * R:(g + 1) * R]).then_inc(os_out, 1)
                    nc.vector.tensor_copy(k.om[:, :, bass.ds(b, 1)], sv_bank[:, 2 * H:2 * H + MH].unsqueeze(2)).then_inc(os_out, 1)

                wait(ve, zero, 1)
                scores(0)
                softmax(0)
                probabilities(0)
                small_sums(0)
                with ve.Fori(1, NB) as b:
                    scores(b)
                    softmax(b)
                    page_sums(b - 1)
                    probabilities(b)
                    small_sums(b)
                page_sums(NB - 1)


def merge(k):
    nc, ps, wait = k.nc, k.ps, k.wait
    halves = lambda a: a.rearrange("p (i n) -> p i n", i=2)
    banks = lambda i: [ps[2 * i], ps[2 * i + 1]]
    with ExitStack() as cx:
        sb, sem = k.makers(cx)
        br = sb("e_br", [P, 12, TT])
        mt = sb("e_mt", [P, DC, TT])
        wout = sb("e_wout", [P, DC, D])
        x = sb("e_x", [P, NT + 1, D])
        gp = sb("e_gp", [P, D])
        wout_in, x_in = sem("e_wout_in"), sem("e_x_in")
        N = 12

        with ExitStack() as ix:
            sb1, _ = k.makers(ix)
            RING = 2
            ring = [sb1(f"e_w{i}", [P, DC, 2 * P]) for i in range(RING)]
            e = [sb1(f"e_e{i}", [P, 2, TH]) for i in range(2)]
            gs = sb1("e_gs", [P, 2, TH])
            sn = sb1("e_sn", [P, 3, 4, NB])
            w_in = [sem(f"e_w_in{i}") for i in range(RING)]
            proj_done, e_done, step, gs_done, turned, br_out, so_done, sn_done = (
                sem("e_" + n) for n in ("proj_done", "e_done", "step", "gs_done", "turned", "br_out", "so_done", "sn_done"))
            cols = [C_NSILU, C_FSILU, C_MSILU]
            with nc.Block() as block:
                @block.sync
                def _(sp):
                    for i in range(N // 2):
                        if i >= RING:
                            sp.wait_ge(proj_done, 2 * (i - RING) + 2)
                        col = cols[i // 2] + (i % 2) * 2 * P
                        sp.dma_start(ring[i % RING][:, :, :], k.w_in[:, col:col + 2 * P].rearrange("(c p) n -> p c n", p=P)).then_inc(w_in[i % RING], 16)
                    sp.dma_start(gp[:, :], k.g_post[0].partition_broadcast(P)).then_inc(x_in, 16)
                    sp.dma_start(x[:, 0:NT, :], k.x_prompt.rearrange("(t p) n -> p t n", p=P)).then_inc(x_in, 16)
                    sp.dma_start(x[0:NB, NT, :], k.x_sample).then_inc(x_in, 16)
                    sp.dma_start(wout[:, :, :], k.w_out.rearrange("(c p) n -> p c n", p=P)).then_inc(wout_in, 16)
                    sp.wait_ge(wout_in, 16)
                    sp.wait_ge(x_in, 48)

                @block.tensor
                def _(te):
                    nc.tensor.matmul(ps[7][:, 0:2 * NB * H], k.dupall, k.ow[:, :, :, :].rearrange("p i b h -> p (i b h)"), start=True, stop=True)
                    nc.tensor.matmul(ps[7][:, 2 * NB * H:3 * NB * H], k.dupall[0:64, :], k.oc[:, :, :].rearrange("p b h -> p (b h)"), start=True, stop=True).then_inc(so_done, 1)
                    for n in range(N):
                        te.wait_ge(w_in[(n // 2) % RING], 16 * (n // (2 * RING) + 1))
                        if n >= 2:
                            te.wait_ge(gs_done, n - 1)
                        for i in range(2):
                            for c in range(DC):
                                last = nc.tensor.matmul(banks(n % 2)[i][:, 0:TH], ring[(n // 2) % RING][:, c, (n % 2) * P:(n % 2) * P + P],
                                                        k.xnT[:, c, i * TH:(i + 1) * TH], start=c == 0, stop=c == DC - 1)
                        last.then_inc(proj_done, 1)
                        if n >= 2:
                            te.wait_ge(br_out, n - 1)
                        for t in range(NT):
                            last = nc.tensor.transpose(ps[4 + n % 2][:, t * P:(t + 1) * P], k.o[:, t, n * P:(n + 1) * P], k.ident)
                        last.then_inc(turned, 1)

                @block.scalar
                def _(sc):
                    for n in range(N):
                        sc.wait_ge(proj_done, n + 1)
                        if n >= 2:
                            sc.wait_ge(gs_done, n - 1)
                        for i in range(2):
                            last = nc.scalar.activation(e[n % 2][:, i, :], banks(n % 2)[i][:, 0:TH], ACT.Exp, scale=-1.0)
                        last.then_inc(e_done, 1)

                @block.gpsimd
                def _(pool):
                    pass

                @block.vector
                def _(ve):
                    ve.wait_ge(so_done, 1)
                    for i in range(3):
                        gate = k.sg[:, ((i + 1) % 3) * 4:((i + 1) % 3) * 4 + 4, :]
                        for j in range(2):
                            rows = slice(64 * j, 64 * j + 64)
                            src = ps[7][rows, i * 64:(i + 1) * 64].rearrange("p (b c j) -> p j c b", b=NB, j=2)[:, j]
                            nc.vector.tensor_tensor(sn[rows, i, :, :], src, gate[rows], ALU.mult).then_inc(sn_done, 1)
                    ve.wait_ge(sn_done, 6)
                    nc.vector.tensor_tensor(sn[:, 0], sn[:, 0], sn[:, 1], ALU.add).then_inc(sn_done, 1)
                    ve.wait_ge(sn_done, 7)
                    nc.vector.tensor_tensor(sn[:, 0], sn[:, 0], sn[:, 2], ALU.add).then_inc(sn_done, 1)
                    ve.wait_ge(sn_done, 8)
                    for n in range(N):
                        ve.wait_ge(e_done, n + 1)
                        en = e[n % 2]
                        nc.vector.tensor_scalar_add(en[:, :, :], en[:, :, :], 1.0).then_inc(step, 1)
                        ve.wait_ge(step, 2 * n + 1)
                        nc.vector.reciprocal(en[:, :, :], en[:, :, :]).then_inc(step, 1)
                        ve.wait_ge(step, 2 * n + 2)
                        if n:
                            ve.wait_ge(br_out, n)
                        for i in range(2):
                            last = nc.vector.tensor_tensor(gs[:, i, :], en[:, i, :], banks(n % 2)[i][:, 0:TH], ALU.mult)
                        last.then_inc(gs_done, 1)
                        ve.wait_ge(gs_done, n + 1)
                        ve.wait_ge(turned, n + 1)
                        flat = gs[:, :, :].rearrange("p i n -> p (i n)")
                        own = (sn[:, 0], k.of[:, :, :], k.om[:, :, :])[n // 4][:, n % 4, :]
                        nc.vector.tensor_tensor(br[:, n, T:TT], flat[:, T:TT], own, ALU.mult)
                        nc.vector.tensor_tensor(br[:, n, 0:T], flat[:, 0:T], ps[4 + n % 2][:, :], ALU.mult).then_inc(br_out, 1)

        with ExitStack() as ix:
            sb1, _ = k.makers(ix)
            wg = [sb1(f"e_wg{i}", [P, DC, P]) for i in range(3)]
            wb = [sb1(f"e_wb{i}", [P, 4, P]) for i in range(3)]
            e = [sb1(f"e_s{i}", [P, 2, TH]) for i in range(2)]
            tmp = sb1("e_tmp", [P, 2, TH])
            w_in = [sem(f"e_m_in{i}") for i in range(3)]
            z_done = [sem(f"e_z_done{i}") for i in range(3)]
            g_done, e_done, step, part, mt_done = (sem("e_m_" + n) for n in ("g_done", "e_done", "step", "part", "mt_done"))
            acc = sb1("e_acc", [P, 2, TH])
            k.prime(*z_done, part)
            with nc.Block() as block:
                @block.sync
                def _(sp):
                    with sp.Fori(0, DC) as d:
                        for b in range(3):
                            wait(sp, z_done[b], d)
                            sp.dma_start(wg[b][:, :, :], k.w_in[:, bass.ds(d * P + (C_BGATE + b * D), P)].rearrange("(c p) n -> p c n", p=P)).then_inc(w_in[b], 16)
                            sp.dma_start(wb[b][:, :, :], k.w_branch[b][:, bass.ds(d * P, P)].rearrange("(c p) n -> p c n", p=P)).then_inc(w_in[b], 16)

                @block.tensor
                def _(te):
                    with te.Fori(0, DC) as d:
                        for b in range(3):
                            wait(te, w_in[b], d * 32 + 32)
                            gb, zb = (ps[0:2], ps[2:4]) if b % 2 == 0 else (ps[4:6], ps[6:8])
                            wait(te, part, d * 3 + max(b - 1, 0))
                            for i in range(2):
                                for c in range(DC):
                                    last = nc.tensor.matmul(gb[i][:, 0:TH], wg[b][:, c, :], k.xnT[:, c, i * TH:(i + 1) * TH], start=c == 0, stop=c == DC - 1)
                            last.then_inc(g_done, 1)
                            for i in range(2):
                                for c in range(4):
                                    last = nc.tensor.matmul(zb[i][:, 0:TH], wb[b][:, c, :], br[:, b * 4 + c, i * TH:(i + 1) * TH], start=c == 0, stop=c == 3)
                            last.then_inc(z_done[b], 1)

                @block.scalar
                def _(sc):
                    with sc.Fori(0, DC) as d:
                        for b in range(3):
                            gb = ps[0:2] if b % 2 == 0 else ps[4:6]
                            wait(sc, g_done, d * 3 + b + 1)
                            wait(sc, part, d * 3 + max(b - 1, 0))
                            for i in range(2):
                                last = nc.scalar.activation(e[b % 2][:, i, :], gb[i][:, 0:TH], ACT.Exp, scale=-1.0)
                            last.then_inc(e_done, 1)

                @block.vector
                def _(ve):
                    with ve.Fori(0, DC) as d:
                        for b in range(3):
                            zb = ps[2:4] if b % 2 == 0 else ps[6:8]
                            wait(ve, e_done, d * 3 + b + 1)
                            nc.vector.tensor_scalar_add(e[b % 2][:, :, :], e[b % 2][:, :, :], 1.0).then_inc(step, 1)
                            wait(ve, step, d * 6 + 2 * b + 1)
                            nc.vector.reciprocal(e[b % 2][:, :, :], e[b % 2][:, :, :]).then_inc(step, 1)
                            wait(ve, step, d * 6 + 2 * b + 2)
                            wait(ve, z_done[b], d + 1)
                            for i in range(2):
                                last = nc.vector.tensor_tensor((tmp if b else acc)[:, i, :], e[b % 2][:, i, :], zb[i][:, 0:TH], ALU.mult)
                            last.then_inc(part, 1)
                            wait(ve, part, d * 3 + b + 1)
                            if b == 1:
                                nc.vector.tensor_tensor(acc[:, :, :], acc[:, :, :], tmp[:, :, :], ALU.add).then_inc(mt_done, 1)
                                wait(ve, mt_done, d * 2 + 1)
                            if b == 2:
                                nc.vector.tensor_tensor(mt[:, bass.ds(d, 1), :].rearrange("p a (i n) -> p (a i) n", i=2), acc[:, :, :], tmp[:, :, :], ALU.add).then_inc(mt_done, 1)
                                wait(ve, mt_done, d * 2 + 2)

        with ExitStack() as ix:
            sb1, _ = k.makers(ix)
            y = [sb1(f"e_y{i}", [P, D]) for i in range(2)]
            sq = sb1("e_sq", [P, 512])
            ss = sb1("e_ss", [P, NT + 1, 2])
            rs = sb1("e_rs", [P, NT + 1])
            wide = [P] * NT + [NB]
            y_done, sq_done, mean_done, rs_done, scaled, y_ready, out_done, sqc = (
                sem("e_y_" + n) for n in ("done", "sq", "mean", "rs", "scaled", "ready", "out", "sq_order"))
            with nc.Block() as block:
                @block.sync
                def _(sp):
                    for t, w in enumerate(wide):
                        sp.wait_ge(y_ready, t + 1)
                        dst = k.o_y_p[t * P:(t + 1) * P, :] if t < NT else k.o_y_s
                        sp.dma_start(dst, y[t % 2][0:w, :]).then_inc(out_done, 16)
                        sp.wait_ge(out_done, 16 * (t + 1))
                        sp.sem_inc(sqc, 1)

                @block.tensor
                def _(te):
                    for t, w in enumerate(wide):
                        if t >= 2:
                            te.wait_ge(scaled, t - 1)
                        for i in range(2):
                            for c in range(DC):
                                last = nc.tensor.matmul(banks(t % 2)[i][0:w, :], mt[:, c, t * P:t * P + w], wout[:, c, i * 512:(i + 1) * 512],
                                                        start=c == 0, stop=c == DC - 1)
                        last.then_inc(y_done, 1)

                @block.scalar
                def _(sc):
                    for t, w in enumerate(wide):
                        sc.wait_ge(y_done, t + 1)
                        for i in range(2):
                            if t or i:
                                sc.wait_ge(sq_done, 2 * t + i)
                            nc.scalar.activation(sq[0:w, :], banks(t % 2)[i][0:w, :], ACT.Square, accum_out=ss[0:w, t, i:i + 1]).then_inc(sq_done, 1)
                        sc.wait_ge(mean_done, 2 * t + 2)
                        nc.scalar.activation(rs[0:w, t:t + 1], rs[0:w, t:t + 1], ACT.Ln).then_inc(rs_done, 1)
                        sc.wait_ge(rs_done, 2 * t + 1)
                        nc.scalar.activation(rs[0:w, t:t + 1], rs[0:w, t:t + 1], ACT.Exp, scale=-0.5).then_inc(rs_done, 1)

                @block.vector
                def _(ve):
                    for t, w in enumerate(wide):
                        ve.wait_ge(sq_done, 2 * t + 2)
                        nc.vector.tensor_tensor(rs[0:w, t:t + 1], ss[0:w, t, 0:1], ss[0:w, t, 1:2], ALU.add).then_inc(mean_done, 1)
                        ve.wait_ge(mean_done, 2 * t + 1)
                        nc.vector.tensor_scalar(rs[0:w, t:t + 1], rs[0:w, t:t + 1], 1.0 / D, EPS, ALU.mult, ALU.add).then_inc(mean_done, 1)
                        ve.wait_ge(rs_done, 2 * t + 2)
                        if t >= 2:
                            ve.wait_ge(sqc, t - 1)
                        for i in range(2):
                            last = nc.vector.scalar_tensor_tensor(out=y[t % 2][0:w, i * 512:(i + 1) * 512], in0=banks(t % 2)[i][0:w, :], scalar=rs[0:w, t:t + 1],
                                                                  in1=gp[0:w, i * 512:(i + 1) * 512], op0=ALU.mult, op1=ALU.mult)
                        last.then_inc(scaled, 1)
                        ve.wait_ge(scaled, t + 1)
                        nc.vector.tensor_tensor(y[t % 2][0:w, :], y[t % 2][0:w, :], x[0:w, t, :], ALU.add).then_inc(y_ready, 1)


def hybrid_step(nc, x_prompt, x_sample, cache_nsa_cmp, cache_nsa_slc, state_nsa_win, cache_fox_kv, cache_fox_logf,
                cache_mem_kv, page_table, mem_prompt, g_pre, g_post, g_mem, w_in, b_fgate, w_mem_kv, w_cmp1, w_cmp2,
                pe_cmp, w_branch, w_out, consts, selectors, *outs):
    k = Shared()
    k.nc = nc
    k.x_prompt, k.x_sample, k.mem_prompt = x_prompt[0], x_sample.rearrange("b s d -> (b s) d"), mem_prompt[0]
    k.cache_cmp = cache_nsa_cmp[0].rearrange("n p v g d -> n p (v g d)")
    k.cache_slc = cache_nsa_slc[0].rearrange("n p v g d -> (n p) (v g d)")
    k.state_win = state_nsa_win[0].rearrange("b t v g d -> b t (v g d)")
    k.cache_fox = cache_fox_kv[0].rearrange("n p v h d -> n p v (h d)")
    k.cache_logf = cache_fox_logf[0].rearrange("n p h -> n (p h)")
    k.cache_mem = cache_mem_kv[0].rearrange("b t v h d -> b t (v h d)")
    k.page_table, k.g_pre, k.g_post, k.g_mem = page_table, g_pre, g_post, g_mem
    k.w_in, k.b_fgate, k.w_mem, k.w_cmp1, k.w_cmp2, k.pe_cmp = w_in[0], b_fgate, w_mem_kv[0], w_cmp1, w_cmp2, pe_cmp
    k.w_branch, k.w_out, k.consts = w_branch[0], w_out[0], consts
    k.selectors = selectors
    (k.o_y_p, k.o_y_s, k.o_cmp_p, k.o_slc_p, k.o_win_p, k.o_fkv_p, k.o_logf_p, k.o_mem_p,
     k.o_cmp_s, k.o_slc_s, k.o_win_s, k.o_fkv_s, k.o_logf_s) = outs

    primed = set()

    def makers(cx):
        held, sems = cx.enter_context(ExitStack()), []

        def semaphore(name):
            sems.append(held.enter_context(nc.semaphore(name)))
            return sems[-1]

        def clear():
            if sems:
                primed.difference_update(s.num for s in sems)
                with nc.Block() as block:
                    @block.gpsimd
                    def _(pool):
                        for s in sems:
                            pool.sem_clear(s)

        cx.callback(clear)
        return (lambda name, shape, dt=F32: cx.enter_context(nc.sbuf_tensor(name, shape, dt))), semaphore

    def prime(*sems):
        with nc.Block() as block:
            @block.gpsimd
            def _(pool):
                for s in sems:
                    primed.add(s.num)
                    pool.sem_inc(s, 1)

    def wait(engine, s, count):
        engine.wait_ge(s, count + 1 if s.num in primed else count)

    k.prime, k.wait = prime, wait

    with ExitStack() as cx:
        k.makers = makers
        sb, sem = makers(cx)
        k.logf_in, k.slc_in = [sem(f"logf_in{i}") for i in range(2)], sem("slc_in")
        k.ps = [cx.enter_context(nc.psum_tensor(f"bank{i}", [P, 512], F32)) for i in range(8)]
        k.cst = sb("cst", [P, NC])
        (k.ident, k.ones, k.swap, k.dup, k.dupall, k.causal, k.later, k.wsuf, k.cum, k.ropec, k.ropes, k.cneg, k.c01,
         k.diag, k.newneg, k.lcol, k.blk, k.blkrow, k.jmask, k.epart, k.headrow) = (
            k.cst[:, AT[name]:AT[name] + n] for name, n in CONSTS.items())
        k.table = sb("table", [1, NB * PAGES], I32)
        k.w2b, k.w2d = sb("w2b", [P, 2, P]), sb("w2d", [P, 2, P])
        k.pebias = sb("pebias", [P, 2])
        k.kcb, k.vcb = sb("kcb", [P, NB, 64]), sb("vcb", [64, NB, P])
        k.rpast = sb("rpast", [P, NB * PAGES, H])
        compress(k)
        forget(k)
        k.xnT = sb("xnT", [P, DC, TT])
        k.o = sb("o", [P, NT, 3 * BRW])
        k.srow, k.slrow = sb("srow", [NB, M_ALL]), sb("slrow", [NB, H])
        k.snew = sb("snew", [P, 3, NB, H])
        k.qd, k.qg, k.qz = sb("qd", [P, NB, H]), sb("qg", [P, NB, H]), sb("qz", [P, NB, 4, 2])
        k.mq, k.sg = sb("mq", [P, NB, MH]), sb("sg", [P, 12, NB])
        k.selrow = sb("selrow", [P, NB * G * 8], I32)
        k.oc, k.ow = sb("oc", [64, NB, H]), sb("ow", [P, 2, NB, H])
        k.of, k.om = sb("of", [P, 4, NB]), sb("om", [P, MH, NB])
        with ExitStack() as px:
            sb1, _ = makers(px)
            k.mnT = sb1("mnT", [P, DC, NM])
            norm(k)
            k.fm = sb1("fm", [P, K_ALL, TT])
            k.row = sb1("row", [P, NT, M_ALL])
            k.mrow, k.mkT = sb1("mrow", [P, NM // P, 2 * BRW]), sb1("mkT", [P, MH, NM])
            k.ncum, k.grow = sb1("ncum", [H, T]), sb1("grow", [P, NT, 24])
            with ExitStack() as gx:
                sb2, _ = makers(gx)
                k.gate, k.logf = sb2("gate", [24, TT]), sb2("logf", [H, TT])
                project(k)
                gates(k)
            prompt_compressed(k)
            sample_compressed(k)
            prompt(k)
        sample(k)
        merge(k)


_INS = ['x_prompt', 'x_sample', 'cache_nsa_cmp', 'cache_nsa_slc', 'state_nsa_win', 'cache_fox_kv', 'cache_fox_logf',
        'cache_mem_kv', 'page_table', 'mem_prompt', 'g_pre', 'g_post', 'g_mem', 'w_in', 'b_fgate', 'w_mem_kv', 'w_cmp1',
        'w_cmp2', 'pe_cmp', 'w_branch', 'w_out']
_OUTS = [((1, T, D), (T, D)), ((NB, 1, D), (NB, D)), ((1, 1, T, 2, G, HD), (T, 256)), ((1, 1, T, 2, G, HD), (T, 256)),
         ((1, 1, WIN, 2, G, HD), (T, 256)), ((1, 1, T, 2, H, HD), (T, 2 * BRW)), ((1, 1, T, H), (T, H)),
         ((1, 1, NM, 2, MH, P), (NM, 2 * BRW)), ((1, NB, 1, 2, G, HD), (NB, 256)), ((1, NB, 1, 2, G, HD), (NB, 256)),
         ((1, NB, WIN, 2, G, HD), (NB, WIN, 256)), ((1, NB, 1, 2, H, HD), (NB, 2 * BRW)), ((1, NB, 1, H), (NB, H))]


def kernel(**inputs):
    import concourse.bacc as bacc
    from concourse.bass_utils import run_bass_kernel_spmd

    nc = bacc.Bacc("TRN2", target_bir_lowering=False, num_devices=1)
    arrays = {name: np.ascontiguousarray(inputs[name]) for name in _INS}
    arrays["consts"], arrays["selectors"] = constants()
    args = [nc.dram_tensor(f"in_{name}", list(a.shape), mybir.dt.from_np(a.dtype), kind="ExternalInput").ap()
            for name, a in arrays.items()]
    args += [nc.dram_tensor(f"out_{i}", list(shape), F32, kind="ExternalOutput").ap() for i, (_, shape) in enumerate(_OUTS)]
    hybrid_step(nc, *args)
    r = run_bass_kernel_spmd(nc, [{f"in_{name}": a for name, a in arrays.items()}], core_ids=[0])
    return tuple(r.results[0][f"out_{i}"].reshape(shape) for i, (shape, _) in enumerate(_OUTS))
```

```python
from contextlib import ExitStack

import numpy as np

import concourse.bass as bass
from concourse import mybir

F32 = mybir.dt.float32
I32 = mybir.dt.int32
U32 = mybir.dt.uint32
ACT = mybir.ActivationFunctionType
ALU = mybir.AluOpType
AX = mybir.AxisListType.X
P = 128
D = 1024
DC = D // P
T = 512
NT = T // P
NB = 8
TT = T + NB
TH = TT // 2
HD = 64
H = 8
G = 2
R = H // G
MH = 4
NM = 256
PAGES = 32
POOL = 320
CB = 64
NBLK = PAGES * P // CB
NSEL = 15
WIN = 512
BRW = 512
EPS = 1e-6
NEG = -1e30
TINY = 1e-30
SCALE = HD ** -0.5
MSCALE = 128 ** -0.5

C_Q, C_CMP, C_SLC, C_WIN, C_GATE, C_NSILU = 0, 512, 768, 1024, 1280, 1304
C_FQ, C_FKV, C_FLOG, C_FSILU = 1816, 2328, 3352, 3360
C_MQ, C_MSILU, C_BGATE, N_IN = 3872, 4384, 4896, 7968
M_CMP, M_SLC, M_WIN, M_FK, M_FV, M_ALL = 0, 256, 512, 768, 1280, 1792
K_Q, K_FQ, K_MQ, K_FK, K_KD, K_ALL = 0, 4, 8, 12, 16, 20

CONSTS = dict(ident=128, ones=128, swap=128, dup=256, dupall=128, causal=128, later=128, wsuf=128,
              cum=512, ropec=TT, ropes=TT, cneg=32, c01=32, diag=NB, newneg=1, lcol=1,
              blk=NBLK, blkrow=NBLK, jmask=8, epart=128, headrow=H)
AT, at = {}, 0
for name, n in CONSTS.items():
    AT[name] = at
    at += n
NC = at


class Shared:
    pass


class Chunk:

    def __init__(self, col, w, mem, store=None, rope=None, turn=None, dup=None, chunks=1, last=None):
        self.col, self.w, self.mem, self.store, self.rope, self.turn = col, w, mem, store, rope, turn
        self.dup, self.chunks, self.last = dup, chunks, last


def constants():
    c = np.zeros((P, NC), np.float32)
    p = np.arange(P)
    col = lambda n: c[:, AT[n]:AT[n] + CONSTS[n]]
    col("ident")[:] = np.eye(P)
    col("ones")[:] = 1
    half = 8
    r = p % HD
    for a in range(P):
        if r[a] < half:
            col("swap")[a, a + half] = col("swap")[a + half, a] = 1
    for g in range(2):
        for m in range(P):
            col("dup")[g * 64 + m % 64, g * P + m] = 1
    col("dupall")[:] = (p[:, None] % 64) == (p[None] % 64)
    col("causal")[:] = np.where(p[None] <= p[:, None], 0, NEG)
    col("later")[:] = p[:, None] > p[None]
    col("wsuf")[:] = (p[:, None] // PAGES == p[None] // PAGES) & (p[:, None] > p[None])
    col("cum")[:] = np.arange(512)[None] >= p[:, None]
    pos = np.concatenate([np.arange(T), np.full(NB, PAGES * P)]).astype(np.float32)
    inv = np.float32(500000.0) ** (-np.arange(half, dtype=np.float32) / np.float32(half))
    ang = (pos[None] * inv[:, None]).astype(np.float32)
    col("ropec")[:] = 1
    for a in range(P):
        if r[a] < 2 * half:
            col("ropec")[a] = np.cos(ang[r[a] % half])
            col("ropes")[a] = np.sin(ang[r[a] % half]) * (-1 if r[a] < half else 1)
    sel = np.zeros((24, 12 * P + H * P), np.float32)
    for h in range(H):
        sel[h, (12 + h) * P:(13 + h) * P] = 1
    t = (np.arange(NT)[None, :, None, None] * P + p[:, None, None, None])
    b = (np.arange(2)[None, None, :, None] + 2 * np.arange(NT)[None, None, None, :])
    ok = ((b + 1) * CB - 1 <= t).reshape(P, 32)
    col("cneg")[:] = np.where(ok, 0, NEG)
    col("c01")[:] = ok
    col("diag")[:] = np.where(p[:, None] == np.arange(NB)[None], 0, NEG)
    col("newneg")[:, 0] = np.where(p < 64, 0, NEG)
    col("lcol")[:, 0] = p % CB
    col("blk")[:] = np.arange(NBLK)[None]
    col("blkrow")[:] = (np.arange(NBLK)[None] % 2) * CB
    col("jmask")[:] = (p[:, None] // 2) == np.arange(8)[None]
    col("epart")[:] = (p[:, None] % 2) == (p[None] // 64)
    col("headrow")[:] = (p[:, None] // 8) == np.arange(H)[None]
    for br in range(3):
        for ch in range(4):
            for m in range(P):
                sel[br * 8 + 2 * ch + m // 64, (br * 4 + ch) * P + m] = 1
    return c, sel


def compress(k):
    nc, ps, wait = k.nc, k.ps, k.wait
    UP = 2 * PAGES
    UNITS = NB * PAGES // UP
    with ExitStack() as cx:
        sb, sem = k.makers(cx)
        w1 = sb("c_w1", [P, 2, CB, P])
        page = [sb(f"c_page{i}", [P, UP + (i == 0), 256]) for i in range(2)]
        table_in, w2_in, pe_in = sem("c_table_in"), sem("c_w2_in"), sem("c_pe_in")
        w_in = [sem(f"c_w_in{v}") for v in range(2)]
        w_zero, pe_placed = sem("c_w_zero"), sem("c_pe_placed")
        page_in = [sem(f"c_page_in{i}") for i in range(2)]
        page_free = [sem(f"c_page_free{i}") for i in range(2)]
        pe_summed, z_done, e_done, inverted, h_done = (sem("c_" + n) for n in ("pe_summed", "z_done", "e_done", "inverted", "h_done"))
        blocks_done, blocks_out = sem("c_blocks_done"), sem("c_blocks_out")
        pe = sb("c_pe", [P, 2, HD])
        z = sb("c_z", [P, 2, 2, UP])
        ez = sb("c_ez", [P, 2, 2, UP])
        hid = sb("c_hid", [P, 2, 2, 2, PAGES])
        hp = [ps[i][:, 0:4 * (UP + 1 - i)].rearrange("p (v g n) -> p v g n", v=2, g=2) for i in range(2)]
        w1_d = k.w_cmp1[0]

        k.prime(*page_free, z_done, h_done, blocks_done, blocks_out)
        with nc.Block() as block:
            def load_pages(queue, i, s):
                wait(queue, page_free[s], i)
                first = 0 if queue is nc.sync else PAGES
                for j in range(first, first + PAGES):
                    pg = queue.value_load(k.table[0:1, bass.ds(i * (2 * UP) + s * UP + j, 1)], min_val=0, max_val=POOL - 1)
                    queue.dma_start(page[s][:, j:j + 1, :],
                                    k.cache_cmp[bass.ds(pg, 1), :, :].rearrange("a p n -> p a n")).then_inc(page_in[s], 16)

            @block.sync
            def _(sp):
                sp.dma_start(k.table[:, :], k.page_table.rearrange("b n -> (b n)").unsqueeze(0)).then_inc(table_in, 16)
                for half in range(2):
                    rows = slice(64 * half, 64 * half + 64)
                    sp.dma_start(pe[rows, :, :], k.pe_cmp[0].rearrange("v l d -> l v d")).then_inc(pe_in, 16)
                for v in range(2):
                    for half in range(2):
                        rows = slice(64 * half, 64 * half + 64)
                        sp.dma_start(w1[rows, v, :, rows], w1_d[v]).then_inc(w_in[v], 16)
                wait(sp, table_in, 16)
                load_pages(sp, 0, 0)
                for half in range(2):
                    rows = slice(64 * half, 64 * half + 64)
                    for v in range(2):
                        sp.dma_start(k.w2b[rows, v, rows], k.w_cmp2[0, v]).then_inc(w2_in, 16)
                        for other in range(2):
                            sp.dma_start(k.w2d[rows, v, 64 * other:64 * other + 64], k.w_cmp2[0, v]).then_inc(w2_in, 16)
                load_pages(sp, 0, 1)
                with sp.Fori(1, UNITS // 2) as i:
                    for s in range(2):
                        load_pages(sp, i, s)
                wait(sp, w2_in, 16 * 12)

            @block.gpsimd
            def _(pool):
                for v in range(2):
                    nc.gpsimd.memset(w1[0:64, v, :, 64:128], 0.0)
                    nc.gpsimd.memset(w1[64:128, v, :, 0:64], 0.0)
                    nc.gpsimd.memset(k.w2b[0:64, v, 64:128], 0.0)
                    nc.gpsimd.memset(k.w2b[64:128, v, 0:64], 0.0).then_inc(w_zero, 1)
                wait(pool, w_zero, 2)
                wait(pool, pe_in, 32)
                for g in range(2):
                    dst = page[0][:, UP, :].rearrange("p (v g d) -> p v g d", v=2, g=2)[:, :, g, :]
                    nc.gpsimd.tensor_copy(dst, pe[:, :, :]).then_inc(pe_placed, 1)

            @block.tensor
            def _(te):
                def products(i, s):
                    wait(te, page_in[s], i * (16 * UP) + 16 * UP)
                    wait(te, z_done, i * 4 + 2 * s - 2 if s else i * 4)
                    rows = page[s][:, :, :].rearrange("p n (v g d) -> p v d g n", v=2, g=2)
                    for v in range(2):
                        if isinstance(i, int) and i == 0 and s == 0:
                            wait(te, w_in[v], 32)
                        for d in range(HD):
                            last = nc.tensor.matmul(hp[s][:, v], w1[:, v, d, :], rows[:, v, d],
                                                    start=d == 0, stop=d == HD - 1)
                    last.then_inc(page_free[s], 1)

                def second_layer(i, s):
                    wait(te, h_done, i * 2 + s + 1)
                    wait(te, blocks_out, i * 4 + 2 * s)
                    nc.tensor.matmul(ps[2][:, 0:128], k.w2b[:, 0, :], hid[:, 0, :, :, :].rearrange("p s g n -> p (s g n)"),
                                     start=True, stop=True)
                    for seq in range(2):
                        last = nc.tensor.matmul(ps[3][0:64, seq * P:(seq + 1) * P], hid[:, 1, seq, :, :].rearrange("p g n -> p (g n)"),
                                                k.w2b[:, 1, :], start=True, stop=True)
                    last.then_inc(blocks_done, 1)

                wait(te, w_zero, 2)
                wait(te, pe_placed, 2)
                products(0, 0)
                wait(te, w2_in, 16 * 12)
                with te.Fori(0, UNITS // 2 - 1) as i:
                    products(i, 1)
                    second_layer(i, 0)
                    products(i + 1, 0)
                    second_layer(i, 1)
                products(UNITS // 2 - 1, 1)
                second_layer(UNITS // 2 - 1, 0)
                second_layer(UNITS // 2 - 1, 1)

            @block.vector
            def _(ve):
                wait(ve, page_free[0], 1)
                nc.vector.tensor_copy(k.pebias[:, :], hp[0][:, :, 0, UP]).then_inc(pe_summed, 1)
                wait(ve, pe_summed, 1)
                with ve.Fori(0, UNITS // 2) as i:
                    for s in range(2):
                        wait(ve, page_free[s], i + 1)
                        wait(ve, h_done, i * 2 + s)
                        for v in range(2):
                            nc.vector.tensor_scalar(z[:, v], hp[s][:, v, :, 0:UP], k.pebias[:, v:v + 1], None, ALU.add).then_inc(z_done, 1)
                        wait(ve, e_done, i * 4 + 2 * s + 1)
                        nc.vector.tensor_scalar_add(ez[:, :, :, :], ez[:, :, :, :], 1.0).then_inc(e_done, 1)
                        wait(ve, e_done, i * 4 + 2 * s + 2)
                        nc.vector.reciprocal(ez[:, :, :, :], ez[:, :, :, :]).then_inc(inverted, 1)
                        wait(ve, inverted, i * 2 + s + 1)
                        wait(ve, blocks_done, i * 2 + s)
                        for v in range(2):
                            halves = lambda a: a[:, v].rearrange("p g (s n) -> p s g n", s=2)
                            last = nc.vector.tensor_tensor(hid[:, v], halves(z), halves(ez), ALU.mult)
                        last.then_inc(h_done, 1)

            @block.scalar
            def _(sc):
                def exponentials(i, s):
                    wait(sc, z_done, i * 4 + 2 * s + 2)
                    wait(sc, h_done, i * 2 + s)
                    nc.scalar.activation(ez[:, :, :, :], z[:, :, :, :], ACT.Exp, scale=-1.0).then_inc(e_done, 1)

                def blocks(i, s):
                    wait(sc, blocks_done, i * 2 + s + 1)
                    at = i * 4 + s * 2
                    at = slice(at, at + 2) if isinstance(at, int) else bass.ds(at, 2)
                    nc.scalar.activation(k.kcb[:, at, :], ps[2][:, 0:128].rearrange("p (s n) -> p s n", s=2), ACT.Copy).then_inc(blocks_out, 1)
                    nc.scalar.activation(k.vcb[:, at, :], ps[3][0:64, 0:256].rearrange("p (s n) -> p s n", s=2), ACT.Copy).then_inc(blocks_out, 1)

                wait(sc, table_in, 16)
                load_pages(sc, 0, 0)
                load_pages(sc, 0, 1)
                with sc.Fori(0, UNITS // 2 - 1) as i:
                    for s in range(2):
                        exponentials(i, s)
                        load_pages(sc, i + 1, s)
                        blocks(i, s)
                for s in range(2):
                    exponentials(UNITS // 2 - 1, s)
                    blocks(UNITS // 2 - 1, s)


def forget(k):
    nc, ps = k.nc, k.ps
    with ExitStack() as cx:
        sb, sem = k.makers(cx)
        logf = sb("g_logf", [P, 2, P * H])
        rows = sb("g_rows", [P, 2, H, P])
        total = sb("g_total", [P, 2, P])
        idx = sb("g_idx", [P, 2], I32)
        idx_in, const_in, logf_in = sem("g_idx_in"), sem("g_const_in"), k.logf_in
        turned, rows_out, tot_done, tot_out, sum_done, sum_out = (sem(n) for n in (
            "g_turned", "g_rows_out", "g_tot_done", "g_tot_out", "g_sum_done", "g_sum_out"))
        r = k.rpast[:, :, :].rearrange("p (a c n) h -> p a h c n", a=2, n=PAGES)
        with nc.Block() as block:
            @block.sync
            def _(sp):
                for a in range(2):
                    sp.dma_start(idx[:, a:a + 1], k.page_table.rearrange("(a c) n -> a (c n)", a=2)[a].unsqueeze(1))\
                      .then_inc(idx_in, 16)
                sp.dma_start(k.cst[:, :], k.consts).then_inc(const_in, 16)
                sp.wait_ge(idx_in, 32)

            @block.gpsimd
            def _(pool):
                pool.wait_ge(idx_in, 32)
                for a in range(2):
                    nc.gpsimd.indirect_dma_start(
                        out=logf[:, a, :], out_offset=None, in_=k.cache_logf,
                        in_offset=bass.IndirectOffsetOnAxis(ap=idx[:, a:a + 1].bitcast(U32), axis=0),
                        bounds_check=POOL - 1, oob_is_err=False).then_inc(logf_in[a], 16)

            @block.tensor
            def _(te):
                te.wait_ge(const_in, 16)
                for a in range(2):
                    te.wait_ge(logf_in[a], 16)
                    for hh in range(2):
                        for h in range(4):
                            src = logf[:, a, :].rearrange("p (r h) -> p h r", h=H)[:, 4 * hh + h]
                            last = nc.tensor.transpose(ps[2 * a + hh][:, h * P:(h + 1) * P], src, k.ident)
                        last.then_inc(turned, 1)
                for n in range(2 * H):
                    a, h = n // H, n % H
                    te.wait_ge(rows_out, n // 4 + 1)
                    if n >= 2:
                        te.wait_ge(tot_out, n - 1)
                    nc.tensor.matmul(ps[4 + n % 2][:, 0:P], rows[:, a, h, :], k.ones, start=True, stop=True).then_inc(tot_done, 1)
                    if n >= 2:
                        te.wait_ge(sum_out, n - 1)
                    te.wait_ge(tot_out, n + 1)
                    nc.tensor.matmul(ps[6 + n % 2][:, 0:P], k.later, rows[:, a, h, :], start=True, stop=False)
                    nc.tensor.matmul(ps[6 + n % 2][:, 0:P], total[:, n % 2, :], k.wsuf, start=False, stop=True).then_inc(sum_done, 1)

            @block.scalar
            def _(sc):
                for n in range(4):
                    sc.wait_ge(turned, n + 1)
                    nc.scalar.activation(rows[:, n // 2, 4 * (n % 2):4 * (n % 2) + 4, :],
                                         ps[n][:, :].rearrange("p (h n) -> p h n", h=4), ACT.Copy).then_inc(rows_out, 1)
                for n in range(2 * H):
                    sc.wait_ge(tot_done, n + 1)
                    if n >= 2:
                        sc.wait_ge(sum_done, n - 1)
                    nc.scalar.activation(total[:, n % 2, :], ps[4 + n % 2][:, 0:P], ACT.Copy).then_inc(tot_out, 1)

            @block.vector
            def _(ve):
                for n in range(2 * H):
                    ve.wait_ge(sum_done, n + 1)
                    nc.vector.tensor_copy(r[:, n // H, n % H], ps[6 + n % 2][:, 0:P].rearrange("p (c n) -> p c n", c=4)).then_inc(sum_out, 1)


def norm(k):
    nc, ps = k.nc, k.ps
    with ExitStack() as cx:
        sb, sem = k.makers(cx)
        NX, NMT = NT + 1, NM // P
        x = sb("n_x", [P, NX + NMT, D])
        gb = sb("n_g", [P, 2, D])
        sq = sb("n_sq", [P, D])
        ss = sb("n_ss", [P, NX + NMT])
        x_in = [sem(f"n_x_in{i}") for i in range(NX + NMT)]
        g_in, sq_done, rstd_done, act_rstd, scaled, turned, placed, ss_set = (sem(n) for n in (
            "n_g_in", "n_sq_done", "n_rstd_done", "n_act_rstd", "n_scaled", "n_turned", "n_placed", "n_ss_set"))
        wide = [P] * NT + [NB] + [P] * NMT

        with nc.Block() as block:
            @block.sync
            def _(sp):
                for t in range(NT):
                    sp.dma_start(x[:, t, :], k.x_prompt[t * P:(t + 1) * P, :]).then_inc(x_in[t], 16)
                sp.dma_start(x[0:NB, NT, :], k.x_sample).then_inc(x_in[NT], 16)
                for i, g in enumerate((k.g_pre, k.g_mem)):
                    sp.dma_start(gb[:, i, :], g[0].partition_broadcast(P)).then_inc(g_in, 16)
                for t in range(NMT):
                    sp.dma_start(x[:, NX + t, :], k.mem_prompt[t * P:(t + 1) * P, :]).then_inc(x_in[NX + t], 16)

            @block.scalar
            def _(sc):
                sc.wait_ge(ss_set, 1)
                for t, w in enumerate(wide):
                    sc.wait_ge(x_in[t], 16)
                    if t:
                        sc.wait_ge(sq_done, t)
                    nc.scalar.activation(sq[0:w, :], x[0:w, t, :], ACT.Square, accum_out=ss[0:w, t:t + 1]).then_inc(sq_done, 1)
                sc.wait_ge(rstd_done, 1)
                nc.scalar.activation(ss[:, :], ss[:, :], ACT.Ln).then_inc(act_rstd, 1)
                sc.wait_ge(act_rstd, 1)
                nc.scalar.activation(ss[:, :], ss[:, :], ACT.Exp, scale=-0.5).then_inc(act_rstd, 1)
                for t, w in enumerate(wide):
                    for half in range(2):
                        n = 2 * t + half
                        sc.wait_ge(turned, n + 1)
                        src = ps[n % 4][:, :].rearrange("p (c n) -> p c n", c=4)[:, :, 0:w]
                        if t < NX:
                            dst = k.xnT[:, 4 * half:4 * half + 4, t * P:t * P + w]
                        else:
                            dst = k.mnT[:, 4 * half:4 * half + 4, (t - NX) * P:(t - NX + 1) * P]
                        nc.scalar.activation(dst, src, ACT.Copy).then_inc(placed, 1)

            @block.vector
            def _(ve):
                ve.wait_ge(sq_done, NX + NMT)
                nc.vector.tensor_scalar(ss[:, :], ss[:, :], 1.0 / D, EPS, ALU.mult, ALU.add).then_inc(rstd_done, 1)
                ve.wait_ge(act_rstd, 2)
                ve.wait_ge(g_in, 32)
                for t, w in enumerate(wide):
                    nc.vector.scalar_tensor_tensor(out=x[0:w, t, :], in0=x[0:w, t, :], scalar=ss[0:w, t:t + 1],
                                                   in1=gb[0:w, int(t >= NX), :], op0=ALU.mult, op1=ALU.mult).then_inc(scaled, 1)

            @block.gpsimd
            def _(pool):
                nc.gpsimd.memset(ss[:, :], 1.0).then_inc(ss_set, 1)

            @block.tensor
            def _(te):
                for t, w in enumerate(wide):
                    te.wait_ge(scaled, t + 1)
                    for half in range(2):
                        n = 2 * t + half
                        if n >= 4:
                            te.wait_ge(placed, n - 3)
                        for c in range(4):
                            f = 4 * half + c
                            last = nc.tensor.transpose(ps[n % 4][:, c * P:c * P + w], x[0:w, t, f * P:(f + 1) * P], k.ident[0:w, 0:w])
                        last.then_inc(turned, 1)


def project(k):
    nc, ps = k.nc, k.ps
    chunks = []

    def add(col, w=P, mem=False, store=None, rope=False, turn=None, dup=None):
        chunks.append(Chunk(col=col, w=w, mem=mem, store=store, rope=rope, turn=turn, dup=dup))

    for c in range(4):
        add(C_Q + c * P, store=("fm", K_Q + c), rope=True)
    add(C_CMP, rope=True, turn=M_CMP)
    add(C_CMP + P, turn=M_CMP + P)
    add(C_SLC, rope=True, turn=M_SLC, dup=K_KD)
    add(C_SLC + P, turn=M_SLC + P)
    add(C_WIN, rope=True, turn=M_WIN, dup=K_KD + 2)
    add(C_WIN + P, turn=M_WIN + P)
    add(C_GATE, 24, store=("gate", 0))
    for c in range(4):
        add(C_FQ + c * P, store=("fm", K_FQ + c))
    for c in range(4):
        add(C_FKV + c * P, store=("fm", K_FK + c), turn=M_FK + c * P)
    for c in range(4):
        add(C_FKV + BRW + c * P, turn=M_FV + c * P)
    add(C_FLOG, 8, store=("logf", 0))
    for c in range(4):
        add(C_MQ + c * P, store=("fm", K_MQ + c))
    for c in range(4):
        add(c * P, mem=True, store=("memk", c), turn=c * P)
    for c in range(4):
        add(BRW + c * P, mem=True, turn=BRW + c * P)

    loads = []
    for n, ch in enumerate(chunks):
        prev = loads[-1] if loads else None
        if prev and prev.chunks == 1 and prev.mem == ch.mem and prev.col + P == ch.col and prev.w == P and ch.w == P:
            prev.w, prev.chunks, prev.last = 2 * P, 2, n
        else:
            loads.append(Chunk(col=ch.col, w=ch.w, mem=ch.mem, chunks=1, last=n))
        ch.load, ch.off = len(loads) - 1, ch.col - loads[-1].col
    ropes = turns = dups = 0
    for ch in chunks:
        ch.rope_no = ropes = ropes + bool(ch.rope)
        ch.turn_no = turns = turns + (ch.turn is not None)
        ch.dup_no = dups = dups + (ch.dup is not None)
    RING, STG = 2, 3

    with ExitStack() as cx:
        sb, sem = k.makers(cx)
        ring = [sb(f"p_w{i}", [P, DC, 2 * P]) for i in range(RING)]
        stg = [sb(f"p_stg{i}", [P, 2, TH]) for i in range(STG)]
        t1, t2 = sb("p_t1", [P, 2, TH]), sb("p_t2", [P, 2, TH])
        w_in = [sem(f"p_w_in{i}") for i in range(RING)]
        (proj_done, stg_ready, swap_done, t1_done, t2_done, rope_done, turned, placed, dup_done, dup_out) = (
            sem("p_" + n) for n in ("proj_done", "stg_ready", "swap_done", "t1_done", "t2_done", "rope_done",
                                    "turned", "placed", "dup_done", "dup_out"))
        pj = [[ps[0], ps[1]], [ps[2], ps[3]]]
        rp, tp, tsp = [ps[4], ps[5]], ps[6], ps[7]
        halves = lambda a: a.rearrange("p (i n) -> p i n", i=2)

        def place(ch):
            kind, i = ch.store if ch.store else ("stg", 0)
            if kind == "fm":
                return halves(k.fm[:, i, :])
            if kind == "gate":
                return halves(k.gate[:, :])
            if kind == "logf":
                return halves(k.logf[:, :])
            if kind == "memk":
                return k.mkT[:, i, :]
            s = stg[ch.n % STG]
            return s[:, 0, 0:NM] if ch.mem else s[:, :, :]

        for n, ch in enumerate(chunks):
            ch.n = n
            ch.first = stg[n % STG][:, :, :] if ch.rope else place(ch)
            ch.final = place(ch)
            ch.uses_stg = ch.store is None or ch.rope

        def free_of(ch, engine):
            if ch.dup is not None:
                engine.wait_ge(dup_done, 2 * ch.dup_no)
            elif ch.turn is not None:
                engine.wait_ge(turned, ch.turn_no)
            if ch.rope:
                engine.wait_ge(rope_done, ch.rope_no)

        with nc.Block() as block:
            @block.sync
            def _(sp):
                for i, ld in enumerate(loads):
                    if i >= RING:
                        sp.wait_ge(proj_done, loads[i - RING].last + 1)
                    src = (k.w_mem if ld.mem else k.w_in)[:, ld.col:ld.col + ld.w]
                    sp.dma_start(ring[i % RING][:, :, 0:ld.w], src.rearrange("(c p) n -> p c n", p=P)).then_inc(w_in[i % RING], 16)

            @block.tensor
            def _(te):
                def product(ch):
                    te.wait_ge(w_in[ch.load % RING], 16 * (ch.load // RING + 1))
                    if ch.n >= 2:
                        te.wait_ge(stg_ready, ch.n - 1)
                    w = ring[ch.load % RING]
                    for i in range(1 if ch.mem else 2):
                        for c in range(DC):
                            rhs = k.mnT[:, c, :] if ch.mem else k.xnT[:, c, i * TH:(i + 1) * TH]
                            last = nc.tensor.matmul(pj[ch.n % 2][i][0:ch.w, 0:NM if ch.mem else TH],
                                                    w[:, c, ch.off:ch.off + ch.w], rhs, start=c == 0, stop=c == DC - 1)
                    last.then_inc(proj_done, 1)

                def swap(ch):
                    te.wait_ge(stg_ready, ch.n + 1)
                    te.wait_ge(t1_done, ch.rope_no - 1)
                    if ch.dup_no - (ch.dup is not None):
                        te.wait_ge(dup_out, 2 * (ch.dup_no - (ch.dup is not None)))
                    for i in range(2):
                        last = nc.tensor.matmul(rp[i][:, 0:TH], k.swap, ch.first[:, i, :], start=True, stop=True)
                    last.then_inc(swap_done, 1)

                def turn(ch):
                    te.wait_ge(stg_ready, ch.n + 1)
                    if ch.rope:
                        te.wait_ge(rope_done, ch.rope_no)
                    if ch.turn_no > 1:
                        te.wait_ge(placed, 2 * (ch.turn_no - 1))
                    src = ch.final if ch.mem else ch.final
                    flat = src if ch.mem else src.rearrange("p i n -> p (i n)")
                    for t in range(NM // P if ch.mem else NT):
                        last = nc.tensor.transpose(tp[:, t * P:(t + 1) * P], flat[:, t * P:(t + 1) * P], k.ident)
                    if not ch.mem:
                        last = nc.tensor.transpose(tsp[0:NB, 0:P], flat[:, T:TT], k.ident)
                    last.then_inc(turned, 1)
                    if ch.dup is not None:
                        for g in range(2):
                            te.wait_ge(t1_done, ch.rope_no)
                            if ch.dup_no > 1 or g:
                                te.wait_ge(dup_out, 2 * (ch.dup_no - 1) + g)
                            for i in range(2):
                                last = nc.tensor.matmul(rp[i][:, 0:TH], k.dup[:, g * P:(g + 1) * P], ch.final[:, i, :], start=True, stop=True)
                            last.then_inc(dup_done, 1)

                for n in range(len(chunks) + 2):
                    if n < len(chunks):
                        product(chunks[n])
                    if 1 <= n <= len(chunks) and chunks[n - 1].rope:
                        swap(chunks[n - 1])
                    if n >= 2 and chunks[n - 2].turn is not None:
                        turn(chunks[n - 2])

            @block.scalar
            def _(sc):
                def copies(ch):
                    for g in range(2):
                        sc.wait_ge(dup_done, 2 * (ch.dup_no - 1) + g + 1)
                        for i in range(2):
                            last = nc.scalar.activation(halves(k.fm[:, ch.dup + g, :])[:, i, :], rp[i][:, 0:TH], ACT.Copy)
                        last.then_inc(dup_out, 1)

                for n in range(len(chunks) + 3):
                    if n < len(chunks):
                        ch = chunks[n]
                        sc.wait_ge(proj_done, n + 1)
                        if n >= STG and ch.uses_stg:
                            for old in range(n - STG, -1, -STG):
                                if chunks[old].uses_stg:
                                    free_of(chunks[old], sc)
                                    break
                        if ch.mem:
                            nc.scalar.activation(ch.first, pj[n % 2][0][:, 0:NM], ACT.Copy).then_inc(stg_ready, 1)
                        else:
                            nc.scalar.activation(ch.first[0:ch.w, 0, :], pj[n % 2][0][0:ch.w, 0:TH], ACT.Copy)
                            nc.scalar.activation(ch.first[0:ch.w, 1, :], pj[n % 2][1][0:ch.w, 0:TH], ACT.Copy).then_inc(stg_ready, 1)
                    if n >= 2 and n - 2 < len(chunks) and chunks[n - 2].dup is not None:
                        copies(chunks[n - 2])

            @block.gpsimd
            def _(pool):
                for ch in chunks:
                    if ch.rope:
                        pool.wait_ge(stg_ready, ch.n + 1)
                        if ch.rope_no > 1:
                            pool.wait_ge(rope_done, ch.rope_no - 1)
                        nc.gpsimd.tensor_tensor(t2[:, :, :], ch.first, halves(k.ropec), ALU.mult).then_inc(t2_done, 1)

            @block.vector
            def _(ve):
                def rope(ch):
                    ve.wait_ge(swap_done, ch.rope_no)
                    if ch.rope_no > 1:
                        ve.wait_ge(rope_done, ch.rope_no - 1)
                    for i in range(2):
                        last = nc.vector.tensor_tensor(t1[:, i, :], rp[i][:, 0:TH], halves(k.ropes)[:, i, :], ALU.mult)
                    last.then_inc(t1_done, 1)
                    ve.wait_ge(t1_done, ch.rope_no)
                    ve.wait_ge(t2_done, ch.rope_no)
                    nc.vector.tensor_tensor(ch.final, t1[:, :, :], t2[:, :, :], ALU.add).then_inc(rope_done, 1)

                def row(ch):
                    ve.wait_ge(turned, ch.turn_no)
                    if ch.mem:
                        nc.vector.tensor_copy(k.mrow[:, 0, ch.turn:ch.turn + P], tp[:, 0:P]).then_inc(placed, 1)
                        nc.vector.tensor_copy(k.mrow[:, 1, ch.turn:ch.turn + P], tp[:, P:2 * P]).then_inc(placed, 1)
                    else:
                        nc.vector.tensor_copy(k.row[:, :, ch.turn:ch.turn + P], tp[:, :].rearrange("p (t n) -> p t n", t=NT)).then_inc(placed, 1)
                        nc.vector.tensor_copy(k.srow[:, ch.turn:ch.turn + P], tsp[0:NB, 0:P]).then_inc(placed, 1)

                for n in range(len(chunks) + 2):
                    if 1 <= n <= len(chunks) and chunks[n - 1].rope:
                        rope(chunks[n - 1])
                    if n >= 2 and chunks[n - 2].turn is not None:
                        row(chunks[n - 2])


def gates(k):
    nc, ps = k.nc, k.ps
    with ExitStack() as cx:
        sb, sem = k.makers(cx)
        e8 = sb("a_e8", [H, TT])
        m8 = sb("a_m8", [H, TT])
        bf = sb("a_bf", [H, 1])
        lrow = sb("a_lrow", [P, NT, H])
        qs = sb("a_qs", [P, 8, NB])
        gsig = sb("a_gsig", [24, TT])
        gsel = sb("a_gsel", [24, 12 * P])
        b_in, gsel_in, out_done = sem("a_b_in"), sem("a_gsel_in"), sem("a_out_done")
        va, vb, vc = sem("a_vector_step"), sem("a_scalar_step"), sem("a_scalar_gate")
        qs_done, q_up, row_done, row_out, cum_done, gate_row, gate_out, new_done, pool_zero, dup_done, scl = (
            sem("a_" + n) for n in ("qs_done", "q_up", "lrow_done", "lrow_out", "cum_done", "gate_row",
                                    "gate_out", "new_done", "pool_zero", "qdup_done", "last"))
        with nc.Block() as block:
            @block.sync
            def _(sp):
                sp.dma_start(bf[:, :], k.b_fgate.rearrange("a h -> h a")).then_inc(b_in, 16)
                sp.dma_start(gsel[:, :], k.selectors[:, 0:12 * P]).then_inc(gsel_in, 16)
                rows = lambda a: a.rearrange("(t p) n -> p t n", p=P)
                outs = [(rows(k.o_cmp_p), k.row[:, :, M_CMP:M_CMP + 256]), (rows(k.o_slc_p), k.row[:, :, M_SLC:M_SLC + 256]),
                        (rows(k.o_win_p), k.row[:, :, M_WIN:M_WIN + 256]), (rows(k.o_fkv_p), k.row[:, :, M_FK:M_ALL]),
                        (rows(k.o_mem_p), k.mrow[:, :, :]),
                        (k.o_cmp_s, k.srow[:, M_CMP:M_CMP + 256]), (k.o_slc_s, k.srow[:, M_SLC:M_SLC + 256]),
                        (k.o_win_s[:, WIN - 1, :], k.srow[:, M_WIN:M_WIN + 256]), (k.o_fkv_s, k.srow[:, M_FK:M_ALL]),
                        (k.o_win_s[:, 0:WIN - 1, :], k.state_win[:, 1:WIN, :])]
                for dst, src in outs:
                    sp.dma_start(dst, src).then_inc(out_done, 16)
                sp.wait_ge(row_out, 2)
                sp.dma_start(rows(k.o_logf_p), lrow[:, :, :]).then_inc(out_done, 16)
                sp.dma_start(k.o_logf_s, k.slrow[:, :]).then_inc(out_done, 16)
                sp.wait_ge(out_done, 16 * (len(outs) + 2))

            @block.vector
            def _(ve):
                ve.wait_ge(b_in, 16)
                nc.vector.tensor_scalar(k.logf[:, :], k.logf[:, :], bf[:, 0:1], None, ALU.add).then_inc(va, 1)
                ve.wait_ge(va, 1)
                nc.vector.tensor_scalar(m8[:, :], k.logf[:, :], -1.0, None, ALU.mult).then_inc(va, 1)
                ve.wait_ge(va, 2)
                nc.vector.tensor_tensor(m8[:, :], m8[:, :], k.logf[:, :], ALU.min).then_inc(va, 1)
                ve.wait_ge(vb, 1)
                nc.vector.tensor_scalar_add(e8[:, :], e8[:, :], 1.0).then_inc(va, 1)
                ve.wait_ge(vb, 2)
                nc.vector.tensor_scalar(k.logf[:, :], k.logf[:, :], 0.0, None, ALU.min).then_inc(va, 1)
                ve.wait_ge(va, 5)
                nc.vector.tensor_tensor(k.logf[:, :], k.logf[:, :], e8[:, :], ALU.subtract).then_inc(va, 1)
                nc.vector.tensor_scalar(qs[:, :, :], k.fm[:, K_Q:K_Q + 8, T:TT], SCALE, None, ALU.mult).then_inc(qs_done, 1)
                nc.vector.tensor_scalar(k.qf[:, :, :], k.fm[:, K_FQ:K_FQ + 4, T:TT].rearrange("p c b -> p b c"), SCALE, None, ALU.mult)
                nc.vector.tensor_scalar(k.mq[:, :, :], k.fm[:, K_MQ:K_MQ + 4, T:TT].rearrange("p c b -> p b c"), MSCALE, None, ALU.mult)
                ve.wait_ge(row_done, 1)
                nc.vector.tensor_copy(lrow[:, :, :], ps[0][:, 0:NT * H].rearrange("p (t h) -> p t h", t=NT)).then_inc(row_out, 1)
                nc.vector.tensor_copy(k.slrow[:, :], ps[1][0:NB, 0:H]).then_inc(row_out, 1)
                ve.wait_ge(cum_done, 1)
                nc.vector.tensor_scalar(k.ncum[:, :], ps[2][0:H, :], -1.0, None, ALU.mult)
                ve.wait_ge(vc, 1)
                nc.vector.tensor_scalar_add(gsig[:, :], gsig[:, :], 1.0).then_inc(gate_row, 1)
                ve.wait_ge(gate_row, 1)
                nc.vector.reciprocal(gsig[:, :], gsig[:, :]).then_inc(gate_row, 1)
                ve.wait_ge(gate_out, 1)
                nc.vector.tensor_copy(k.grow[:, :, :], ps[3][:, 0:NT * 24].rearrange("p (t h) -> p t h", t=NT))
                nc.vector.tensor_copy(k.sg[:, :, :], ps[4][:, 0:12 * NB].rearrange("p (c b) -> p c b", c=12))
                ve.wait_ge(dup_done, 1)
                ve.wait_ge(pool_zero, 1)
                for q in range(2):
                    src = ps[5][:, q * 32:(q + 1) * 32].rearrange("p (c b) -> p b c", c=4)
                    nc.vector.tensor_copy(k.qd[:, :, :].rearrange("p b (c q) -> p q b c", q=2)[:, q], src)
                    for g in range(2):
                        rows = slice(64 * g, 64 * g + 64)
                        nc.vector.tensor_copy(k.qg[rows, :, 4 * g:4 * g + 4].rearrange("p b (c q) -> p q b c", q=2)[:, q],
                                              src[rows, :, 2 * g:2 * g + 2])
                ve.wait_ge(new_done, 1)
                ve.wait_ge(pool_zero, 2)
                diag = k.diag[0:NB, :].unsqueeze(1).to_broadcast([NB, 4, NB])
                for br in range(3):
                    for j in range(2):
                        sc = ps[6 + j][0:NB, br * 32:(br + 1) * 32].rearrange("p (c b) -> p c b", c=4)
                        nc.vector.tensor_tensor(k.snew[0:NB, br, :, :].rearrange("p b (c j) -> p j c b", j=2)[:, j], sc, diag, ALU.add).then_inc(scl, 1)
                ve.wait_ge(scl, 6)
                ve.wait_ge(row_out, 2)
                nc.vector.tensor_tensor(k.snew[0:NB, 0, :, :], k.snew[0:NB, 0, :, :],
                                        k.slrow[:, :].unsqueeze(1).to_broadcast([NB, NB, H]), ALU.subtract)

            @block.scalar
            def _(sc):
                sc.wait_ge(va, 3)
                nc.scalar.activation(e8[:, :], m8[:, :], ACT.Exp).then_inc(vb, 1)
                nc.scalar.activation(gsig[:, :], k.gate[:, :], ACT.Exp, scale=-1.0).then_inc(vc, 1)
                sc.wait_ge(va, 4)
                nc.scalar.activation(e8[:, :], e8[:, :], ACT.Ln).then_inc(vb, 1)

            @block.gpsimd
            def _(pool):
                nc.gpsimd.memset(k.qg[:, :, :], 0.0).then_inc(pool_zero, 1)
                nc.gpsimd.memset(k.snew[:, :, :, :], NEG).then_inc(pool_zero, 1)
                nc.gpsimd.tensor_scalar(k.fm[:, K_Q:K_MQ, 0:T], k.fm[:, K_Q:K_MQ, 0:T], SCALE, None, ALU.mult)
                nc.gpsimd.tensor_scalar(k.fm[:, K_MQ:K_FK, 0:T], k.fm[:, K_MQ:K_FK, 0:T], MSCALE, None, ALU.mult)

            @block.tensor
            def _(te):
                te.wait_ge(va, 6)
                for t in range(NT):
                    nc.tensor.transpose(ps[0][:, t * H:(t + 1) * H], k.logf[:, t * P:(t + 1) * P], k.ident[0:H, 0:H])
                nc.tensor.transpose(ps[1][0:NB, 0:H], k.logf[:, T:TT], k.ident[0:H, 0:H]).then_inc(row_done, 1)
                te.wait_ge(row_out, 1)
                for t in range(NT):
                    last = nc.tensor.matmul(ps[2][0:H, t * P:T], lrow[:, t, :], k.cum[:, 0:T - t * P],
                                            start=t == 0, stop=t == NT - 1, skip_group_check=True)
                last.then_inc(cum_done, 1)
                te.wait_ge(gate_row, 2)
                te.wait_ge(gsel_in, 16)
                for t in range(NT):
                    nc.tensor.transpose(ps[3][:, t * 24:(t + 1) * 24], gsig[:, t * P:(t + 1) * P], k.ident[0:24, 0:24])
                for n in range(12):
                    last = nc.tensor.matmul(ps[4][:, n * NB:(n + 1) * NB], gsel[:, n * P:(n + 1) * P], gsig[:, T:TT], start=True, stop=True)
                last.then_inc(gate_out, 1)
                te.wait_ge(qs_done, 1)
                for q in range(2):
                    last = nc.tensor.matmul(ps[5][:, q * 32:(q + 1) * 32], k.dup[:, q * P:(q + 1) * P],
                                            qs[:, 0:4, :].rearrange("p c b -> p (c b)"), start=True, stop=True)
                last.then_inc(dup_done, 1)
                for br in range(3):
                    for h in range(H):
                        c, rows = h // 2, slice(64 * (h % 2), 64 * (h % 2) + 64)
                        place = K_FK + c if br == 0 else K_KD + 2 * (br - 1) + h // R
                        last = nc.tensor.matmul(ps[6 + h % 2][0:NB, (br * 4 + c) * NB:(br * 4 + c + 1) * NB], k.fm[rows, place, T:TT],
                                                qs[rows, (4 if br == 0 else 0) + c, :], start=True, stop=True)
                last.then_inc(new_done, 1)


def prompt_compressed(k):
    nc, ps = k.nc, k.ps
    with ExitStack() as cx:
        sb, sem = k.makers(cx)
        w1 = sb("b_w1", [P, CB, P])
        z = sb("b_z", [P, 2, 8])
        ez = sb("b_ez", [P, 2, 8])
        hid = sb("b_hid", [P, 2, 8])
        hv = sb("b_hv", [P, H, 2, NT])
        kp = sb("b_kp", [P, G, 2, NT])
        vbd = sb("b_vbd", [64, H, HD])
        s = sb("b_s", [P, NT, H, 8])
        m, den = sb("b_m", [P, NT, H]), sb("b_den", [P, NT, H])
        pt = w1[0:64, 0:NT, :]
        w_in, zeroed, hid_done, z_done, e_done, h_done, step, hv_done, kp_done, kp_out, v_done, vbd_done = (
            sem("b_" + n) for n in ("w_in", "zeroed", "hid_done", "z_done", "e_done", "h_done", "step", "hv_done",
                                    "kp_done", "kp_out", "v_done", "vbd_done"))
        q_done, s_done, x_step, exp_done, turned, pt_out, o_done, o_out = (
            sem("b_" + n) for n in ("q_done", "s_done", "x_step", "exp_done", "turned", "pt_out", "o_done", "o_out"))
        masked = sem("b_masked")
        hp = ps[0][:, 0:16].rearrange("p (v n) -> p v n", v=2)
        with nc.Block() as block:
            @block.sync
            def _(sp):
                sp.wait_ge(zeroed, 1)
                for v in range(2):
                    if v:
                        sp.wait_ge(hid_done, 1)
                    for half in range(2):
                        rows = slice(64 * half, 64 * half + 64)
                        sp.dma_start(w1[rows, :, rows], k.w_cmp1[0, v]).then_inc(w_in, 16)

            @block.gpsimd
            def _(pool):
                nc.gpsimd.memset(w1[0:64, :, 64:128], 0.0)
                nc.gpsimd.memset(w1[64:128, :, 0:64], 0.0).then_inc(zeroed, 1)
                pool.wait_ge(zeroed, 1)
                nc.gpsimd.memset(hv[:, :, :, :], 0.0).then_inc(zeroed, 1)

            @block.tensor
            def _(te):
                te.wait_ge(zeroed, 1)
                for v in range(2):
                    te.wait_ge(w_in, 32 * (v + 1))
                    rows = k.row[:, :, M_CMP + 128 * v:M_CMP + 128 * v + 128].rearrange("p t (g d) -> p d g t", g=2)
                    for d in range(HD):
                        last = nc.tensor.matmul(hp[:, v], w1[:, d, :], rows[:, d], start=d == 0, stop=d == HD - 1)
                    last.then_inc(hid_done, 1)
                te.wait_ge(h_done, 1)
                for half in range(2):
                    rows = slice(64 * half, 64 * half + 64)
                    last = nc.tensor.matmul(ps[1 + half][:, 0:8], k.w2d[rows, 0, :], hid[rows, 0, :], start=True, stop=True)
                last.then_inc(kp_done, 1)
                te.wait_ge(hv_done, 4)
                nc.tensor.matmul(ps[3][0:64, 0:HD], hv[:, :, :, :].rearrange("p h a t -> p (h a t)"), k.w2d[:, 1, 0:HD],
                                 start=True, stop=True).then_inc(v_done, 1)
                te.wait_ge(kp_out, 2)
                for t in range(NT):
                    for h in range(H):
                        c, rows = h // 2, slice(64 * (h % 2), 64 * (h % 2) + 64)
                        last = nc.tensor.matmul(ps[1 + h % 2][:, (t * 4 + c) * 8:(t * 4 + c + 1) * 8], k.fm[rows, K_Q + c, t * P:(t + 1) * P],
                                                kp[rows, h // R, :, :].rearrange("p a t -> p (a t)"), start=True, stop=True)
                last.then_inc(s_done, 1)
                te.wait_ge(x_step, 5)
                for t in range(NT):
                    last = nc.tensor.transpose(ps[5][0:64, t * P:(t + 1) * P], s[:, t, :, :].rearrange("p h n -> p (h n)"), k.ident)
                last.then_inc(turned, 1)
                te.wait_ge(pt_out, 1)
                te.wait_ge(vbd_done, 1)
                for t in range(NT):
                    if t >= 2:
                        te.wait_ge(o_out, t - 1)
                    nc.tensor.matmul(ps[6 + t % 2][:, :], pt[:, t, :], vbd[:, :, :].rearrange("p h d -> p (h d)"),
                                     start=True, stop=True).then_inc(o_done, 1)

            @block.scalar
            def _(sc):
                sc.wait_ge(z_done, 2)
                nc.scalar.activation(ez[:, :, :], z[:, :, :], ACT.Exp, scale=-1.0).then_inc(e_done, 1)
                sc.wait_ge(x_step, 2)
                nc.scalar.activation(s[:, :, :, :], s[:, :, :, :], ACT.Exp).then_inc(exp_done, 1)

            @block.vector
            def _(ve):
                ve.wait_ge(hid_done, 2)
                for v in range(2):
                    nc.vector.tensor_scalar(z[:, v], hp[:, v], k.pebias[:, v:v + 1], None, ALU.add).then_inc(z_done, 1)
                ve.wait_ge(e_done, 1)
                nc.vector.tensor_scalar_add(ez[:, :, :], ez[:, :, :], 1.0).then_inc(step, 1)
                ve.wait_ge(step, 1)
                nc.vector.reciprocal(ez[:, :, :], ez[:, :, :]).then_inc(step, 1)
                ve.wait_ge(step, 2)
                nc.vector.tensor_tensor(hid[:, :, :], z[:, :, :], ez[:, :, :], ALU.mult).then_inc(h_done, 1)
                ve.wait_ge(h_done, 1)
                ve.wait_ge(zeroed, 2)
                for half in range(2):
                    rows = slice(64 * half, 64 * half + 64)
                    for g in range(G):
                        src = hid[rows, 1, g * NT:(g + 1) * NT].unsqueeze(1).to_broadcast([64, R, NT])
                        nc.vector.tensor_copy(hv[rows, g * R:(g + 1) * R, half, :], src).then_inc(hv_done, 1)
                ve.wait_ge(kp_done, 1)
                for half in range(2):
                    nc.vector.tensor_copy(kp[:, :, half, :], ps[1 + half][:, 0:8].rearrange("p (g t) -> p g t", g=2)).then_inc(kp_out, 1)
                ve.wait_ge(v_done, 1)
                nc.vector.tensor_tensor(vbd[:, :, :], ps[3][0:64, 0:HD].unsqueeze(1).to_broadcast([64, H, HD]),
                                        k.headrow[0:64, :].unsqueeze(2).to_broadcast([64, H, HD]), ALU.mult).then_inc(vbd_done, 1)
                ve.wait_ge(s_done, 1)
                per = lambda a: a.rearrange("p (t n) -> p t n", t=NT).unsqueeze(2).to_broadcast([P, NT, H, 8])
                wide = lambda a: a[:, :, :].unsqueeze(3).to_broadcast([P, NT, H, 8])
                for j in range(2):
                    for t in range(NT):
                        nc.vector.tensor_tensor(s[:, t, :, :].rearrange("p (c j) n -> p j c n", j=2)[:, j],
                                                ps[1 + j][:, t * 32:(t + 1) * 32].rearrange("p (c n) -> p c n", c=4),
                                                k.cneg[:, t * 8:(t + 1) * 8].unsqueeze(1).to_broadcast([P, 4, 8]), ALU.add).then_inc(masked, 1)
                ve.wait_ge(masked, 2 * NT)
                nc.vector.tensor_reduce(m[:, :, :], s[:, :, :, :], AX, ALU.max).then_inc(x_step, 1)
                ve.wait_ge(x_step, 1)
                nc.vector.tensor_tensor(s[:, :, :, :], s[:, :, :, :], wide(m), ALU.subtract).then_inc(x_step, 1)
                ve.wait_ge(exp_done, 1)
                nc.vector.tensor_tensor(s[:, :, :, :], s[:, :, :, :], per(k.c01), ALU.mult).then_inc(x_step, 1)
                ve.wait_ge(x_step, 3)
                nc.vector.tensor_reduce(den[:, :, :], s[:, :, :, :], AX, ALU.add).then_inc(step, 1)
                ve.wait_ge(step, 3)
                nc.vector.tensor_scalar(den[:, :, :], den[:, :, :], TINY, None, ALU.max).then_inc(step, 1)
                ve.wait_ge(step, 4)
                nc.vector.reciprocal(den[:, :, :], den[:, :, :]).then_inc(x_step, 1)
                ve.wait_ge(x_step, 4)
                nc.vector.tensor_tensor(s[:, :, :, :], s[:, :, :, :], wide(den), ALU.mult).then_inc(x_step, 1)
                ve.wait_ge(turned, 1)
                nc.vector.tensor_copy(pt[:, :, :], ps[5][0:64, :].rearrange("p (t n) -> p t n", t=NT)).then_inc(pt_out, 1)
                for t in range(NT):
                    ve.wait_ge(o_done, t + 1)
                    gate = k.grow[:, t, 0:H].unsqueeze(2).to_broadcast([P, H, HD])
                    nc.vector.tensor_tensor(k.o[:, t, 0:BRW].rearrange("p (h d) -> p h d", h=H),
                                            ps[6 + t % 2][:, :].rearrange("p (h d) -> p h d", h=H), gate, ALU.mult).then_inc(o_out, 1)


def sample_compressed(k):
    nc, ps = k.nc, k.ps
    NG = NB * G
    with ExitStack() as cx:
        sb, sem = k.makers(cx)
        s = sb("s_s", [R, NG, NBLK])
        m, den = sb("s_m", [R, NG]), sb("s_den", [R, NG])
        pt = sb("s_pt", [64, NB, 2, R])
        flat = sb("s_flat", [1, NG * NBLK])
        imp, imp2 = sb("s_imp", [NG, NBLK]), sb("s_imp2", [NG, NBLK])
        mx = sb("s_mx", [NG, 16])
        ix = sb("s_ix", [NG, 16], U32)
        ixf = sb("s_ixf", [NG, 16])
        tab_i = sb("s_tab_i", [NG, PAGES], I32)
        tab_f = sb("s_tab_f", [NG, PAGES])
        tab = sb("s_tab", [NG, PAGES, 2])
        hot = sb("s_hot", [NG, 16, NBLK])
        first = sb("s_first", [NG, 16])
        firstT = sb("s_firstT", [16, NG])
        spread = sb("s_spread", [16, NG, 8])
        rowf = sb("s_rowf", [P, NG * 8])
        s_done, x, exp_done, imp_done, imp_out, imp_in, tab_in, t, first_turned, spread_done, rows_done, p_turned, pt_out, o_done, top = (
            sem("s_" + n) for n in ("s_done", "x", "exp_done", "imp_done", "imp_out", "imp_in", "tab_in", "t",
                                    "first_turned", "spread_done", "rows_done", "p_turned", "pt_out", "o_done", "top"))
        with nc.Block() as block:
            @block.sync
            def _(sp):
                for g in range(G):
                    for b in range(NB):
                        sp.dma_start(tab_i[b * G + g:b * G + g + 1, :], k.page_table[b:b + 1, :]).then_inc(tab_in, 16)
                sp.wait_ge(imp_out, 2)
                sp.dma_start(imp[:, :], flat[0:1, :].rearrange("o (n b) -> o n b", n=NG)).then_inc(imp_in, 16)

            @block.tensor
            def _(te):
                for b in range(NB):
                    for g in range(G):
                        n = b * G + g
                        for half in range(2):
                            rows = slice(64 * half, 64 * half + 64)
                            last = nc.tensor.matmul(ps[half][0:R, n * PAGES:(n + 1) * PAGES], k.qd[rows, b, g * R:(g + 1) * R],
                                                    k.kcb[rows, b, g * PAGES:(g + 1) * PAGES], start=True, stop=True)
                last.then_inc(s_done, 1)
                te.wait_ge(x, 7)
                for i in range(2):
                    nc.tensor.matmul(ps[2 + i][0:1, :], k.ones[0:R, 0:1], s[:, 8 * i:8 * i + 8, :].rearrange("p n b -> p (n b)"),
                                     start=True, stop=True).then_inc(imp_done, 1)
                for b in range(NB):
                    for half in range(2):
                        src = s[:, 2 * b:2 * b + 2, :].rearrange("p g (n a) -> p a (g n)", a=2)[:, half]
                        last = nc.tensor.transpose(ps[4][0:64, (b * 2 + half) * R:(b * 2 + half + 1) * R], src, k.ident[0:R, 0:R])
                last.then_inc(p_turned, 1)
                te.wait_ge(pt_out, 1)
                for b in range(NB):
                    for g in range(G):
                        rows = slice(32 * g, 32 * g + 32)
                        for half in range(2):
                            last = nc.tensor.matmul(ps[5 + g][0:64, b * R:(b + 1) * R], k.vcb[rows, b, 64 * half:64 * half + 64],
                                                    pt[rows, b, half, :], start=half == 0, stop=half == 1, skip_group_check=True)
                last.then_inc(o_done, 1)
                te.wait_ge(t, 4)
                nc.tensor.transpose(ps[2][0:16, 0:NG], first[:, :], k.ident[0:NG, 0:NG]).then_inc(first_turned, 1)
                te.wait_ge(spread_done, 1)
                nc.tensor.matmul(ps[3][:, 0:NG * 8], k.epart[0:16, :], spread[:, :, :].rearrange("p n j -> p (n j)"),
                                 start=True, stop=True).then_inc(rows_done, 1)

            @block.scalar
            def _(sc):
                sc.wait_ge(x, 4)
                nc.scalar.activation(s[:, :, :], s[:, :, :], ACT.Exp).then_inc(exp_done, 1)

            @block.gpsimd
            def _(pool):
                pass

            @block.vector
            def _(ve):
                wide = lambda a: a[:, :].unsqueeze(2).to_broadcast([R, NG, NBLK])
                ve.wait_ge(s_done, 1)
                for half in range(2):
                    nc.vector.tensor_copy(s[:, :, :].rearrange("p n (b a) -> p a n b", a=2)[:, half],
                                          ps[half][0:R, :].rearrange("p (n b) -> p n b", n=NG)).then_inc(x, 1)
                ve.wait_ge(x, 2)
                nc.vector.tensor_reduce(m[:, :], s[:, :, :], AX, ALU.max).then_inc(x, 1)
                ve.wait_ge(x, 3)
                nc.vector.tensor_tensor(s[:, :, :], s[:, :, :], wide(m), ALU.subtract).then_inc(x, 1)
                ve.wait_ge(exp_done, 1)
                nc.vector.tensor_reduce(den[:, :], s[:, :, :], AX, ALU.add).then_inc(x, 1)
                ve.wait_ge(x, 5)
                nc.vector.reciprocal(den[:, :], den[:, :]).then_inc(x, 1)
                ve.wait_ge(x, 6)
                nc.vector.tensor_tensor(s[:, :, :], s[:, :, :], wide(den), ALU.mult).then_inc(x, 1)
                ve.wait_ge(imp_done, 2)
                for i in range(2):
                    nc.vector.tensor_copy(flat[0:1, 512 * i:512 * i + 512], ps[2 + i][0:1, :]).then_inc(imp_out, 1)
                ve.wait_ge(tab_in, 16 * NG)
                nc.vector.tensor_copy(tab_f[:, :], tab_i[:, :]).then_inc(t, 1)
                ve.wait_ge(t, 1)
                nc.vector.tensor_scalar(tab_f[:, :], tab_f[:, :], float(P), None, ALU.mult).then_inc(t, 1)
                ve.wait_ge(t, 2)
                nc.vector.tensor_tensor(tab[:, :, :], tab_f[:, :].unsqueeze(2).to_broadcast([NG, PAGES, 2]),
                                        k.blkrow[0:NG, :].rearrange("p (n a) -> p n a", a=2), ALU.add).then_inc(t, 1)
                ve.wait_ge(p_turned, 1)
                nc.vector.tensor_copy(pt[:, :, :, :], ps[4][0:64, 0:NB * 2 * R].rearrange("p (b a r) -> p b a r", b=NB, a=2)).then_inc(pt_out, 1)
                ve.wait_ge(imp_in, 16)
                nc.vector.max(out=mx[:, 0:8], in_=imp[:, :]).then_inc(top, 1)
                ve.wait_ge(top, 1)
                nc.vector.max_index(out=ix[:, 0:8], in_max=mx[:, 0:8], in_values=imp[:, :]).then_inc(top, 1)
                nc.vector.match_replace(out=imp2[:, :], in_to_replace=mx[:, 0:8], in_values=imp[:, :], imm_value=NEG).then_inc(top, 1)
                ve.wait_ge(top, 3)
                nc.vector.max(out=mx[:, 8:16], in_=imp2[:, :]).then_inc(top, 1)
                ve.wait_ge(top, 4)
                nc.vector.max_index(out=ix[:, 8:16], in_max=mx[:, 8:16], in_values=imp2[:, :]).then_inc(top, 1)
                ve.wait_ge(top, 5)
                nc.vector.tensor_copy(ixf[:, :], ix[:, :]).then_inc(top, 1)
                ve.wait_ge(top, 6)
                nc.vector.tensor_tensor(hot[:, :, :], ixf[:, :].unsqueeze(2).to_broadcast([NG, 16, NBLK]),
                                        k.blk[0:NG, :].unsqueeze(1).to_broadcast([NG, 16, NBLK]), ALU.is_equal).then_inc(top, 1)
                ve.wait_ge(top, 7)
                ve.wait_ge(t, 3)
                nc.vector.tensor_tensor(hot[:, :, :], hot[:, :, :],
                                        tab[:, :, :].rearrange("p n a -> p (n a)").unsqueeze(1).to_broadcast([NG, 16, NBLK]), ALU.mult).then_inc(top, 1)
                ve.wait_ge(top, 8)
                nc.vector.tensor_reduce(first[:, :], hot[:, :, :], AX, ALU.add).then_inc(t, 1)
                ve.wait_ge(first_turned, 1)
                nc.vector.tensor_copy(firstT[:, :], ps[2][0:16, 0:NG]).then_inc(top, 1)
                ve.wait_ge(top, 9)
                nc.vector.tensor_tensor(spread[:, :, :], firstT[:, :].unsqueeze(2).to_broadcast([16, NG, 8]),
                                        k.jmask[0:16, :].unsqueeze(1).to_broadcast([16, NG, 8]), ALU.mult).then_inc(spread_done, 1)
                ve.wait_ge(rows_done, 1)
                nc.vector.tensor_scalar(rowf[:, :], ps[3][:, 0:NG * 8], k.lcol, None, ALU.add).then_inc(top, 1)
                ve.wait_ge(top, 10)
                nc.vector.tensor_copy(k.selrow[:, :], rowf[:, :])
                ve.wait_ge(o_done, 1)
                for g in range(G):
                    nc.vector.tensor_copy(k.oc[:, :, g * R:(g + 1) * R], ps[5 + g][0:64, 0:NB * R].rearrange("p (b r) -> p b r", b=NB))


def attention(k, name, pairs, units, keys, vwide, loops, addresses, mask, forget_sums, place):
    nc, ps, wait = k.nc, k.ps, k.wait
    U = len(units)
    with ExitStack() as cx:
        sb, sem = k.makers(cx)
        q, kk = ([sb(f"{name}_{n}{i}", [P, T]) for i in range(2)] for n in "qk")
        hs = [sb(f"{name}_hs{i}", [H, 2, P]) for i in range(2)]
        hsel = sb(name + "_hsel", [H, H, P])
        e = [sb(f"{name}_e{i}", [P, T]) for i in range(4)]
        pt = [sb(f"{name}_pt{i}", [P, T]) for i in range(2)]
        nm, su, rc = sb(name + "_nm", [P, U]), sb(name + "_su", [P, U]), sb(name + "_rc", [P, U])
        staged, s_done, m_done, e_done, turned, pt_out, o_done, rc_done, o_out, gr_done = (
            sem(name + "_" + n) for n in ("staged", "s_done", "m_done", "e_done", "turned", "pt_out", "o_done", "rc_done", "o_out", "gr_done"))
        masked = sem(name + "_masked")
        score_bank = [ps[0], ps[1], ps[6], ps[7]]
        AHEAD = 2
        kw = keys(NT - 1)
        STAGES = 3 if forget_sums else 2

        def every(engine, body):
            def nest(idx, n, rest, final):
                if not rest:
                    for turn in range(2):
                        body(n * 2 + turn, idx + [turn], final and turn == 1)
                elif final:
                    if rest[0] > 1:
                        with engine.Fori(0, rest[0] - 1) as i:
                            nest(idx + [i], n * rest[0] + i if idx else i, rest[1:], False)
                    nest(idx + [rest[0] - 1], n * rest[0] + rest[0] - 1, rest[1:], True)
                else:
                    with engine.Fori(0, rest[0]) as i:
                        nest(idx + [i], n * rest[0] + i, rest[1:], False)
            nest([], 0, list(loops), True)

        hsel_in = sem(name + "_hsel_in")
        k.prime(pt_out, o_done, o_out)
        k.prime(e_done, turned, by=4)
        k.prime(s_done, by=U + 1)
        with nc.Block() as block:
            @block.sync
            def _(sp):
                if forget_sums:
                    sp.dma_start(hsel[:, :, :], k.selectors[0:H, 12 * P:].rearrange("k (h n) -> k h n", h=H)).then_inc(hsel_in, 16)

            @block.gpsimd
            def _(pool):
                def body(it, idx, final):
                    qc, kc, _, _ = addresses(idx)
                    turn = idx[-1]
                    wait(pool, s_done, it * U - U)
                    nc.gpsimd.tensor_copy(q[turn][:, :].unsqueeze(1), k.fm[:, bass.ds(qc, 1), 0:T]).then_inc(staged, 1)
                    src = k.fm if kc[0] == "fm" else k.mkT
                    nc.gpsimd.tensor_copy(kk[turn][:, 0:kw].unsqueeze(1), src[:, bass.ds(kc[1], 1), 0:kw]).then_inc(staged, 1)
                    if forget_sums:
                        nc.gpsimd.tensor_copy(hs[turn][:, :, :], hsel[:, bass.ds(it * 2, 2), :]).then_inc(staged, 1)
                if forget_sums:
                    wait(pool, hsel_in, 16)
                every(pool, body)

            @block.tensor
            def _(te):
                def scores(it, turn, u):
                    rows, t = units[u]
                    n = keys(t)
                    if u == 0:
                        wait(te, staged, it * STAGES + STAGES)
                    wait(te, e_done, it * U + u - 3)
                    parts = [(q[turn][rows, t * P:(t + 1) * P], kk[turn][rows, 0:n])]
                    if forget_sums:
                        parts.append((hs[turn][:, rows.start // 64, :], k.ncum[:, 0:n]))
                    for i, (left, right) in enumerate(parts):
                        last = nc.tensor.matmul(score_bank[u % 4][:, 0:n], left, right, start=i == 0, stop=i == len(parts) - 1)
                    last.then_inc(s_done, 1)

                def body(it, idx, final):
                    _, _, vc, vstep = addresses(idx)

                    def values(u):
                        rows, t = units[u]
                        n = keys(t)
                        wait(te, e_done, it * U + u + 1)
                        wait(te, pt_out, it * U + u - 1) if u else wait(te, pt_out, it * U)
                        for j in range(n // P):
                            last = nc.tensor.transpose(ps[2 + u % 2][:, j * P:(j + 1) * P], e[u % 4][:, j * P:(j + 1) * P], k.ident)
                        last.then_inc(turned, 1)

                    def sums(u):
                        rows, t = units[u]
                        n = keys(t)
                        wait(te, pt_out, it * U + u + 1)
                        wait(te, o_out, it * U + u - 1) if u else wait(te, o_out, it * U)
                        src = k.mrow if kc_mem else k.row
                        for j in range(n // P):
                            last = nc.tensor.matmul(ps[4 + u % 2][:, 0:vwide], pt[u % 2][:, j * P:(j + 1) * P],
                                                    src[:, j, bass.ds(vc + vstep * (rows.start // 64), vwide)],
                                                    start=j == 0, stop=j == n // P - 1)
                        last.then_inc(o_done, 1)

                    kc_mem = addresses(idx)[1][0] != "fm"
                    for u in range(U):
                        if u + AHEAD < U:
                            scores(it, idx[-1], u + AHEAD)
                        elif not final:
                            scores(it + 1, 1 - idx[-1], u + AHEAD - U)
                        values(u)
                        if u:
                            sums(u - 1)
                    sums(U - 1)
                for u in range(AHEAD):
                    scores(0, 0, u)
                every(te, body)

            @block.vector
            def _(ve):
                def mask_later(it, u):
                    rows, t = units[u]
                    wait(ve, s_done, it * U + u + 1)
                    if mask:
                        own = score_bank[u % 4][:, t * P:keys(t)]
                        nc.vector.tensor_tensor(own, own, k.causal, ALU.add).then_inc(masked, 1)

                def maximum(it, u):
                    rows, t = units[u]
                    if mask:
                        wait(ve, masked, it * U + u + 1)
                    nc.vector.tensor_reduce(nm[:, u:u + 1], score_bank[u % 4][:, 0:keys(t)], AX, ALU.max, negate=True).then_inc(m_done, 1)

                def body(it, idx, final):
                    def place_of(u):
                        return place(idx, units[u][0].start // 64)

                    def scale_out(u):
                        t = units[u][1]
                        wait(ve, o_done, it * U + u + 1)
                        col, gate, add = place_of(u)
                        dst, src = k.o[:, t, bass.ds(col, vwide)], ps[4 + u % 2][:, 0:vwide]
                        if add:
                            nc.vector.scalar_tensor_tensor(out=dst, in0=src, scalar=rc[:, u:u + 1], in1=dst, op0=ALU.mult, op1=ALU.add).then_inc(o_out, 1)
                        else:
                            nc.vector.tensor_scalar(dst, src, rc[:, u:u + 1], None, ALU.mult).then_inc(o_out, 1)

                    for u in range(U):
                        t = units[u][1]
                        after = (it, u + AHEAD) if u + AHEAD < U else (it + 1, u + AHEAD - U) if not final else None
                        gate = place_of(u)[1]
                        if after:
                            mask_later(*after)
                        wait(ve, e_done, it * U + u + 1)
                        nc.vector.reciprocal(rc[:, u:u + 1], su[:, u:u + 1]).then_inc(rc_done, 1)
                        if after:
                            maximum(*after)
                        wait(ve, rc_done, it * U + u + 1)
                        if gate is not None:
                            nc.vector.tensor_tensor(rc[:, u:u + 1], rc[:, u:u + 1], k.grow[:, t, bass.ds(gate, 1)], ALU.mult).then_inc(gr_done, 1)
                        wait(ve, turned, it * U + u + 1)
                        wait(ve, o_done, it * U + u - 1) if u else wait(ve, o_done, it * U)
                        nc.vector.tensor_copy(pt[u % 2][:, 0:keys(t)], ps[2 + u % 2][:, 0:keys(t)]).then_inc(pt_out, 1)
                        if gate is not None:
                            wait(ve, gr_done, it * U + u + 1)
                        if u:
                            scale_out(u - 1)
                    scale_out(U - 1)

                for u in range(AHEAD):
                    mask_later(0, u)
                    maximum(0, u)
                every(ve, body)

            @block.scalar
            def _(sc):
                def body(it, idx, final):
                    for u, (rows, t) in enumerate(units):
                        wait(sc, m_done, it * U + u + 1)
                        wait(sc, turned, it * U + u - 3)
                        nc.scalar.activation(e[u % 4][:, 0:keys(t)], score_bank[u % 4][:, 0:keys(t)], ACT.Exp, bias=nm[:, u:u + 1],
                                             accum_out=su[:, u:u + 1]).then_inc(e_done, 1)
                every(sc, body)


def prompt(k):
    two = [(slice(64 * j, 64 * j + 64), t) for j in range(2) for t in (0, 3, 1, 2)]
    one = [(slice(0, P), t) for t in range(NT)]
    causal = lambda t: (t + 1) * P
    chunk = lambda i: i[0] * 2 + i[1]
    attention(k, "f", None, two, causal, HD, [2],
              lambda i: (K_FQ + chunk(i), ("fm", K_FK + chunk(i)), M_FV + chunk(i) * P, HD), True, True,
              lambda i, j: (BRW + chunk(i) * P + j * HD, None, False))
    attention(k, "m", None, one, lambda t: NM, P, [2],
              lambda i: (K_MQ + chunk(i), ("mem", chunk(i)), BRW + chunk(i) * P, 0), False, False,
              lambda i, j: (2 * BRW + chunk(i) * P, None, False))
    attention(k, "w", None, two, causal, HD, [2, G],
              lambda i: (K_Q + i[1] * 2 + i[2], ("fm", K_KD + i[0] * 2 + i[1]), M_SLC + P + i[0] * 256 + i[1] * HD, 0),
              True, False,
              lambda i, j: (i[1] * 256 + i[2] * P + j * HD, (i[0] + 1) * 8 + i[1] * 4 + i[2] * 2 + j, True))


def sample(k):
    nc, ps, wait = k.nc, k.ps, k.wait
    KR = 4
    SLOTS = 4 * KR
    GROUPS = SLOTS // KR
    ROUNDS = PAGES // SLOTS
    NSLC, NWIN, NMEM = 16, WIN // P, NM // P
    FT, ST, WT = PAGES + 1, NSLC // 2 + 1, NWIN + 1
    small = [("slc", n) for n in range(4)] + [("win", 0)]
    TURNS = len(small)
    SUMS = PAGES // KR + 1
    NS = H + H + H + MH
    with ExitStack() as cx:
        sb, sem = k.makers(cx)
        kpage = sb("d_kpage", [P, SLOTS, BRW])
        vpage = sb("d_vpage", [P, SLOTS, BRW])
        slc = sb("d_slc", [P, NSLC, 256])
        win = sb("d_win", [P, NWIN, 256])
        mem = sb("d_mem", [P, NMEM, 2 * BRW])
        kT = [sb(f"d_kT{i}", [P, 4 * P]) for i in range(2)]
        product = [sb(f"d_product{i}", [P, KR, BRW]) for i in range(2)]
        qdiag = sb("d_qdiag", [P, 4, P])
        qrow = sb("d_qrow", [P, 2, BRW])
        fvs, mvs = sb("d_fvs", [H, BRW]), sb("d_mvs", [MH, BRW])
        svs = sb("d_svs", [R, 2, G * HD])
        sf = sb("d_sf", [P, FT, H])
        pf = sb("d_pf", [P, FT, H])
        ss = sb("d_ss", [P, ST + WT, H])
        sm = sb("d_sm", [P, NMEM, MH])
        mx, den, rden = sb("d_mx", [P, NS]), sb("d_den", [P, NS]), sb("d_rden", [P, NS])
        col, dia = sb("d_col", [NS, 1]), sb("d_dia", [NS, NS])

        k_in = [sem(f"d_k_in{i}") for i in range(SLOTS)]
        v_in = [sem(f"d_v_in{i}") for i in range(SLOTS)]
        k_free, v_free = ([sem(f"d_{n}{i}") for i in range(GROUPS)] for n in ("k_free", "v_free"))
        slc_in = k.slc_in
        win_in, mem_in, small_free = (sem("d_" + n) for n in ("win_in", "mem_in", "small_free"))
        turned, kT_out, used, small_out = (sem("d_" + n) for n in ("turned", "kT_out", "used", "small_out"))
        mx_done, mx_turned, col_done, dia_done, mx_spread, shifted, exp_done = (
            sem("d_" + n) for n in ("mx_done", "mx_turned", "col_done", "dia_done", "mx_spread", "shifted", "exp_done"))
        den_done, den_spread, rden_done, p_done, pf_done, of_out, os_out, zero = (
            sem("d_" + n) for n in ("den_done", "den_spread", "rden_done", "p_done", "pf_done", "of_out", "os_out", "zero"))
        late_masked, new_in, sc_out = sem("d_late_masked"), sem("d_new_in"), sem("d_sc_out")
        qdiag_done, q_spread, q_in, summed, mem_product, sums_turned, placed = (
            sem("d_" + n) for n in ("qdiag_done", "q_spread", "q_in", "summed", "mem_product", "sums_turned", "placed"))
        turn_bank, small_bank, spread_bank, mv_bank, stat_bank, sv_bank, fv_bank = ps[0:2], ps[2], ps[3], ps[4], ps[5], ps[6], ps[7]
        stat_max, stat_spread, stat_den = stat_bank[0:NS, 0:P], stat_bank[:, P:P + NS], stat_bank[:, 2 * P:2 * P + NS]
        of_turned, ow_turned = stat_bank[:, 3 * P:3 * P + 8], stat_bank[:, 3 * P + 8:3 * P + 16]
        om_turned = stat_bank[:, 3 * P + 16:3 * P + 16 + MH]

        k.prime(*k_free, *v_free, q_spread, q_in, sums_turned, placed, small_free, kT_out, used, small_out, of_out, os_out, pf_done)
        with nc.Block() as block:
            def load_pages(queue, b, st, which, groups=range(GROUPS)):
                buf, arrive, free = ((kpage, k_in, k_free), (vpage, v_in, v_free))[which]
                for group in groups:
                    wait(queue, free[group], b * ROUNDS + st)
                    for slot in range(group * KR, group * KR + KR):
                        pg = queue.value_load(k.table[0:1, bass.ds(b * PAGES + st * SLOTS + slot, 1)], min_val=0, max_val=POOL - 1)
                        queue.dma_start(buf[:, slot, :].unsqueeze(1),
                                        k.cache_fox[bass.ds(pg, 1), :, which, :].rearrange("a p n -> p a n")).then_inc(arrive[slot], 16)

            @block.sync
            def _(sp):
                with sp.Fori(0, NB) as b:
                    load_pages(sp, b, 0, 0)
                    load_pages(sp, b, 1, 0, range(0, 2))
                    wait(sp, small_free, b)
                    for t in range(NWIN):
                        sp.dma_start(win[:, t, :].unsqueeze(1), k.state_win[bass.ds(b, 1), t * P:(t + 1) * P, :].rearrange("a p n -> p a n")).then_inc(win_in, 16)
                    for t in range(NMEM):
                        sp.dma_start(mem[:, t, :].unsqueeze(1), k.cache_mem[bass.ds(b, 1), t * P:(t + 1) * P, :].rearrange("a p n -> p a n")).then_inc(mem_in, 16)
                    load_pages(sp, b, 1, 0, range(2, GROUPS))

            @block.gpsimd
            def _(pool):
                nc.gpsimd.memset(k.ow[:, :, :, :], 0.0).then_inc(zero, 1)
                for b in range(NB):
                    if b:
                        wait(pool, small_free, b)
                    for n in range(NSLC):
                        at = b * NSLC + n
                        nc.gpsimd.indirect_dma_start(
                            out=slc[:, n, :], out_offset=None, in_=k.cache_slc,
                            in_offset=bass.IndirectOffsetOnAxis(ap=k.selrow[:, at:at + 1].bitcast(U32), axis=0),
                            bounds_check=POOL * P - 1, oob_is_err=False).then_inc(slc_in, 16)

            @block.tensor
            def _(te):
                def spread_queries(b):
                    for i in range(2):
                        wait(te, qdiag_done, b * 2 + i + 1)
                        wait(te, q_in, b * 2 + i)
                        nc.tensor.matmul(spread_bank[:, :], k.ones, qdiag[:, :, :].rearrange("p c n -> p (c n)"),
                                         start=True, stop=True).then_inc(q_spread, 1)

                def page_values(b, first, end):
                    if first == 0:
                        wait(te, pf_done, b + 1)
                        wait(te, of_out, b)
                    for page in range(first, end):
                        st, slot = page // SLOTS, page % SLOTS
                        wait(te, v_in[slot], (b * ROUNDS + st) * 16 + 16)
                        last = nc.tensor.matmul(fv_bank[0:H, :], pf[:, page, :], vpage[:, slot, :],
                                                start=page == 0, stop=page == PAGES - 1)
                        if page == 0:
                            nc.tensor.matmul(fv_bank[0:H, :], pf[0:NB, PAGES, :], k.srow[:, M_FV:M_FV + BRW], start=False, stop=False)
                        if slot % KR == KR - 1:
                            last.then_inc(v_free[slot // KR], 1)

                def small_keys(b):
                    wait(te, slc_in, b * (16 * NSLC) + 16 * NSLC)
                    wait(te, win_in, b * (16 * NWIN) + 16 * NWIN)
                    wait(te, small_out, b * 2)

                    def turn(no):
                        kind, n = small[no]
                        wait(te, kT_out, b * TURNS + max(no - 1, 0))
                        for i in range(4):
                            src = {"slc": slc[:, (4 * n + i) % NSLC, 0:P], "win": win[:, i, 0:P]}[kind]
                            last = nc.tensor.transpose(turn_bank[no % 2][:, i * P:(i + 1) * P], src, k.ident)
                        last.then_inc(turned, 1)

                    def score(no):
                        kind, n = small[no]
                        wait(te, kT_out, b * TURNS + no + 1)
                        for i in range(4):
                            if kind == "slc":
                                tile = 4 * n + i
                                out, right = small_bank[:, tile * R:(tile + 1) * R], k.qg[:, bass.ds(b, 1), (tile // 8) * R:(tile // 8 + 1) * R]
                            else:
                                out, right = small_bank[:, 64 + i * H:64 + (i + 1) * H], k.qg[:, bass.ds(b, 1), :]
                            last = nc.tensor.matmul(out, kT[no % 2][:, i * P:(i + 1) * P], right.rearrange("p a n -> p (a n)"), start=True, stop=True)
                        last.then_inc(used, 1)

                    turn(0)
                    for no in range(len(small)):
                        if no + 1 < len(small):
                            turn(no + 1)
                        score(no)

                def softmax_step(b, i):
                    if i == 0:
                        wait(te, mx_done, b * 4 + 4)
                        nc.tensor.transpose(stat_max, mx[:, :], k.ident).then_inc(mx_turned, 1)
                    elif i == 1:
                        wait(te, dia_done, b + 1)
                        nc.tensor.matmul(stat_spread, k.ones[0:NS, :], dia[:, :], start=True, stop=True).then_inc(mx_spread, 1)
                    else:
                        wait(te, den_done, b * 4 + 4)
                        nc.tensor.matmul(stat_den, k.ones, den[:, :], start=True, stop=True).then_inc(den_spread, 1)

                def small_values(b):
                    wait(te, p_done, b * 3 + 3)
                    wait(te, os_out, b * 2)
                    parts = []
                    for g in range(G):
                        heads, feats = slice(g * R, (g + 1) * R), slice(g * HD, (g + 1) * HD)
                        late = lambda at: slice(at + g * HD, at + (g + 1) * HD)
                        for n in range(8):
                            parts.append((feats, ss[:, n, heads], slc[:, g * 8 + n, late(P)]))
                        parts.append((feats, ss[0:NB, ST - 1, heads], k.srow[:, late(M_SLC + P)]))
                        for n in range(NWIN):
                            parts.append((late(P), ss[:, ST + n, heads], win[:, n, late(P)]))
                        parts.append((late(P), ss[0:NB, ST + WT - 1, heads], k.srow[:, late(M_WIN + P)]))
                    for i, (cols, left, right) in enumerate(parts):
                        nc.tensor.matmul(sv_bank[0:R, cols], left, right, start=i == 0, stop=i == len(parts) - 1, skip_group_check=True)
                    for n in range(NMEM):
                        last = nc.tensor.matmul(mv_bank[0:MH, :], sm[:, n, :], mem[:, n, BRW:2 * BRW], start=n == 0, stop=n == NMEM - 1)
                    last.then_inc(small_free, 1)

                def turn_sums(b):
                    wait(te, of_out, b + 1)
                    wait(te, os_out, b * 2 + 2)
                    wait(te, placed, b * 5)
                    for c in range(4):
                        nc.tensor.matmul(of_turned[:, 2 * c:2 * c + 2], fvs[:, c * P:(c + 1) * P], k.ident[0:H, 2 * c:2 * c + 2], start=True, stop=True)
                    for br in range(2):
                        nc.tensor.matmul(ow_turned[:, br * R:(br + 1) * R], svs[:, br, :], k.ident[0:R, 0:R], start=True, stop=True)
                    for c in range(MH):
                        last = nc.tensor.matmul(om_turned[:, c:c + 1], mvs[:, c * P:(c + 1) * P], k.ident[0:MH, c:c + 1], start=True, stop=True)
                    last.then_inc(sums_turned, 1)

                def step(b, before=2):
                    spread_queries(b)
                    if before:
                        small_values(b - 1)
                        if before > 1:
                            turn_sums(b - 2)
                        page_values(b - 1, 0, PAGES - 8)
                    small_keys(b)
                    for i in range(3):
                        if before:
                            page_values(b - 1, PAGES - (8, 4, 2)[i], PAGES - (4, 2, 0)[i])
                        softmax_step(b, i)

                step(0, 0)
                step(1, 1)
                with te.Fori(2, NB) as b:
                    step(b)
                small_values(NB - 1)
                turn_sums(NB - 2)
                page_values(NB - 1, 0, PAGES)
                turn_sums(NB - 1)

            @block.scalar
            def _(sc):
                with sc.Fori(0, NB) as b:
                    load_pages(sc, b, 0, 1, range(0, 1))
                    for no in range(TURNS):
                        wait(sc, turned, b * TURNS + no + 1)
                        wait(sc, used, b * TURNS + max(no - 1, 0))
                        nc.scalar.activation(kT[no % 2][:, :], turn_bank[no % 2][:, :], ACT.Copy).then_inc(kT_out, 1)
                    load_pages(sc, b, 0, 1, range(1, 2))
                    for i, s in enumerate((ss, sm, sf)):
                        wait(sc, shifted, b * 4 + (2, 3, 4)[i])
                        nc.scalar.activation(s[:, :, :], s[:, :, :], ACT.Exp).then_inc(exp_done, 1)
                    load_pages(sc, b, 0, 1, range(2, GROUPS))
                    load_pages(sc, b, 1, 1)

            @block.vector
            def _(ve):
                kinds = [(ss, slice(0, ST), H, H), (ss, slice(ST, ST + WT), H, 2 * H), (sm, slice(0, NMEM), MH, 3 * H),
                         (sf, slice(0, FT), H, 0)]

                def spread(cols, tiles, heads, at):
                    return cols[:, at:at + heads].unsqueeze(1).to_broadcast([P, tiles.stop - tiles.start, heads])

                def spread_queries(b):
                    for i, q in enumerate((k.qf, k.mq)):
                        wait(ve, q_spread, b * 2 + i)
                        nc.vector.tensor_tensor(qdiag[:, :, :], k.ident.unsqueeze(1).to_broadcast([P, 4, P]),
                                                q[:, bass.ds(b, 1), :].rearrange("p a c -> p (a c)").unsqueeze(2).to_broadcast([P, 4, P]),
                                                ALU.mult).then_inc(qdiag_done, 1)
                        wait(ve, q_spread, b * 2 + i + 1)
                        nc.vector.tensor_copy(qrow[:, i, :], spread_bank[:, :]).then_inc(q_in, 1)

                def page_scores(b, before):
                    def multiply(n):
                        st, group = n // GROUPS, n % GROUPS
                        for slot in range(group * KR, (group + 1) * KR):
                            wait(ve, k_in[slot], (b * ROUNDS + st) * 16 + 16)
                        if n >= 2:
                            wait(ve, summed, b * SUMS + n - 1)
                        nc.vector.tensor_tensor(product[n % 2][:, :, :], kpage[:, group * KR:(group + 1) * KR, :],
                                                qrow[:, 0, :].unsqueeze(1).to_broadcast([P, KR, BRW]), ALU.mult).then_inc(k_free[group], 1)

                    def add_up(n):
                        st, group = n // GROUPS, n % GROUPS
                        wait(ve, k_free[group], b * ROUNDS + st + 1)
                        nc.vector.tensor_reduce(sf[:, n * KR:(n + 1) * KR, :], product[n % 2][:, :, :].rearrange("p n (h d) -> p n h d", h=H),
                                                AX, ALU.add).then_inc(summed, 1)

                    wait(ve, q_in, b * 2 + 2)
                    for n in range(SUMS - 1):
                        multiply(n)
                        if n:
                            add_up(n - 1)
                        if n == 3 and before:
                            small_sums(b - 1)
                            if before > 1:
                                place_sums(b - 2)
                    wait(ve, mem_in, b * (16 * NMEM) + 16 * NMEM)
                    wait(ve, summed, b * SUMS + SUMS - 2)
                    m = (SUMS - 1) % 2
                    nc.vector.tensor_tensor(product[m][:, 0:NMEM, :], mem[:, :, 0:BRW], qrow[:, 1, :].unsqueeze(1).to_broadcast([P, NMEM, BRW]),
                                            ALU.mult).then_inc(mem_product, 1)
                    add_up(SUMS - 2)
                    wait(ve, mem_product, b + 1)
                    nc.vector.tensor_reduce(sm[:, :, :], product[m][:, 0:NMEM, :].rearrange("p n (h d) -> p n h d", h=MH), AX, ALU.add).then_inc(summed, 1)
                    wait(ve, summed, b * SUMS + SUMS)
                    nc.vector.tensor_tensor(sf[:, 0:PAGES, :], sf[:, 0:PAGES, :], k.rpast[:, bass.ds(b * PAGES, PAGES), :], ALU.add).then_inc(sc_out, 1)

                def scores(b, before):
                    page_scores(b, before)
                    nc.vector.tensor_copy(sf[:, FT - 1, :].unsqueeze(1), k.snew[:, 0, bass.ds(b, 1), :]).then_inc(new_in, 1)
                    nc.vector.tensor_copy(ss[:, ST - 1, :].unsqueeze(1), k.snew[:, 1, bass.ds(b, 1), :]).then_inc(new_in, 1)
                    nc.vector.tensor_copy(ss[:, ST + WT - 1, :].unsqueeze(1), k.snew[:, 2, bass.ds(b, 1), :]).then_inc(new_in, 1)
                    wait(ve, used, b * TURNS + TURNS)
                    nc.vector.tensor_copy(ss[:, 0:8, :].rearrange("p j (g r) -> p g j r", g=G),
                                          small_bank[:, 0:64].rearrange("p (g j r) -> p g j r", g=G, r=R)).then_inc(small_out, 1)
                    nc.vector.tensor_copy(ss[:, ST:ST + NWIN, :], small_bank[:, 64:96].rearrange("p (n h) -> p n h", h=H)).then_inc(small_out, 1)
                    wait(ve, small_out, b * 2 + 2)
                    nc.vector.tensor_scalar(ss[:, 7, :], ss[:, 7, :], k.newneg, None, ALU.add).then_inc(late_masked, 1)
                    wait(ve, late_masked, b + 1)

                def softmax(b):
                    wait(ve, new_in, b * 3 + 3)
                    wait(ve, sc_out, b + 1)
                    for s, tiles, heads, at in kinds:
                        nc.vector.tensor_reduce(mx[:, at:at + heads], s[:, tiles, :].rearrange("p n h -> p h n"), AX, ALU.max).then_inc(mx_done, 1)
                    wait(ve, mx_turned, b + 1)
                    nc.vector.tensor_reduce(col[:, :], stat_max, AX, ALU.max).then_inc(col_done, 1)
                    wait(ve, col_done, b + 1)
                    nc.vector.tensor_scalar(dia[:, :], k.ident[0:NS, 0:NS], col[:, 0:1], None, ALU.mult).then_inc(dia_done, 1)
                    wait(ve, mx_spread, b + 1)
                    for s, tiles, heads, at in kinds:
                        nc.vector.tensor_tensor(s[:, tiles, :], s[:, tiles, :], spread(stat_spread, tiles, heads, at), ALU.subtract).then_inc(shifted, 1)
                    wait(ve, exp_done, b * 3 + 3)
                    for s, tiles, heads, at in kinds:
                        nc.vector.tensor_reduce(den[:, at:at + heads], s[:, tiles, :].rearrange("p n h -> p h n"), AX, ALU.add).then_inc(den_done, 1)
                    wait(ve, den_spread, b + 1)
                    nc.vector.reciprocal(rden[:, :], stat_den).then_inc(rden_done, 1)
                    wait(ve, rden_done, b + 1)
                    for s, tiles, heads, at in kinds[:3]:
                        nc.vector.tensor_tensor(s[:, tiles, :], s[:, tiles, :], spread(rden, tiles, heads, at), ALU.mult).then_inc(p_done, 1)

                def page_sums(b):
                    wait(ve, v_free[GROUPS - 1], b * ROUNDS + ROUNDS)
                    wait(ve, sums_turned, b)
                    nc.vector.tensor_copy(fvs[:, :], fv_bank[0:H, :]).then_inc(of_out, 1)

                def probabilities(b):
                    s, tiles, heads, at = kinds[3]
                    nc.vector.tensor_tensor(pf[:, :, :], sf[:, :, :], spread(rden, tiles, heads, at), ALU.mult).then_inc(pf_done, 1)

                def small_sums(b):
                    wait(ve, small_free, b + 1)
                    wait(ve, sums_turned, b)
                    nc.vector.tensor_copy(svs[:, :, :], sv_bank[0:R, 0:4 * HD].rearrange("p (i n) -> p i n", i=2)).then_inc(os_out, 1)
                    nc.vector.tensor_copy(mvs[:, :], mv_bank[0:MH, :]).then_inc(os_out, 1)

                def place_sums(b):
                    wait(ve, sums_turned, b + 1)
                    for j in range(2):
                        rows = slice(64 * j, 64 * j + 64)
                        nc.vector.tensor_copy(k.of[rows, :, bass.ds(b, 1)],
                                              of_turned[rows, :].rearrange("p (c j) -> p c j", j=2)[:, :, j:j + 1]).then_inc(placed, 1)
                        nc.vector.tensor_copy(k.ow[rows, :, bass.ds(b, 1), j * R:(j + 1) * R],
                                              ow_turned[rows, :].rearrange("p (i a h) -> p i a h", i=2, a=1)).then_inc(placed, 1)
                    nc.vector.tensor_copy(k.om[:, :, bass.ds(b, 1)], om_turned.unsqueeze(2)).then_inc(placed, 1)

                wait(ve, zero, 1)
                def step(b, before=2):
                    spread_queries(b)
                    wait(ve, pf_done, b)
                    scores(b, before)
                    softmax(b)
                    if before:
                        page_sums(b - 1)
                    probabilities(b)

                step(0, 0)
                step(1, 1)
                with ve.Fori(2, NB) as b:
                    step(b)
                small_sums(NB - 1)
                place_sums(NB - 2)
                page_sums(NB - 1)
                place_sums(NB - 1)


def merge(k):
    nc, ps, wait = k.nc, k.ps, k.wait
    halves = lambda a: a.rearrange("p (i n) -> p i n", i=2)
    banks = lambda i: [ps[2 * i], ps[2 * i + 1]]
    with ExitStack() as cx:
        sb, sem = k.makers(cx)
        br = sb("e_br", [P, 12, TT])
        mt = sb("e_mt", [P, DC, TT])
        wout = sb("e_wout", [P, DC, D])
        x = sb("e_x", [P, NT + 1, D])
        gp = sb("e_gp", [P, D])
        wout_in, x_in = sem("e_wout_in"), sem("e_x_in")
        N = 12

        with ExitStack() as ix:
            sb1, _ = k.makers(ix)
            RING = 2
            ring = [sb1(f"e_w{i}", [P, DC, 2 * P]) for i in range(RING)]
            e = [sb1(f"e_e{i}", [P, 2, TH]) for i in range(2)]
            gs = sb1("e_gs", [P, 2, TH])
            sn = sb1("e_sn", [P, 3, 4, NB])
            w_in = [sem(f"e_w_in{i}") for i in range(RING)]
            proj_done, e_done, step, gs_done, turned, br_out, so_done, sn_done = (
                sem("e_" + n) for n in ("proj_done", "e_done", "step", "gs_done", "turned", "br_out", "so_done", "sn_done"))
            cols = [C_NSILU, C_FSILU, C_MSILU]
            with nc.Block() as block:
                @block.sync
                def _(sp):
                    for i in range(N // 2):
                        if i >= RING:
                            sp.wait_ge(proj_done, 2 * (i - RING) + 2)
                        col = cols[i // 2] + (i % 2) * 2 * P
                        sp.dma_start(ring[i % RING][:, :, :], k.w_in[:, col:col + 2 * P].rearrange("(c p) n -> p c n", p=P)).then_inc(w_in[i % RING], 16)
                    sp.dma_start(gp[:, :], k.g_post[0].partition_broadcast(P)).then_inc(x_in, 16)
                    sp.dma_start(x[:, 0:NT, :], k.x_prompt.rearrange("(t p) n -> p t n", p=P)).then_inc(x_in, 16)
                    sp.dma_start(x[0:NB, NT, :], k.x_sample).then_inc(x_in, 16)
                    sp.dma_start(wout[:, :, :], k.w_out.rearrange("(c p) n -> p c n", p=P)).then_inc(wout_in, 16)
                    sp.wait_ge(wout_in, 16)
                    sp.wait_ge(x_in, 48)

                @block.tensor
                def _(te):
                    nc.tensor.matmul(ps[7][:, 0:2 * NB * H], k.dupall, k.ow[:, :, :, :].rearrange("p i b h -> p (i b h)"), start=True, stop=True)
                    nc.tensor.matmul(ps[7][:, 2 * NB * H:3 * NB * H], k.dupall[0:64, :], k.oc[:, :, :].rearrange("p b h -> p (b h)"), start=True, stop=True).then_inc(so_done, 1)
                    for n in range(N):
                        te.wait_ge(w_in[(n // 2) % RING], 16 * (n // (2 * RING) + 1))
                        if n >= 2:
                            te.wait_ge(gs_done, n - 1)
                        for i in range(2):
                            for c in range(DC):
                                last = nc.tensor.matmul(banks(n % 2)[i][:, 0:TH], ring[(n // 2) % RING][:, c, (n % 2) * P:(n % 2) * P + P],
                                                        k.xnT[:, c, i * TH:(i + 1) * TH], start=c == 0, stop=c == DC - 1)
                        last.then_inc(proj_done, 1)
                        if n >= 2:
                            te.wait_ge(br_out, n - 1)
                        for t in range(NT):
                            last = nc.tensor.transpose(ps[4 + n % 2][:, t * P:(t + 1) * P], k.o[:, t, n * P:(n + 1) * P], k.ident)
                        last.then_inc(turned, 1)

                @block.scalar
                def _(sc):
                    for n in range(N):
                        sc.wait_ge(proj_done, n + 1)
                        if n >= 2:
                            sc.wait_ge(gs_done, n - 1)
                        for i in range(2):
                            last = nc.scalar.activation(e[n % 2][:, i, :], banks(n % 2)[i][:, 0:TH], ACT.Exp, scale=-1.0)
                        last.then_inc(e_done, 1)

                @block.gpsimd
                def _(pool):
                    pass

                @block.vector
                def _(ve):
                    ve.wait_ge(so_done, 1)
                    for i in range(3):
                        gate = k.sg[:, ((i + 1) % 3) * 4:((i + 1) % 3) * 4 + 4, :]
                        for j in range(2):
                            rows = slice(64 * j, 64 * j + 64)
                            src = ps[7][rows, i * 64:(i + 1) * 64].rearrange("p (b c j) -> p j c b", b=NB, j=2)[:, j]
                            nc.vector.tensor_tensor(sn[rows, i, :, :], src, gate[rows], ALU.mult).then_inc(sn_done, 1)
                    ve.wait_ge(sn_done, 6)
                    nc.vector.tensor_tensor(sn[:, 0], sn[:, 0], sn[:, 1], ALU.add).then_inc(sn_done, 1)
                    ve.wait_ge(sn_done, 7)
                    nc.vector.tensor_tensor(sn[:, 0], sn[:, 0], sn[:, 2], ALU.add).then_inc(sn_done, 1)
                    ve.wait_ge(sn_done, 8)
                    for n in range(N):
                        ve.wait_ge(e_done, n + 1)
                        en = e[n % 2]
                        nc.vector.tensor_scalar_add(en[:, :, :], en[:, :, :], 1.0).then_inc(step, 1)
                        ve.wait_ge(step, 2 * n + 1)
                        nc.vector.reciprocal(en[:, :, :], en[:, :, :]).then_inc(step, 1)
                        ve.wait_ge(step, 2 * n + 2)
                        if n:
                            ve.wait_ge(br_out, n)
                        for i in range(2):
                            last = nc.vector.tensor_tensor(gs[:, i, :], en[:, i, :], banks(n % 2)[i][:, 0:TH], ALU.mult)
                        last.then_inc(gs_done, 1)
                        ve.wait_ge(gs_done, n + 1)
                        ve.wait_ge(turned, n + 1)
                        flat = gs[:, :, :].rearrange("p i n -> p (i n)")
                        own = (sn[:, 0], k.of[:, :, :], k.om[:, :, :])[n // 4][:, n % 4, :]
                        nc.vector.tensor_tensor(br[:, n, T:TT], flat[:, T:TT], own, ALU.mult)
                        nc.vector.tensor_tensor(br[:, n, 0:T], flat[:, 0:T], ps[4 + n % 2][:, :], ALU.mult).then_inc(br_out, 1)

        with ExitStack() as ix:
            sb1, _ = k.makers(ix)
            wg = [sb1(f"e_wg{i}", [P, DC, P]) for i in range(3)]
            wb = [sb1(f"e_wb{i}", [P, 4, P]) for i in range(3)]
            e = [sb1(f"e_s{i}", [P, 2, TH]) for i in range(2)]
            tmp = sb1("e_tmp", [P, 2, TH])
            w_in = [sem(f"e_m_in{i}") for i in range(3)]
            z_done = [sem(f"e_z_done{i}") for i in range(3)]
            g_done, e_done, step, part, mt_done = (sem("e_m_" + n) for n in ("g_done", "e_done", "step", "part", "mt_done"))
            acc = sb1("e_acc", [P, 2, TH])
            k.prime(*z_done, part)
            with nc.Block() as block:
                @block.sync
                def _(sp):
                    with sp.Fori(0, DC) as d:
                        for b in range(3):
                            wait(sp, z_done[b], d)
                            sp.dma_start(wg[b][:, :, :], k.w_in[:, bass.ds(d * P + (C_BGATE + b * D), P)].rearrange("(c p) n -> p c n", p=P)).then_inc(w_in[b], 16)
                            sp.dma_start(wb[b][:, :, :], k.w_branch[b][:, bass.ds(d * P, P)].rearrange("(c p) n -> p c n", p=P)).then_inc(w_in[b], 16)

                @block.tensor
                def _(te):
                    with te.Fori(0, DC) as d:
                        for b in range(3):
                            wait(te, w_in[b], d * 32 + 32)
                            gb, zb = (ps[0:2], ps[2:4]) if b % 2 == 0 else (ps[4:6], ps[6:8])
                            wait(te, part, d * 3 + max(b - 1, 0))
                            for i in range(2):
                                for c in range(DC):
                                    last = nc.tensor.matmul(gb[i][:, 0:TH], wg[b][:, c, :], k.xnT[:, c, i * TH:(i + 1) * TH], start=c == 0, stop=c == DC - 1)
                            last.then_inc(g_done, 1)
                            for i in range(2):
                                for c in range(4):
                                    last = nc.tensor.matmul(zb[i][:, 0:TH], wb[b][:, c, :], br[:, b * 4 + c, i * TH:(i + 1) * TH], start=c == 0, stop=c == 3)
                            last.then_inc(z_done[b], 1)

                @block.scalar
                def _(sc):
                    with sc.Fori(0, DC) as d:
                        for b in range(3):
                            gb = ps[0:2] if b % 2 == 0 else ps[4:6]
                            wait(sc, g_done, d * 3 + b + 1)
                            wait(sc, part, d * 3 + max(b - 1, 0))
                            for i in range(2):
                                last = nc.scalar.activation(e[b % 2][:, i, :], gb[i][:, 0:TH], ACT.Exp, scale=-1.0)
                            last.then_inc(e_done, 1)

                @block.vector
                def _(ve):
                    with ve.Fori(0, DC) as d:
                        for b in range(3):
                            zb = ps[2:4] if b % 2 == 0 else ps[6:8]
                            wait(ve, e_done, d * 3 + b + 1)
                            nc.vector.tensor_scalar_add(e[b % 2][:, :, :], e[b % 2][:, :, :], 1.0).then_inc(step, 1)
                            wait(ve, step, d * 6 + 2 * b + 1)
                            nc.vector.reciprocal(e[b % 2][:, :, :], e[b % 2][:, :, :]).then_inc(step, 1)
                            wait(ve, step, d * 6 + 2 * b + 2)
                            wait(ve, z_done[b], d + 1)
                            for i in range(2):
                                last = nc.vector.tensor_tensor((tmp if b else acc)[:, i, :], e[b % 2][:, i, :], zb[i][:, 0:TH], ALU.mult)
                            last.then_inc(part, 1)
                            wait(ve, part, d * 3 + b + 1)
                            if b == 1:
                                nc.vector.tensor_tensor(acc[:, :, :], acc[:, :, :], tmp[:, :, :], ALU.add).then_inc(mt_done, 1)
                                wait(ve, mt_done, d * 2 + 1)
                            if b == 2:
                                nc.vector.tensor_tensor(mt[:, bass.ds(d, 1), :].rearrange("p a (i n) -> p (a i) n", i=2), acc[:, :, :], tmp[:, :, :], ALU.add).then_inc(mt_done, 1)
                                wait(ve, mt_done, d * 2 + 2)

        with ExitStack() as ix:
            sb1, _ = k.makers(ix)
            y = [sb1(f"e_y{i}", [P, D]) for i in range(2)]
            sq = sb1("e_sq", [P, 512])
            ss = sb1("e_ss", [P, NT + 1, 2])
            rs = sb1("e_rs", [P, NT + 1])
            wide = [P] * NT + [NB]
            y_done, sq_done, mean_done, rs_done, scaled, y_ready, out_done, sqc = (
                sem("e_y_" + n) for n in ("done", "sq", "mean", "rs", "scaled", "ready", "out", "sq_order"))
            with nc.Block() as block:
                @block.sync
                def _(sp):
                    for t, w in enumerate(wide):
                        sp.wait_ge(y_ready, t + 1)
                        dst = k.o_y_p[t * P:(t + 1) * P, :] if t < NT else k.o_y_s
                        sp.dma_start(dst, y[t % 2][0:w, :]).then_inc(out_done, 16)
                        sp.wait_ge(out_done, 16 * (t + 1))
                        sp.sem_inc(sqc, 1)

                @block.tensor
                def _(te):
                    for t, w in enumerate(wide):
                        if t >= 2:
                            te.wait_ge(scaled, t - 1)
                        for i in range(2):
                            for c in range(DC):
                                last = nc.tensor.matmul(banks(t % 2)[i][0:w, :], mt[:, c, t * P:t * P + w], wout[:, c, i * 512:(i + 1) * 512],
                                                        start=c == 0, stop=c == DC - 1)
                        last.then_inc(y_done, 1)

                @block.scalar
                def _(sc):
                    for t, w in enumerate(wide):
                        sc.wait_ge(y_done, t + 1)
                        for i in range(2):
                            if t or i:
                                sc.wait_ge(sq_done, 2 * t + i)
                            nc.scalar.activation(sq[0:w, :], banks(t % 2)[i][0:w, :], ACT.Square, accum_out=ss[0:w, t, i:i + 1]).then_inc(sq_done, 1)
                        sc.wait_ge(mean_done, 2 * t + 2)
                        nc.scalar.activation(rs[0:w, t:t + 1], rs[0:w, t:t + 1], ACT.Ln).then_inc(rs_done, 1)
                        sc.wait_ge(rs_done, 2 * t + 1)
                        nc.scalar.activation(rs[0:w, t:t + 1], rs[0:w, t:t + 1], ACT.Exp, scale=-0.5).then_inc(rs_done, 1)

                @block.vector
                def _(ve):
                    for t, w in enumerate(wide):
                        ve.wait_ge(sq_done, 2 * t + 2)
                        nc.vector.tensor_tensor(rs[0:w, t:t + 1], ss[0:w, t, 0:1], ss[0:w, t, 1:2], ALU.add).then_inc(mean_done, 1)
                        ve.wait_ge(mean_done, 2 * t + 1)
                        nc.vector.tensor_scalar(rs[0:w, t:t + 1], rs[0:w, t:t + 1], 1.0 / D, EPS, ALU.mult, ALU.add).then_inc(mean_done, 1)
                        ve.wait_ge(rs_done, 2 * t + 2)
                        if t >= 2:
                            ve.wait_ge(sqc, t - 1)
                        for i in range(2):
                            last = nc.vector.scalar_tensor_tensor(out=y[t % 2][0:w, i * 512:(i + 1) * 512], in0=banks(t % 2)[i][0:w, :], scalar=rs[0:w, t:t + 1],
                                                                  in1=gp[0:w, i * 512:(i + 1) * 512], op0=ALU.mult, op1=ALU.mult)
                        last.then_inc(scaled, 1)
                        ve.wait_ge(scaled, t + 1)
                        nc.vector.tensor_tensor(y[t % 2][0:w, :], y[t % 2][0:w, :], x[0:w, t, :], ALU.add).then_inc(y_ready, 1)


def hybrid_step(nc, x_prompt, x_sample, cache_nsa_cmp, cache_nsa_slc, state_nsa_win, cache_fox_kv, cache_fox_logf,
                cache_mem_kv, page_table, mem_prompt, g_pre, g_post, g_mem, w_in, b_fgate, w_mem_kv, w_cmp1, w_cmp2,
                pe_cmp, w_branch, w_out, consts, selectors, *outs):
    k = Shared()
    k.nc = nc
    k.x_prompt, k.x_sample, k.mem_prompt = x_prompt[0], x_sample.rearrange("b s d -> (b s) d"), mem_prompt[0]
    k.cache_cmp = cache_nsa_cmp[0].rearrange("n p v g d -> n p (v g d)")
    k.cache_slc = cache_nsa_slc[0].rearrange("n p v g d -> (n p) (v g d)")
    k.state_win = state_nsa_win[0].rearrange("b t v g d -> b t (v g d)")
    k.cache_fox = cache_fox_kv[0].rearrange("n p v h d -> n p v (h d)")
    k.cache_logf = cache_fox_logf[0].rearrange("n p h -> n (p h)")
    k.cache_mem = cache_mem_kv[0].rearrange("b t v h d -> b t (v h d)")
    k.page_table, k.g_pre, k.g_post, k.g_mem = page_table, g_pre, g_post, g_mem
    k.w_in, k.b_fgate, k.w_mem, k.w_cmp1, k.w_cmp2, k.pe_cmp = w_in[0], b_fgate, w_mem_kv[0], w_cmp1, w_cmp2, pe_cmp
    k.w_branch, k.w_out, k.consts = w_branch[0], w_out[0], consts
    k.selectors = selectors
    (k.o_y_p, k.o_y_s, k.o_cmp_p, k.o_slc_p, k.o_win_p, k.o_fkv_p, k.o_logf_p, k.o_mem_p,
     k.o_cmp_s, k.o_slc_s, k.o_win_s, k.o_fkv_s, k.o_logf_s) = outs

    primed = {}

    def makers(cx):
        held, sems = cx.enter_context(ExitStack()), []

        def semaphore(name):
            sems.append(held.enter_context(nc.semaphore(name)))
            return sems[-1]

        def clear():
            if sems:
                for s in sems:
                    primed.pop(s.num, None)
                with nc.Block() as block:
                    @block.gpsimd
                    def _(pool):
                        for s in sems:
                            pool.sem_clear(s)

        cx.callback(clear)
        return (lambda name, shape, dt=F32: cx.enter_context(nc.sbuf_tensor(name, shape, dt))), semaphore

    def prime(*sems, by=1):
        with nc.Block() as block:
            @block.gpsimd
            def _(pool):
                for s in sems:
                    primed[s.num] = by
                    pool.sem_inc(s, by)

    def wait(engine, s, count):
        engine.wait_ge(s, count + primed.get(s.num, 0))

    k.prime, k.wait = prime, wait

    with ExitStack() as cx:
        k.makers = makers
        sb, sem = makers(cx)
        k.logf_in, k.slc_in = [sem(f"logf_in{i}") for i in range(2)], sem("slc_in")
        k.ps = [cx.enter_context(nc.psum_tensor(f"bank{i}", [P, 512], F32)) for i in range(8)]
        k.table = sb("table", [1, NB * PAGES], I32)
        k.w2b, k.w2d = sb("w2b", [P, 2, P]), sb("w2d", [P, 2, P])
        k.pebias = sb("pebias", [P, 2])
        k.kcb, k.vcb = sb("kcb", [P, NB, 64]), sb("vcb", [64, NB, P])
        compress(k)
        k.cst = sb("cst", [P, NC])
        (k.ident, k.ones, k.swap, k.dup, k.dupall, k.causal, k.later, k.wsuf, k.cum, k.ropec, k.ropes, k.cneg, k.c01,
         k.diag, k.newneg, k.lcol, k.blk, k.blkrow, k.jmask, k.epart, k.headrow) = (
            k.cst[:, AT[name]:AT[name] + n] for name, n in CONSTS.items())
        k.rpast = sb("rpast", [P, NB * PAGES, H])
        forget(k)
        k.xnT = sb("xnT", [P, DC, TT])
        k.o = sb("o", [P, NT, 3 * BRW])
        k.srow, k.slrow = sb("srow", [NB, M_ALL]), sb("slrow", [NB, H])
        k.snew = sb("snew", [P, 3, NB, H])
        k.qd, k.qg, k.qf = sb("qd", [P, NB, H]), sb("qg", [P, NB, H]), sb("qf", [P, NB, 4])
        k.mq, k.sg = sb("mq", [P, NB, MH]), sb("sg", [P, 12, NB])
        k.selrow = sb("selrow", [P, NB * G * 8], I32)
        k.oc, k.ow = sb("oc", [64, NB, H]), sb("ow", [P, 2, NB, H])
        k.of, k.om = sb("of", [P, 4, NB]), sb("om", [P, MH, NB])
        with ExitStack() as px:
            sb1, _ = makers(px)
            k.mnT = sb1("mnT", [P, DC, NM])
            norm(k)
            k.fm = sb1("fm", [P, K_ALL, TT])
            k.row = sb1("row", [P, NT, M_ALL])
            k.mrow, k.mkT = sb1("mrow", [P, NM // P, 2 * BRW]), sb1("mkT", [P, MH, NM])
            k.ncum, k.grow = sb1("ncum", [H, T]), sb1("grow", [P, NT, 24])
            with ExitStack() as gx:
                sb2, _ = makers(gx)
                k.gate, k.logf = sb2("gate", [24, TT]), sb2("logf", [H, TT])
                project(k)
                gates(k)
            prompt_compressed(k)
            sample_compressed(k)
            prompt(k)
        sample(k)
        merge(k)


_INS = ['x_prompt', 'x_sample', 'cache_nsa_cmp', 'cache_nsa_slc', 'state_nsa_win', 'cache_fox_kv', 'cache_fox_logf',
        'cache_mem_kv', 'page_table', 'mem_prompt', 'g_pre', 'g_post', 'g_mem', 'w_in', 'b_fgate', 'w_mem_kv', 'w_cmp1',
        'w_cmp2', 'pe_cmp', 'w_branch', 'w_out']
_OUTS = [((1, T, D), (T, D)), ((NB, 1, D), (NB, D)), ((1, 1, T, 2, G, HD), (T, 256)), ((1, 1, T, 2, G, HD), (T, 256)),
         ((1, 1, WIN, 2, G, HD), (T, 256)), ((1, 1, T, 2, H, HD), (T, 2 * BRW)), ((1, 1, T, H), (T, H)),
         ((1, 1, NM, 2, MH, P), (NM, 2 * BRW)), ((1, NB, 1, 2, G, HD), (NB, 256)), ((1, NB, 1, 2, G, HD), (NB, 256)),
         ((1, NB, WIN, 2, G, HD), (NB, WIN, 256)), ((1, NB, 1, 2, H, HD), (NB, 2 * BRW)), ((1, NB, 1, H), (NB, H))]


def kernel(**inputs):
    import concourse.bacc as bacc
    from concourse.bass_utils import run_bass_kernel_spmd

    nc = bacc.Bacc("TRN2", target_bir_lowering=False, num_devices=1)
    arrays = {name: np.ascontiguousarray(inputs[name]) for name in _INS}
    arrays["consts"], arrays["selectors"] = constants()
    args = [nc.dram_tensor(f"in_{name}", list(a.shape), mybir.dt.from_np(a.dtype), kind="ExternalInput").ap()
            for name, a in arrays.items()]
    args += [nc.dram_tensor(f"out_{i}", list(shape), F32, kind="ExternalOutput").ap() for i, (_, shape) in enumerate(_OUTS)]
    hybrid_step(nc, *args)
    r = run_bass_kernel_spmd(nc, [{f"in_{name}": a for name, a in arrays.items()}], core_ids=[0])
    return tuple(r.results[0][f"out_{i}"].reshape(shape) for i, (shape, _) in enumerate(_OUTS))
```
